# Optimizing a Trainium2 kernel written in Bass

```python
import jax, jax.numpy as jnp
from jax import lax
import numpy as np

D_MODEL = 1024
BATCH = 1
SEQ = 512
DEPTH = 2

GRID_W = 64
CTX_LEN = 256
N_MIXERS = 2
BLK = 128
WINDOW = 128
ROPE_BASE = 10000.0
EPS = 1e-6
NEG_INF = -1e30

A_HEADS = 16
A_KV_HEADS = 4
A_GROUP = A_HEADS // A_KV_HEADS
A_HEAD_DIM = 64
A_WIDTH = A_HEADS * A_HEAD_DIM
A_KV_WIDTH = A_KV_HEADS * A_HEAD_DIM
A_IN = A_WIDTH + 2 * A_KV_WIDTH + A_WIDTH

B_HEADS = 16
B_NOPE = 64
B_ROPE = 32
B_V = 64
B_Q_RANK = 256
B_KV_RANK = 128
B_WIDTH = B_HEADS * B_V
B_IN = B_Q_RANK + B_KV_RANK + B_ROPE + B_WIDTH


def rmsnorm(x, g):
    xf = x.astype(jnp.float32)
    y = xf * lax.rsqrt(jnp.mean(xf * xf, axis=-1, keepdims=True) + EPS)
    return (y * g.astype(jnp.float32)).astype(x.dtype)

def axial_rope_tables(n_tokens, rot_dim, dtype):
    n_rows = n_tokens // GRID_W
    row = jnp.broadcast_to(jnp.arange(n_rows)[:, None], (n_rows, GRID_W)).reshape(-1)
    col = jnp.broadcast_to(jnp.arange(GRID_W)[None, :], (n_rows, GRID_W)).reshape(-1)
    nf = rot_dim // 4
    inv = ROPE_BASE ** (-jnp.arange(nf, dtype=jnp.float32) / nf)
    ar = row.astype(jnp.float32)[:, None] * inv
    ac = col.astype(jnp.float32)[:, None] * inv
    ang = jnp.concatenate([ar, ar, ac, ac], axis=-1)
    return jnp.cos(ang).astype(dtype), jnp.sin(ang).astype(dtype)

def apply_rope(x, cos, sin):
    a1, a2, b1, b2 = jnp.split(x, 4, axis=-1)
    rot = jnp.concatenate([-a2, a1, -b2, b1], axis=-1)
    shp = (x.shape[1],) + (1,) * (x.ndim - 3) + (x.shape[-1],)
    return x * cos.reshape(shp) + rot * sin.reshape(shp)

def modulate(x, g, shift, scale):
    return rmsnorm(x, g) * (1 + scale) + shift

def mixer_a(h, hc, w_in, sinks, w_o, cos, sin, ctx_out):
    bsz, S, _ = h.shape
    dt = h.dtype
    q, k, v, g = jnp.split(h @ w_in, [A_WIDTH, A_WIDTH + A_KV_WIDTH, A_WIDTH + 2 * A_KV_WIDTH], axis=-1)
    q = apply_rope(q.reshape(bsz, S, A_KV_HEADS, A_GROUP, A_HEAD_DIM), cos, sin)
    k = apply_rope(k.reshape(bsz, S, A_KV_HEADS, A_HEAD_DIM), cos, sin)
    v = v.reshape(bsz, S, A_KV_HEADS, A_HEAD_DIM)
    kvc = hc @ w_in[:, A_WIDTH:A_WIDTH + 2 * A_KV_WIDTH]
    kc, vc = jnp.split(kvc.reshape(bsz, -1, 2 * A_KV_HEADS, A_HEAD_DIM), 2, axis=2)
    sink_logit = sinks.astype(jnp.float32).reshape(A_KV_HEADS, A_GROUP)
    scale = A_HEAD_DIM ** -0.5
    kp = jnp.pad(k, ((0, 0), (BLK, BLK), (0, 0), (0, 0)))
    vp = jnp.pad(v, ((0, 0), (BLK, BLK), (0, 0), (0, 0)))

    def block(i):
        qs = lax.dynamic_slice_in_dim(q, i * BLK, BLK, axis=1)
        ks = lax.dynamic_slice_in_dim(kp, i * BLK, 3 * BLK, axis=1)
        vs = lax.dynamic_slice_in_dim(vp, i * BLK, 3 * BLK, axis=1)
        q_pos = i * BLK + jnp.arange(BLK)
        k_pos = (i - 1) * BLK + jnp.arange(3 * BLK)
        valid = (jnp.abs(q_pos[:, None] - k_pos[None, :]) <= WINDOW) & (k_pos >= 0)[None, :] & (k_pos < S)[None, :]
        s_loc = jnp.einsum('bqhgd,bkhd->bhgqk', qs, ks).astype(jnp.float32) * scale
        s_loc = jnp.where(valid, s_loc, NEG_INF)
        s_ctx = jnp.einsum('bqhgd,bkhd->bhgqk', qs, kc).astype(jnp.float32) * scale
        sink = jnp.broadcast_to(sink_logit[None, :, :, None, None], s_loc.shape[:-1] + (1,))
        p = jax.nn.softmax(jnp.concatenate([s_loc, s_ctx, sink], axis=-1), axis=-1).astype(dt)
        n_loc = 3 * BLK
        return (jnp.einsum('bhgqk,bkhd->bqhgd', p[..., :n_loc], vs)
                + jnp.einsum('bhgqk,bkhd->bqhgd', p[..., n_loc:-1], vc))

    o = lax.map(block, jnp.arange(S // BLK))
    o = jnp.moveaxis(o, 0, 1).reshape(bsz, S, A_WIDTH)
    y = (o * jax.nn.silu(g)) @ w_o
    if not ctx_out:
        return y, None
    C = hc.shape[1]
    qc = (hc @ w_in[:, :A_WIDTH]).reshape(bsz, C, A_KV_HEADS, A_GROUP, A_HEAD_DIM)
    gc = hc @ w_in[:, A_WIDTH + 2 * A_KV_WIDTH:]
    s = jnp.einsum('bqhgd,bkhd->bhgqk', qc, kc).astype(jnp.float32) * scale
    sink = jnp.broadcast_to(sink_logit[None, :, :, None, None], s.shape[:-1] + (1,))
    p = jax.nn.softmax(jnp.concatenate([s, sink], axis=-1), axis=-1)[..., :-1].astype(dt)
    oc = jnp.einsum('bhgqk,bkhd->bqhgd', p, vc).reshape(bsz, C, A_WIDTH)
    yc = (oc * jax.nn.silu(gc)) @ w_o
    return y, yc

def mixer_b(h, hc, w_in, q_norm_g, w_uq, kv_norm_g, w_ukv, w_o, cos, sin, ctx_out):
    bsz, S, _ = h.shape
    C = hc.shape[1]
    dt = h.dtype
    splits = [B_Q_RANK, B_Q_RANK + B_KV_RANK, B_Q_RANK + B_KV_RANK + B_ROPE]
    cq, ckv, kr, g = jnp.split(h @ w_in, splits, axis=-1)
    q = (rmsnorm(cq, q_norm_g) @ w_uq).reshape(bsz, S, B_HEADS, B_NOPE + B_ROPE)
    qn, qr = q[..., :B_NOPE], apply_rope(q[..., B_NOPE:], cos, sin)
    kv = (rmsnorm(ckv, kv_norm_g) @ w_ukv).reshape(bsz, S, B_HEADS, B_NOPE + B_V)
    kn, v = kv[..., :B_NOPE], kv[..., B_NOPE:]
    kr = apply_rope(kr, cos, sin)
    ckv_c, kr_c = jnp.split(hc @ w_in[:, B_Q_RANK:splits[2]], [B_KV_RANK], axis=-1)
    kv_c = (rmsnorm(ckv_c, kv_norm_g) @ w_ukv).reshape(bsz, C, B_HEADS, B_NOPE + B_V)
    kn_c, v_c = kv_c[..., :B_NOPE], kv_c[..., B_NOPE:]
    kn_all = jnp.concatenate([kn_c, kn], axis=1)
    kr_all = jnp.concatenate([kr_c, kr], axis=1)
    v_all = jnp.concatenate([v_c, v], axis=1)
    scale = (B_NOPE + B_ROPE) ** -0.5

    def block(i):
        qn_b = lax.dynamic_slice_in_dim(qn, i * BLK, BLK, axis=1)
        qr_b = lax.dynamic_slice_in_dim(qr, i * BLK, BLK, axis=1)
        s = (jnp.einsum('bqhd,bkhd->bhqk', qn_b, kn_all)
             + jnp.einsum('bqhr,bkr->bhqk', qr_b, kr_all)).astype(jnp.float32) * scale
        p = jax.nn.softmax(s, axis=-1).astype(dt)
        return jnp.einsum('bhqk,bkhd->bqhd', p, v_all)

    o = lax.map(block, jnp.arange(S // BLK))
    o = jnp.moveaxis(o, 0, 1).reshape(bsz, S, B_WIDTH)
    y = (o * jax.nn.silu(g)) @ w_o
    if not ctx_out:
        return y, None
    qc = (rmsnorm(hc @ w_in[:, :B_Q_RANK], q_norm_g) @ w_uq).reshape(bsz, C, B_HEADS, B_NOPE + B_ROPE)
    gc = hc @ w_in[:, splits[2]:]
    s = (jnp.einsum('bqhd,bkhd->bhqk', qc[..., :B_NOPE], kn_c)
         + jnp.einsum('bqhr,bkr->bhqk', qc[..., B_NOPE:], kr_c)).astype(jnp.float32) * scale
    p = jax.nn.softmax(s, axis=-1).astype(dt)
    oc = jnp.einsum('bhqk,bkhd->bqhd', p, v_c).reshape(bsz, C, B_WIDTH)
    yc = (oc * jax.nn.silu(gc)) @ w_o
    return y, yc

def first_inputs(seed: int = 0) -> dict:
    key = jax.random.key(seed)
    ks = jax.random.split(key, 24)
    f = jnp.float32
    D = D_MODEL

    def w(k, shape, fan_in):
        return jax.random.normal(k, shape, f) * fan_in ** -0.5

    def gain(k, n):
        return 1.0 + 0.02 * jax.random.normal(k, (n,), f)

    return {
        "x": jax.random.normal(ks[0], (BATCH, SEQ, D), f),
        "c": jax.random.normal(ks[1], (BATCH, D), f),
        "ctx": jax.random.normal(ks[2], (BATCH, CTX_LEN, D), f),
        "c_ctx": jax.random.normal(ks[3], (D,), f),
        "norm_g_0": gain(ks[4], D),
        "ada_w_0": w(ks[5], (D, 3 * D), D),
        "ada_b_0": 0.02 * jax.random.normal(ks[6], (3 * D,), f),
        "a_w_in_0": w(ks[7], (D, A_IN), D),
        "a_sinks_0": 0.5 * jax.random.normal(ks[8], (A_HEADS,), f),
        "a_w_o_0": w(ks[9], (A_WIDTH, D), A_WIDTH),
        "norm_g_1": gain(ks[10], D),
        "ada_w_1": w(ks[11], (D, 3 * D), D),
        "ada_b_1": 0.02 * jax.random.normal(ks[12], (3 * D,), f),
        "b_w_in_1": w(ks[13], (D, B_IN), D),
        "b_q_norm_1": gain(ks[14], B_Q_RANK),
        "b_w_uq_1": w(ks[15], (B_Q_RANK, B_HEADS * (B_NOPE + B_ROPE)), B_Q_RANK),
        "b_kv_norm_1": gain(ks[16], B_KV_RANK),
        "b_w_ukv_1": w(ks[17], (B_KV_RANK, B_HEADS * (B_NOPE + B_V)), B_KV_RANK),
        "b_w_o_1": w(ks[18], (B_WIDTH, D), B_WIDTH),
        "final_g": gain(ks[19], D),
    }

def first_block(x, c, ctx, c_ctx, norm_g_0, ada_w_0, ada_b_0, a_w_in_0, a_sinks_0, a_w_o_0,
              norm_g_1, ada_w_1, ada_b_1, b_w_in_1, b_q_norm_1, b_w_uq_1, b_kv_norm_1,
              b_w_ukv_1, b_w_o_1, final_g):
    S = x.shape[1]
    cos_a, sin_a = axial_rope_tables(S, A_HEAD_DIM, x.dtype)
    cos_b, sin_b = axial_rope_tables(S, B_ROPE, x.dtype)
    layers = [
        (norm_g_0, ada_w_0, ada_b_0, (a_w_in_0, a_sinks_0, a_w_o_0)),
        (norm_g_1, ada_w_1, ada_b_1, (b_w_in_1, b_q_norm_1, b_w_uq_1, b_kv_norm_1, b_w_ukv_1, b_w_o_1)),
    ]
    for i in range(DEPTH):
        g_norm, ada_w, ada_b, mp = layers[i]
        last = i == DEPTH - 1
        shift, scale, gate = jnp.split(jax.nn.silu(c) @ ada_w + ada_b, 3, axis=-1)
        shift_c, scale_c, gate_c = jnp.split(jax.nn.silu(c_ctx) @ ada_w + ada_b, 3, axis=-1)
        h = modulate(x, g_norm, shift[:, None], scale[:, None])
        hc = modulate(ctx, g_norm, shift_c, scale_c)
        if i % N_MIXERS == 0:
            y, yc = mixer_a(h, hc, *mp, cos_a, sin_a, not last)
        else:
            y, yc = mixer_b(h, hc, *mp, cos_b, sin_b, not last)
        x = x + gate[:, None] * y
        if not last:
            ctx = ctx + gate_c * yc
    return rmsnorm(x, final_g)


DEPTH_2 = 1

NA_W = D_MODEL // 2
NA_HEAD_DIM = 64
NA_HEADS = NA_W // NA_HEAD_DIM
NA_KH = 8
NA_KW = 16
ML_W = D_MODEL // 2
ML_HEADS = 4
ML_HEAD_DIM = ML_W // ML_HEADS
MIX_W = NA_W + ML_W
ML_CHUNK = 64
CONV_W = 5
IN_SPLITS = (NA_W,) * 4 + (ML_W,) * 5 + (ML_HEADS,) * 4
IN_W = 4 * NA_W + 5 * ML_W + 4 * ML_HEADS


def rmsnorm_2(x, w):
    x32 = x.astype(jnp.float32)
    return x32 * lax.rsqrt(jnp.mean(x32 * x32, axis=-1, keepdims=True) + EPS) * w

def centred_short_conv(u, w, b):
    T = u.shape[1]
    pad = CONV_W // 2
    up = jnp.pad(u, ((0, 0), (pad, pad), (0, 0)))
    out = up[:, 0:T] * w[0]
    for j in range(1, CONV_W):
        out = out + up[:, j:j + T] * w[j]
    return out + b

def neighbourhood_attention(q, k, v, rpb):
    B, T, _ = q.shape
    rows = T // GRID_W
    kh = min(NA_KH, rows)

    def to_grid(t):
        return t.reshape(B, rows, GRID_W, NA_HEADS, NA_HEAD_DIM).transpose(0, 3, 1, 2, 4)

    qg = to_grid(q) * (NA_HEAD_DIM ** -0.5)
    kgrid, vgrid = to_grid(k), to_grid(v)
    r = jnp.arange(rows)
    row_idx = jnp.clip(r - kh // 2, 0, rows - kh)[:, None] + jnp.arange(kh)[None, :]
    kg = kgrid[:, :, row_idx]
    vg = vgrid[:, :, row_idx]
    col = jnp.arange(GRID_W)
    col_start = jnp.clip(col - NA_KW // 2, 0, GRID_W - NA_KW)
    col_mask = (col[None, :] >= col_start[:, None]) & (col[None, :] < col_start[:, None] + NA_KW)
    dy = row_idx - r[:, None] + NA_KH - 1
    dx = jnp.clip(col[None, :] - col[:, None], -(NA_KW - 1), NA_KW - 1) + NA_KW - 1
    bias = rpb[:, dy[:, None, :, None], dx[None, :, None, :]]
    s = jnp.einsum('bhrcd,bhrjkd->bhrcjk', qg, kg).astype(jnp.float32) + bias[None]
    s = jnp.where(col_mask[:, None, :], s, -jnp.inf)
    p = jax.nn.softmax(s.reshape(B, NA_HEADS, rows, GRID_W, kh * GRID_W), axis=-1).reshape(s.shape)
    o = jnp.einsum('bhrcjk,bhrjkd->bhrcd', p, vg)
    return o.transpose(0, 2, 3, 1, 4).reshape(B, T, NA_W)

def mlstm_chunkwise(q, k, v, i_pre, f_pre):
    B, H, T, d = q.shape
    L = ML_CHUNK
    nc = T // L
    q = q.reshape(B, H, nc, L, d)
    k = (k * (d ** -0.5)).reshape(B, H, nc, L, d)
    v = v.reshape(B, H, nc, L, d)
    i_pre = i_pre.reshape(B, H, nc, L)
    b = jnp.cumsum(jax.nn.log_sigmoid(f_pre).reshape(B, H, nc, L), axis=-1)
    b_last = b[..., -1]
    a = b_last[..., None] - b + i_pre

    def step(carry, inp):
        C, n, m = carry
        k_c, v_c, a_c, bl_c = inp
        m_new = jnp.maximum(bl_c + m, jnp.max(a_c, axis=-1))
        decay = jnp.exp(bl_c + m - m_new)
        w = jnp.exp(a_c - m_new[..., None])
        C_new = decay[..., None, None] * C + jnp.einsum('bhs,bhse,bhsd->bhed', w, v_c, k_c)
        n_new = decay[..., None] * n + jnp.einsum('bhs,bhsd->bhd', w, k_c)
        return (C_new, n_new, m_new), (C, n, m)

    init = (jnp.zeros((B, H, d, d), q.dtype), jnp.zeros((B, H, d), q.dtype), jnp.zeros((B, H), q.dtype))
    xs = (jnp.moveaxis(k, 2, 0), jnp.moveaxis(v, 2, 0), jnp.moveaxis(a, 2, 0), jnp.moveaxis(b_last, 2, 0))
    _, (C_prev, n_prev, m_prev) = lax.scan(step, init, xs)
    C_prev = jnp.moveaxis(C_prev, 0, 2)
    n_prev = jnp.moveaxis(n_prev, 0, 2)
    m_prev = jnp.moveaxis(m_prev, 0, 2)

    lower = jnp.tril(jnp.ones((L, L), dtype=bool))
    Dlog = jnp.where(lower, b[..., :, None] - b[..., None, :] + i_pre[..., None, :], -jnp.inf)
    m_inter = b + m_prev[..., None]
    m_t = jnp.maximum(m_inter, jnp.max(Dlog, axis=-1))
    S = jnp.einsum('bhntd,bhnsd->bhnts', q, k) * jnp.exp(Dlog - m_t[..., None])
    inter = jnp.exp(m_inter - m_t)
    num = jnp.einsum('bhnts,bhnse->bhnte', S, v) + inter[..., None] * jnp.einsum('bhned,bhntd->bhnte', C_prev, q)
    den = jnp.sum(S, axis=-1) + inter * jnp.einsum('bhnd,bhntd->bhnt', n_prev, q)
    h = num / jnp.maximum(jnp.abs(den), jnp.exp(-m_t))[..., None]
    return h.reshape(B, H, T, d)

def hybrid_mixer(h, w_in, b_in, conv_w, conv_b, rpb, ml_norm_w, w_out):
    B, T, _ = h.shape
    proj = h @ w_in + b_in
    split_idx = np.cumsum(IN_SPLITS)[:-1].tolist()
    (na_q, na_k, na_v, na_z, ml_q, ml_k, ml_v, ml_o, ml_z,
     i_f, f_f, i_b, f_b) = jnp.split(proj, split_idx, axis=-1)

    na_out = neighbourhood_attention(na_q, na_k, na_v, rpb) * jax.nn.silu(na_z)

    qk = jax.nn.silu(centred_short_conv(jnp.concatenate([ml_q, ml_k], axis=-1), conv_w, conv_b))
    mq, mk = jnp.split(qk, 2, axis=-1)

    def heads(t):
        return t.reshape(B, T, ML_HEADS, ML_HEAD_DIM).transpose(0, 2, 1, 3)

    mq, mk, mv = heads(mq), heads(mk), heads(ml_v)
    i_f, f_f, i_b, f_b = (g.transpose(0, 2, 1) for g in (i_f, f_f, i_b, f_b))
    h_fwd = mlstm_chunkwise(mq, mk, mv, i_f, f_f)
    flip = lambda t: jnp.flip(t, axis=2)
    h_bwd = flip(mlstm_chunkwise(flip(mq), flip(mk), flip(mv), flip(i_b), flip(f_b)))
    hm = (h_fwd + h_bwd).transpose(0, 2, 1, 3) * jax.nn.sigmoid(ml_o).reshape(B, T, ML_HEADS, ML_HEAD_DIM)
    mu = jnp.mean(hm, axis=-1, keepdims=True)
    var = jnp.mean(jnp.square(hm - mu), axis=-1, keepdims=True)
    hm = ((hm - mu) * lax.rsqrt(var + EPS)).reshape(B, T, ML_W) * ml_norm_w
    ml_out = hm * jax.nn.silu(ml_z)

    return jnp.concatenate([na_out, ml_out], axis=-1) @ w_out

def second_inputs(seed: int = 0) -> dict:
    key = jax.random.key(seed)
    ks = jax.random.split(key, 14)
    D = D_MODEL
    x = jax.random.normal(ks[0], (BATCH, SEQ, D), jnp.float32)
    c = jax.random.normal(ks[1], (BATCH, D), jnp.float32)
    w_ada = jax.random.normal(ks[2], (DEPTH_2, D, 3 * D), jnp.float32) * (0.5 * D ** -0.5)
    b_ada = jax.random.normal(ks[3], (DEPTH_2, 3 * D), jnp.float32) * 0.02
    norm_w = 1.0 + 0.1 * jax.random.normal(ks[4], (DEPTH_2, D), jnp.float32)
    w_in = jax.random.normal(ks[5], (DEPTH_2, D, IN_W), jnp.float32) * (D ** -0.5)
    n_main = 4 * NA_W + 5 * ML_W
    fgate_base = jnp.linspace(3.0, 6.0, ML_HEADS, dtype=jnp.float32)
    gk = jax.random.split(ks[6], 5)
    b_in = jnp.concatenate([
        0.02 * jax.random.normal(gk[0], (DEPTH_2, n_main), jnp.float32),
        0.1 * jax.random.normal(gk[1], (DEPTH_2, ML_HEADS), jnp.float32),
        fgate_base + 0.1 * jax.random.normal(gk[2], (DEPTH_2, ML_HEADS), jnp.float32),
        0.1 * jax.random.normal(gk[3], (DEPTH_2, ML_HEADS), jnp.float32),
        fgate_base + 0.1 * jax.random.normal(gk[4], (DEPTH_2, ML_HEADS), jnp.float32),
    ], axis=-1)
    conv_w = jax.random.normal(ks[7], (DEPTH_2, CONV_W, 2 * ML_W), jnp.float32) * (CONV_W ** -0.5)
    conv_b = 0.02 * jax.random.normal(ks[8], (DEPTH_2, 2 * ML_W), jnp.float32)
    rpb = 0.1 * jax.random.normal(ks[9], (DEPTH_2, NA_HEADS, 2 * NA_KH - 1, 2 * NA_KW - 1), jnp.float32)
    ml_norm_w = 1.0 + 0.1 * jax.random.normal(ks[10], (DEPTH_2, ML_W), jnp.float32)
    w_out = jax.random.normal(ks[11], (DEPTH_2, MIX_W, D), jnp.float32) * (MIX_W ** -0.5)
    final_norm_w = 1.0 + 0.1 * jax.random.normal(ks[12], (D,), jnp.float32)
    return {'x': x, 'c': c, 'w_ada': w_ada, 'b_ada': b_ada, 'norm_w': norm_w, 'w_in': w_in,
            'b_in': b_in, 'conv_w': conv_w, 'conv_b': conv_b, 'rpb': rpb, 'ml_norm_w': ml_norm_w,
            'w_out': w_out, 'final_norm_w': final_norm_w}

def second_block(x, c, w_ada, b_ada, norm_w, w_in, b_in, conv_w, conv_b, rpb, ml_norm_w, w_out, final_norm_w):
    h_res = x.astype(jnp.float32)
    c_act = jax.nn.silu(c.astype(jnp.float32))
    for l in range(DEPTH_2):
        mod = c_act @ w_ada[l] + b_ada[l]
        shift, scale, gate = jnp.split(mod, 3, axis=-1)
        h = rmsnorm_2(h_res, norm_w[l]) * (1.0 + scale[:, None, :]) + shift[:, None, :]
        y = hybrid_mixer(h, w_in[l], b_in[l], conv_w[l], conv_b[l], rpb[l], ml_norm_w[l], w_out[l])
        h_res = h_res + gate[:, None, :] * y
    return rmsnorm_2(h_res, final_norm_w).astype(x.dtype)


def setup_inputs(seed=0):
    out = dict(first_inputs(seed))
    for name, value in second_inputs(seed + 1).items():
        if name != "x":
            out[name + "_2"] = value
    return out


def reference(
    x, c, ctx, c_ctx, norm_g_0, ada_w_0, ada_b_0, a_w_in_0, a_sinks_0, a_w_o_0, norm_g_1,
    ada_w_1, ada_b_1, b_w_in_1, b_q_norm_1, b_w_uq_1, b_kv_norm_1, b_w_ukv_1, b_w_o_1, final_g,
    c_2, w_ada_2, b_ada_2, norm_w_2, w_in_2, b_in_2, conv_w_2, conv_b_2, rpb_2, ml_norm_w_2,
    w_out_2, final_norm_w_2,
):
    x = first_block(
        x, c, ctx, c_ctx, norm_g_0, ada_w_0, ada_b_0, a_w_in_0, a_sinks_0, a_w_o_0, norm_g_1,
        ada_w_1, ada_b_1, b_w_in_1, b_q_norm_1, b_w_uq_1, b_kv_norm_1, b_w_ukv_1, b_w_o_1,
        final_g,
    )
    return second_block(
        x, c_2, w_ada_2, b_ada_2, norm_w_2, w_in_2, b_in_2, conv_w_2, conv_b_2, rpb_2,
        ml_norm_w_2, w_out_2, final_norm_w_2,
    )


_drawn_inputs = setup_inputs


def setup_inputs(seed=0):
    import zlib

    import numpy as np

    out = dict(_drawn_inputs(seed))
    spreads = {}
    factors = {'norm_g_0': 8.0,
     'ada_b_0': 3.476,
     'a_sinks_0': 8.0,
     'norm_g_1': 8.0,
     'ada_b_1': 4.908,
     'b_q_norm_1': 8.0,
     'b_kv_norm_1': 8.0,
     'final_g': 2.801,
     'b_ada_2': 4.155,
     'norm_w_2': 2.695,
     'conv_b_2': 58.921,
     'rpb_2': 8.0,
     'ml_norm_w_2': 3.666}
    for name, (base, spread) in spreads.items():
        noise = np.random.default_rng([zlib.crc32(name.encode()), seed]).standard_normal(out[name].shape)
        drawn = base * np.exp(spread * noise) if base else spread * noise
        out[name] = __import__('jax').numpy.asarray(drawn.astype(out[name].dtype))
    for name, factor in factors.items():
        out[name] = (out[name] * factor).astype(out[name].dtype)
    return out
```

```python
from contextlib import ExitStack

import numpy as np
import concourse.bass as bass
from concourse import mybir

P = 128
D = 1024
KD = D // P
S = 512
C = 256
T = S + C
QT = S // P
GRID = 64
EPS = 1e-6
MASKED = -1e30
N_PAIR = 8
N_NA = 4
N_ML = 4
N_RAW = 5
N_CONST = 4
N_SPLIT = 3
CHUNK = 1024
SCALE_A = 64 ** -0.5
SCALE_B = 96 ** -0.5

F32 = mybir.dt.float32
F32R = mybir.dt.float32r
ALU = mybir.AluOpType
ACT = mybir.ActivationFunctionType
AX = mybir.AxisListType.X


def column_layout():
    at, n = {}, 0
    for name, width in (("c", 16), ("c2", 16), ("ab0", 48), ("ab1", 48), ("ab2", 48), ("ng0", 16), ("ng1", 16),
                        ("ng2", 16), ("fg", 8), ("fw", 8), ("qg", 2), ("kg", 1), ("bna", 12), ("bml", 16),
                        ("cw", 40), ("cb", 8), ("mw", 4), ("bg", 1), ("sink", 16)):
        at[name] = n
        n += width
    return at, n


def chunk_plan():
    plan = []

    def ada(layer, b):
        plan.extend((f"ada{layer}.{b}.{q}", False) for q in range(4))

    def split(*names):
        plan.extend((n, True) for n in names)

    for b in range(6):
        ada(0, b)
    split("A.k0", "A.k1", "A.v0", "A.v1", "A.q0", "A.g0")
    for p in range(1, N_PAIR):
        split(f"A.q{p}", f"A.g{p}")
        if p <= 6:
            ada(1, p - 1)
    split(*[f"A.o{j}" for j in range(KD)])
    for b in range(6):
        ada(2, b)
    split("B.cq0", "B.cq1", "B.ckv", "B.kr", *[f"B.g{j}" for j in range(KD)])
    split("B.uv", "B.uqr", "B.uq0", "B.uq1", "B.uk")
    split(*[f"B.o{j}" for j in range(KD)])
    split("C.v0", "C.v1", "C.v2", "C.v3")
    for p in range(N_NA):
        split(f"C.q{p}", f"C.k{p}", f"C.z{p}")
    split("D.gate", "D.v0", "D.v1", "D.v2", "D.v3")
    for h in range(N_ML):
        split(f"D.q{h}", f"D.k{h}", f"D.o{h}", f"D.z{h}")
    split(*[f"C.o{j}" for j in range(KD)])
    return plan


def task_plan():
    count, tasks, last_use, ring = {}, {}, {}, [0]

    def task(name, bank, *chunks):
        count[bank] = count.get(bank, 0) + 1
        tasks[name] = (bank, count[bank])
        for c in chunks:
            last_use[c] = name

    def spread(name, *chunks, banks=(0, 1, 2, 3, 7)):
        task(name, banks[ring[0] % len(banks)], *chunks)
        ring[0] += 1

    def ada(layer, b, put):
        put(f"ada{layer}.{b}", *[f"ada{layer}.{b}.{q}" for q in range(4)])

    alone = lambda name, *chunks: task(name, 7, *chunks)
    for part in ("x", "c"):
        task(f"A.stat.{part}", {"x": 4, "c": 5}[part])
    for b in range(6):
        ada(0, b, spread)
        if b >= 1:
            spread(f"ada0.{b - 1}.t")
    spread("ada0.5.t")
    for j in range(2):
        spread(f"A.k{j}.x", f"A.k{j}")
        spread(f"A.k{j}.c", f"A.k{j}")
        spread(f"A.k{j}.rot")
    for t in range(T // P):
        spread(f"A.v.{t}", "A.v0", "A.v1")
    spread("A.q0.x", "A.q0")
    spread("A.q0.rot")
    spread("A.qg0.c", "A.q0", "A.g0")
    spread("A.g0.x", "A.g0")
    for p in range(1, N_PAIR):
        for step in range(6):
            for name in fillers_a(p, step):
                alone(name, *filler_chunks(name))
    for j in range(KD):
        spread(f"A.o{j}.x", f"A.o{j}")
        spread(f"A.o{j}.c", f"A.o{j}")
        if j == 0:
            task("B.stat.x", 4)
            task("B.stat.c", 5)
    for b in range(6):
        ada(2, b, spread)
        if b >= 1:
            spread(f"ada2.{b - 1}.t")
    spread("ada2.5.t")
    for name in ("B.cq0.x", "B.cq1.x", "B.ckv.x", "B.ckv.c", "B.kr.x", "B.kr.c"):
        spread(name, name[:-2])
    for j in range(KD):
        spread(f"B.g{j}.x", f"B.g{j}")
        if j == 1:
            spread("B.kr.rot")
            task("B.cq.stat", 4)
            task("B.ckv.stat.x", 5)
            task("B.ckv.stat.c", 4)
    for t in range(T // P):
        for h in range(2):
            spread(f"B.v.{t}.{h}", "B.uv")
    for i in range(4):
        spread(f"B.qr{i}.x", "B.uqr")
        if i >= 1:
            spread(f"B.qr{i - 1}.rot")
    spread("B.qr3.rot")
    for step in range(3):
        spread(*fillers_b(0, step))
    for p in range(1, N_PAIR):
        for step in range(4):
            for name in fillers_b(p, step):
                alone(name, *filler_chunks(name))
    for j in range(KD):
        spread(f"B.o{j}.x", f"B.o{j}")
        if j == 0:
            task("C.stat.1", 4)
            task("C.stat.2", 5)
    for t in range(QT):
        spread(f"C.v.{t}", "C.v0", "C.v1", "C.v2", "C.v3")
    for name in ("C.q0.x", "C.k0.x", "C.z0.x"):
        spread(name, name[:-2])
    for p in range(1, N_NA):
        for step in range(4):
            for name in fillers_c(p, step):
                alone(name, *filler_chunks(name))
    spread("D.gate.x", "D.gate")
    for t in range(QT):
        spread(f"D.v.{t}", "D.v0", "D.v1", "D.v2", "D.v3")
    order_d(lambda name, bank, *chunks: task(name, bank, *chunks))
    for j in range(KD):
        spread(f"C.o{j}.x", f"C.o{j}")
        if j == 0:
            task("E.stat", 4)
    return tasks, last_use


def fillers_a(p, step):
    out = [f"A.q{p}.x", f"A.q{p}.rot", f"A.qg{p}.c", f"A.g{p}.x"] + [f"ada1.{p - 1}", f"ada1.{p - 1}.t"] * (p <= 6)
    return out[step:step + 1]


def fillers_b(p, step):
    return [f"B.qn{p}.x", f"B.kn{p}.x", f"B.kn{p}.c"][step:step + 1]


def fillers_c(p, step):
    return [f"C.q{p}.x", f"C.k{p}.x", f"C.z{p}.x"][step:step + 1]


def filler_chunks(name):
    if name.startswith("ada"):
        return [f"{name}.{q}" for q in range(4)] if name.count(".") == 1 else []
    if name.endswith(".rot") or name.startswith(("B.qn", "B.kn")):
        return []
    if name.startswith("A.qg"):
        return [f"A.q{name[4:-2]}", f"A.g{name[4:-2]}"]
    return [name[:-2]]


def order_d(task):
    def project(h, what, bank):
        task(f"D.{what}{h}.x", bank, f"D.{what}{h}")

    task("D.gcol", 6)
    project(0, "q", 4)
    project(0, "k", 5)
    for h in range(N_ML + 1):
        if h < N_ML:
            project(h, "o", 4)
            for j in range(QT):
                task(f"D.s{h}.{j}", j)
        if h >= 1:
            task(f"D.mu{h - 1}", 6)
        if h < N_ML:
            project(h, "z", 5)
        if h >= 1:
            task(f"D.var{h - 1}", 7)
        if h + 1 < N_ML:
            project(h + 1, "q", 4)
        if h < N_ML:
            for way in ("f", "b"):
                task(f"D.num{h}.{way}", 6)
                task(f"D.den{h}.{way}", 7)
        if h + 1 < N_ML:
            project(h + 1, "k", 5)


def build(nc, wstream, cst, rope, cols, x_in, ctx_in, vbias, rpb_band, rows_dram, out):
    AT, _ = column_layout()
    chunks = chunk_plan()
    chunk_at = {name: c for c, (name, _) in enumerate(chunks)}
    splits = [name for name, split in chunks if split]
    split_at = {name: g for g, name in enumerate(splits)}
    RESIDENT = ["B.uq0", "B.uq1", "B.uk"]
    in_ring = [name for name in splits if name not in RESIDENT]
    tasks, last_use = task_plan()

    es = ExitStack()
    with es:
        def sb(name, shape, dt):
            return es.enter_context(nc.sbuf_tensor(name, shape, dt))

        def sem(name):
            return es.enter_context(nc.semaphore(name))

        NR = 12288 + 6144 + 3840 + 512 + N_SPLIT * 2048
        AR_BASE = -(-nc.sbuf_base // 32) * 32
        AR = sb("AR", [P, NR], F32R)
        NF = 28120
        AF = sb("AF", [P, NF], F32)
        place = {"F": 0, "R": 0}

        def region(kind, n):
            at = place[kind]
            place[kind] += n
            assert place[kind] <= (NF if kind == "F" else NR), (kind, place)
            return (AF if kind == "F" else AR)[:, at:at + n]

        def tiles(ap, *dims):
            n = int(np.prod(dims))
            ap = ap[:, 0:n]
            if len(dims) == 1:
                return ap
            names = "abcd"[:len(dims)]
            return ap.rearrange(f"p ({' '.join(names)}) -> p {' '.join(names)}",
                                **{k: d for k, d in zip(names, dims)})

        R1, R3, R2 = region("R", 12288), region("R", 3840), region("R", 6144)
        RC, RW = region("R", 512), region("R", N_SPLIT * 2048)
        identR, mask3R = RC[:, 0:128], RC[:, 128:512]
        WS = tiles(RW, N_SPLIT, 2, CHUNK)

        XL = tiles(region("F", KD * S), KD, S)
        OG = tiles(region("F", KD * S), KD, S)
        OGC_ = region("F", KD * C)
        LOC_ = region("F", KD * C + 4096)
        XC = tiles(LOC_, KD, C)
        RAW = tiles(region("F", N_RAW * CHUNK), N_RAW, CHUNK)
        PPT = region("F", 6 * T)
        PROB = tiles(PPT, 2, T)
        PT = tiles(PPT[:, 2 * T:], 2, 2, T)
        CST = region("F", 384)
        ident, perm, ones = CST[:, 0:128], CST[:, 128:256], CST[:, 256:384]
        ROPE = tiles(region("F", 2 * S), 2, S)
        COLS = region("F", column_layout()[1])
        MOD = tiles(region("F", 3 * 48), 3, 24, 2)
        GAIN = tiles(region("F", 3 * 16), 3, KD, 2)
        SILC = tiles(region("F", 32), 2, KD, 2)
        NSINK = region("F", 16)
        SILT = LOC_[:, 5888:5920]
        STAT = tiles(region("F", 20), 5, 4)

        PS = es.enter_context(nc.psum_tensor("PS", [P, 8, 512], F32))
        bank = [PS[:, b, :] for b in range(8)]
        SC = [PS[:, 0:2, :].rearrange("p b n -> p (b n)"), PS[:, 2:4, :].rearrange("p b n -> p (b n)")]
        PTP = PS[:, 4:6, :].rearrange("p b n -> p (b n)")

        def col(name, i=0, n=1):
            return COLS[:, AT[name] + i:AT[name] + i + n]

        HA = [tiles(R1, KD, T), tiles(R1[:, KD * T:], KD, T)]
        KZ = tiles(R2, 2, 2, 2, T)
        QA = tiles(R3, 2, 2, T)
        VA = tiles(LOC_[:, 2048:], T // P, 256)
        QRAW, COSP, QP = LOC_[:, 3584:4096], LOC_[:, 4096:4608], LOC_[:, 4608:5376]
        SQ = tiles(PPT, 2, T)
        RSTD = PPT[:, 2 * T:3 * T]
        XN = tiles(PPT[:, 3 * T:], 2, T)
        OGC = tiles(OGC_, KD, C)
        OA = HA
        KB = tiles(R1, 2, 2, 2, T)
        QB = tiles(R1[:, 6144:], 2, 2, 2, S)
        UB = tiles(R2, 3, 2, CHUNK)
        CQN = tiles(R3, 2, 2, S)
        CKN = tiles(R3[:, 2048:], 2, T)
        VB = tiles(LOC_, T // P, D)
        QR = tiles(OGC_, 4, S)
        QRH = tiles(R1[:, 10240:], 4, S)
        CQR, SQCQ, RSQ = tiles(PPT, 2, S), tiles(PPT[:, 1024:], 2, S), PPT[:, 2048:2560]
        QRAWB, COSB, KRF = PPT[:, 2560:3072], PPT[:, 3072:3584], PPT[:, 3584:4352]
        CKR, SQCK, RSK = LOC_[:, 0:768], LOC_[:, 768:1536], LOC_[:, 1536:2304]
        OB = [tiles(R1, KD, S), tiles(R1[:, KD * S:], KD, S)]
        AROW = LOC_[:, 5376:5888]
        SQ2 = tiles(PPT, 2, 2, S)
        RSTD2 = tiles(PPT[:, 2048:], 2, S)
        XNC = tiles(PPT[:, 3072:], 2, S)
        HC = OB
        KC = tiles(R2[:, 2048:], 2, 2, 2, S)
        QC = tiles(R3, 2, 2, S)
        BIAS = [[tiles(R1[:, 8192:], 2, 896), tiles(R1[:, 9984:], 2, 896)],
                [tiles(R2, 2, 896), tiles(R3[:, 2048:], 2, 896)]]
        VC = tiles(LOC_, QT, S)
        BRAW = tiles(LOC_[:, 2048:], 2, 14, GRID)
        ZB, ZT = LOC_[:, 3840:4352], LOC_[:, 4352:4864]
        DIAG = tiles(OGC_, 2, P)
        CMASK = OGC_[:, 256:320]
        BRAW2 = tiles(LOC_[:, 2048:], 2, 896)
        VBC = tiles(OGC_[:, 320:], 2, S)
        QM, KM = tiles(R2[:, 2048:], 2, 2, S), tiles(R2[:, 4096:], 2, 2, S)
        AD = nc.alloc_sbuf_tensor_at("AD", [P, 4096 + 3840 + 2048], F32, offset=AR_BASE + 4 * 8192)
        RB = tiles(AD[:, 0:4096], 2, 2, 2, S)
        R3F = AD[:, 4096:7936]
        U, CV = tiles(R3F, 2, S + 4), tiles(R3F[:, 1032:], 2, S)
        TQ, XD = R3F[:, 2056:2568], tiles(R3F[:, 2568:], 2, QT, P)
        W = tiles(AD[:, 7936:], 4, S)
        PM = tiles(LOC_[:, 2048:], 2, QT, S)
        ROWS = tiles(LOC_[:, 2048:], 3, 2, S)
        MV = tiles(LOC_, QT, S)
        PPW = tiles(PPT, 9, S)
        GALL, GI, GF = PPW[:, 0], PPW[:, 1:3], PPW[:, 3:5]
        GX, GL = PPW[:, 5:7], PPW[:, 7:9]
        TO, ZTM, ZM, T1, T2, HM, DV, SQD, RSM = (PPW[:, i] for i in range(9))
        HALF_B = OGC_[:, 1344:1360]
        GCOL = tiles(OGC_[:, 1360:], 2, QT, N_ML)

        sp_const, sp_x, sp_rope, sp_vb = (sem(n) for n in ("const_in", "x_in", "rope_in", "vbias_in"))
        raw_in = [sem(f"raw_in{i}") for i in range(N_RAW)]
        hi_done, lo_done, v_used = sem("weights_high"), sem("weights_low"), sem("v_chunk_used")
        acc_ready = [sem(f"acc_ready{b}") for b in range(8)]
        acc_read = [sem(f"acc_read{b}") for b in range(8)]
        dve_step, act_step, pool_step = sem("dve_step"), sem("act_step"), sem("pool_step")
        s_ready, nm_ready, exp_done, p_ready = (sem(n) for n in ("scores_ready", "negmax_ready", "exp_done", "probs_ready"))
        pt_ready, pt_read, pv_done, o_read = (sem(n) for n in ("probs_turned", "turned_read", "pv_done", "o_read"))
        cos_done, rope_sum = sem("cos_done"), sem("rope_sum")
        kz_done, q_hi, q_lo = sem("keys_split", ), sem("q_high"), sem("q_low")
        sq_done, sq_read = sem("squares_done"), sem("squares_read")
        root_done = sem("root_done")
        xn_done, hf_done, hhi_done, hlo_done = (sem(n) for n in ("normed", "modulated", "h_high", "h_low"))
        og_hi, og_lo = sem("out_high"), sem("out_low")
        x_new = sem("x_new")
        s_out = sem("out_stored")
        kz_zero, kc_zero = sem("keys_zeroed_a"), sem("keys_zeroed_c")
        tanh_done, b_hi = sem("tanh_done"), sem("pair_high_b")
        mod_done, silt_done, silc_done = sem("modulation_done"), sem("tanh_c"), sem("silu_c")
        consts_ready = sem("consts_ready")
        lat_sq, cqn_ready, ckn_ready, b_ready, c_ready = (sem(n) for n in (
            "latent_squares", "cq_normed", "ckv_normed", "pair_ready_b", "pair_ready_c"))
        bias_raw, bias_hi, bias_lo, bias_in = (sem(n) for n in ("bias_masked", "bias_high", "bias_low", "bias_in"))
        c_hi, zg_done, ms2_done, root2_done = (sem(n) for n in ("pair_high_c", "gate_c", "mean_square2", "root2"))

        vm_ready, gates_abs, gates_log, gates_max, rows_ready = (sem(n) for n in (
            "mlstm_begin", "gates_abs", "gates_log", "gates_max", "rows_ready"))
        rows_stored, rows_in = sem("rows_stored"), [sem("rows_in0"), sem("rows_in1")]
        conv_done, tq_ready, tq_used, qk_hi, qk_lo = (sem(n) for n in (
            "conv_done", "tanh_conv", "tanh_conv_used", "qk_high", "qk_low"))
        xd_ready, w_ready, pm_ready = sem("diagonals"), sem("decay_weights"), sem("weighted_scores")
        o_gate, z_gate, hm_ready, dv_ready, sqd_ready, root_m, ml_done = (sem(n) for n in (
            "o_gate", "z_gate", "hm_ready", "centred", "centred_squares", "root_m", "head_done"))
        y_ready = sem("y_ready")

        block = es.enter_context(nc.Block())

        units, groups = [], []

        def unit(**u):
            u["n"] = len(units)
            units.append(u)

        for p in range(N_PAIR):
            tile = p // 4
            for part, n_q in (("x", QT), ("c", C // P)):
                for t in range(n_q):
                    q0 = t * P if part == "x" else S + t * P
                    for half in range(2):
                        near = [b for b in (t - 1, t, t + 1) if 0 <= b < QT] if part == "x" else []
                        segments = []
                        if near:
                            c0 = 512 - P * len(near)
                            m0 = 0 if t > 0 else P
                            k0 = near[0] * P
                            segments.append((c0, P * len(near), [(identR, mask3R[:, m0:m0 + P * len(near)])] + [
                                (QA[:, a, p % 2, q0:q0 + P], KZ[:, b, tile, half, k0:k0 + P * len(near)])
                                for a, b in ((0, 0), (0, 1), (1, 0))]))
                        segments.append((512, C, [
                            (QA[:, a, p % 2, q0:q0 + P], KZ[:, b, tile, half, S:T])
                            for a, b in ((0, 0), (0, 1), (1, 0))]))
                        g0 = 64 * (2 * tile + half)
                        unit(c0=segments[0][0], c1=512 + C, segments=segments, scale=SCALE_A,
                             sink=col("sink", 2 * p + half), half=half,
                             values=[VA[:, b, g0:g0 + 64] for b in near + [4, 5]],
                             o0=t * P, first=t == 0, layer="A", pair=p, pair_first=part == "x" and t == 0,
                             out=(OG if part == "x" else OGC)[:, p, :] if t == n_q - 1 else None, width=P * n_q)
        A_END = len(units) // 2
        for p in range(N_PAIR):
            for t in range(QT):
                for half in range(2):
                    pairs = ((0, 0), (0, 1), (1, 0))
                    q = [QB[0:96, a, p % 2, half, t * P:t * P + P] for a in range(2)]
                    k = [KB[0:96, b, p % 2, half, :] for b in range(2)]
                    unit(c0=256, c1=1024, segments=[
                        (256, C, [(q[a], k[b][:, S:T]) for a, b in pairs]),
                        (512, S, [(q[a], k[b][:, 0:S]) for a, b in pairs])],
                         scale=SCALE_B, sink=None, half=half,
                         values=[VB[:, b, 64 * (2 * p + half):64 * (2 * p + half) + 64] for b in (4, 5, 0, 1, 2, 3)],
                         o0=t * P, first=t == 0, layer="B", pair=p, pair_first=t == 0,
                         out=OG[:, p, :] if t == QT - 1 else None, width=S)
        B_END = len(units) // 2
        for p in range(N_NA):
            for t in range(QT):
                for half in range(2):
                    q = [QC[:, a, p % 2, t * P:t * P + P] for a in range(2)]
                    d0 = (6 - 2 * t) * GRID
                    unit(c0=0, c1=S, segments=[
                        (0, S, [(identR, BIAS[p % 2][a][:, half, d0:d0 + S]) for a in range(2)]
                         + [(q[a], KC[:, b, p % 2, half, :]) for a, b in ((0, 0), (0, 1), (1, 0))])],
                         scale=SCALE_A, sink=None, half=half,
                         values=[VC[:, b, 64 * (2 * p + half):64 * (2 * p + half) + 64] for b in range(QT)],
                         o0=t * P, first=t == 0, layer="C", pair=p, pair_first=t == 0,
                         out=OG[:, p, :] if t == QT - 1 else None, width=S)
        C_END = len(units) // 2
        group_of, g = {}, 0
        for m in range(C_END):
            group_of[m] = g
            g += units[2 * m]["out"] is not None
        per_pair = {"A": 6, "B": 4, "C": 4}
        start_of = {"A": 0, "B": A_END, "C": B_END}

        def pair_scored(layer, p):
            return 2 * (start_of[layer] + per_pair[layer] * (p + 1))

        def weight(name):
            return UB[:, RESIDENT.index(name)] if name in RESIDENT else WS[:, in_ring.index(name) % N_SPLIT]

        def reach(way, j):
            return (j * P, S) if way == 0 else (0, (j + 1) * P)

        def key_tiles(way):
            return range(QT) if way == 0 else range(QT - 1, -1, -1)

        V_FREED = ["C.v0", "C.v1", "C.v2", "D.v0", "D.v1", "D.v2"]

        @block.tensor
        def _(pe):
            opened = []

            def acc_open(name):
                b, i = tasks[name]
                opened.append(name)
                if i > 1:
                    pe.wait_ge(acc_read[b], i - 1)
                return bank[b]

            def acc_close(mm, name):
                mm.then_inc(acc_ready[tasks[name][0]], 1)

            def chunk_ready(name):
                pe.wait_ge(lo_done, split_at[name] + 1)

            def sum_of(out, products):
                for i, (stationary, moving) in enumerate(products):
                    mm = pe.matmul(out, stationary, moving, start=i == 0, stop=i == len(products) - 1)
                return mm

            def three(w, x):
                return [(w[0], x[0]), (w[0], x[1]), (w[1], x[0])]

            def project(name, chunk, src, t0, t1, nk=KD, at=0, ready=None):
                out = acc_open(name)
                chunk_ready(chunk)
                w = weight(chunk)
                for k in range(nk):
                    if ready:
                        ready(k)
                    for i, (a, b) in enumerate(three((w[:, 0, at + k * P:at + k * P + P], w[:, 1, at + k * P:at + k * P + P]),
                                                     (src[0][:, k, t0:t1], src[1][:, k, t0:t1]))):
                        mm = pe.matmul(out[:, 0:t1 - t0], a, b, start=k == 0 and i == 0, stop=k == nk - 1 and i == 2)
                acc_close(mm, name)

            def rotate(name, raw_name, raw):
                out = acc_open(name)
                b, i = tasks[raw_name]
                pe.wait_ge(acc_read[b], i)
                acc_close(pe.matmul(out, perm, raw, start=True, stop=True), name)

            def ada_rows(layer, b):
                name = f"ada{layer}.{b}"
                out = acc_open(name)
                pe.wait_ge(silc_done, 1)
                for k in range(KD):
                    c = chunk_at[f"{name}.{k // 2}"]
                    if k % 2 == 0:
                        pe.wait_ge(raw_in[c % N_RAW], 16 * (c // N_RAW + 1))
                    g = k % 4
                    mm = pe.matmul(out[32 * g:32 * g + 2, :], SILC[:, layer // 2, k, :],
                                   RAW[:, c % N_RAW, (k % 2) * 512:(k % 2) * 512 + 512], start=k < 4, stop=k >= 4)
                acc_close(mm, name)

            def ada_columns(layer, b):
                name = f"ada{layer}.{b}.t"
                out = acc_open(name)
                rows, i = tasks[f"ada{layer}.{b}"]
                pe.wait_ge(acc_read[rows], i)
                for i in range(4):
                    mm = pe.transpose(out[:, i * P:i * P + P], AROW[:, i * P:i * P + P], ident)
                acc_close(mm, name)

            def make(name):
                what, part = name.split(".")[1], name.split(".")[-1]
                if name.startswith("ada"):
                    layer, b = int(name[3]), int(what)
                    ada_columns(layer, b) if part == "t" else ada_rows(layer, b)
                elif name.startswith("A."):
                    if what[0:2] == "qg":
                        out = acc_open(name)
                        for at, chunk in ((0, f"A.q{what[2:]}"), (C, f"A.g{what[2:]}")):
                            chunk_ready(chunk)
                            w = weight(chunk)
                            mm = sum_of(out[:, at:at + C], [
                                ab for k in range(KD) for ab in three((w[:, 0, k * P:k * P + P], w[:, 1, k * P:k * P + P]),
                                                                      (HA[0][:, k, S:T], HA[1][:, k, S:T]))])
                        acc_close(mm, name)
                    elif part == "rot":
                        rotate(name, name[:-3] + "x", QRAW)
                    else:
                        project(name, name[:-2], HA, *((0, S) if part == "x" else (S, T)))
                elif name.startswith("B.qn"):
                    p = int(what[2:])
                    project(name, f"B.uq{p // 4}", (CQN[:, 0], CQN[:, 1]), 0, S, nk=2, at=256 * (p % 4))
                elif name.startswith("B.kn"):
                    p = int(what[2:])
                    project(name, "B.uk", (CKN[:, 0:1], CKN[:, 1:2]), *((0, S) if part == "x" else (S, T)), nk=1, at=P * p)
                elif name.startswith("C."):
                    project(name, name[:-2], HC, 0, S)
                else:
                    raise ValueError(name)

            def scores(n):
                u = units[n]
                if n >= 2:
                    pe.wait_ge(exp_done, n - 1)
                for c0, width, products in u["segments"]:
                    mm = sum_of(SC[n % 2][:, c0:c0 + width], products)
                mm.then_inc(s_ready, 1)

            def turn(n):
                u = units[n]
                pe.wait_ge(p_ready, n + 1)
                if n >= 1:
                    pe.wait_ge(pt_read, n)
                for i in range(len(u["values"])):
                    mm = pe.transpose(PTP[:, i * P:i * P + P], PROB[:, n % 2, i * P:i * P + P], ident)
                mm.then_inc(pt_ready, 1)

            def weigh_values(m):
                a, b = units[2 * m], units[2 * m + 1]
                pe.wait_ge(pt_read, 2 * m + 2)
                if a["first"] and group_of[m] >= 1:
                    pe.wait_ge(o_read, group_of[m])
                nk = len(a["values"])
                for i in range(nk):
                    for u in (a, b):
                        h = u["half"]
                        mm = pe.matmul(bank[6][64 * h:64 * h + 64, u["o0"]:u["o0"] + P], u["values"][i],
                                       PT[:, m % 2, h, i * P:i * P + P], start=i == 0, stop=i == nk - 1,
                                       skip_group_check=True)
                mm.then_inc(pv_done, 1)

            def attend(m0, m1, pair_ready, fillers):
                for b in (0, 1, 2, 3, 4, 5, 6, 7):
                    last = max((tasks[n][1] for n in opened if tasks[n][0] == b), default=0)
                    if last:
                        pe.wait_ge(acc_read[b], last)
                for m in range(m0, m1 + 2):
                    if m < m1:
                        if units[2 * m]["pair_first"]:
                            pair_ready(units[2 * m]["pair"])
                        scores(2 * m)
                        scores(2 * m + 1)
                    if m0 <= m - 1 < m1:
                        turn(2 * (m - 1))
                    if m0 <= m - 2 < m1:
                        weigh_values(m - 2)
                    if m0 <= m - 1 < m1:
                        turn(2 * (m - 1) + 1)
                    if m < m1:
                        for name in fillers(m):
                            make(name)
                pe.wait_ge(exp_done, 2 * m1)
                pe.wait_ge(pt_read, 2 * m1)
                pe.wait_ge(o_read, group_of[m1 - 1] + 1)

            def stats(j, base, jobs):
                pe.wait_ge(sq_done, base + j + 1)
                for name, moving in jobs:
                    out = acc_open(name) if j == 0 else bank[tasks[name][0]]
                    mm = pe.matmul(out[:, 0:moving.shape[-1]], ones, moving, start=j == 0, stop=j == KD - 1)
                    if j == KD - 1:
                        acc_close(mm, name)
                if j < KD - 1:
                    mm.then_inc(sq_read, 1)

            pe.wait_ge(consts_ready, 1)
            for j in range(KD):
                stats(j, 0, [("A.stat.x", SQ[:, j % 2, 0:S]), ("A.stat.c", SQ[:, j % 2, S:T])])
            for b in range(6):
                ada_rows(0, b)
                if b >= 1:
                    ada_columns(0, b - 1)
            ada_columns(0, 5)
            h_ready = lambda base: (lambda k: pe.wait_ge(hlo_done, base + k + 1))
            for j in range(2):
                project(f"A.k{j}.x", f"A.k{j}", HA, 0, S, ready=h_ready(0) if j == 0 else None)
                project(f"A.k{j}.c", f"A.k{j}", HA, S, T)
                rotate(f"A.k{j}.rot", f"A.k{j}.x", QRAW)
            for t in range(T // P):
                out = acc_open(f"A.v.{t}")
                for k in range(KD):
                    chunk = f"A.v{k // 4}"
                    chunk_ready(chunk)
                    w = weight(chunk)
                    for i, (a, b) in enumerate(three((HA[0][:, k, t * P:t * P + P], HA[1][:, k, t * P:t * P + P]),
                                                     (w[:, 0, (k % 4) * 256:(k % 4) * 256 + 256],
                                                      w[:, 1, (k % 4) * 256:(k % 4) * 256 + 256]))):
                        mm = pe.matmul(out[:, 0:256], a, b, start=k == 0 and i == 0, stop=k == KD - 1 and i == 2)
                acc_close(mm, f"A.v.{t}")
            for name in ("A.q0.x", "A.q0.rot", "A.qg0.c", "A.g0.x"):
                make(name)

            def ready_a(p):
                pe.wait_ge(q_lo, p + 1)
                if p == 0:
                    pe.wait_ge(kz_done, 2)

            attend(0, A_END, ready_a, lambda m: fillers_a(m // 6 + 1, m % 6) if m // 6 + 1 < N_PAIR else [])
            for j in range(KD):
                ready = (lambda k: (pe.wait_ge(og_hi, k + 1), pe.wait_ge(og_lo, k + 1))) if j == 0 else None
                project(f"A.o{j}.x", f"A.o{j}", OA, 0, S, ready=ready)
                project(f"A.o{j}.c", f"A.o{j}", OA, S, T)
                if j >= 1:
                    stats(j - 1, 8, [("B.stat.x", SQ[:, (j - 1) % 2, 0:S]), ("B.stat.c", SQ[:, (j - 1) % 2, S:T])])
            stats(7, 8, [("B.stat.x", SQ[:, 1, 0:S]), ("B.stat.c", SQ[:, 1, S:T])])
            for b in range(6):
                ada_rows(2, b)
                if b >= 1:
                    ada_columns(2, b - 1)
            ada_columns(2, 5)
            for name in ("B.cq0.x", "B.cq1.x", "B.ckv.x", "B.ckv.c", "B.kr.x", "B.kr.c"):
                project(name, name[:-2], HA, *((0, S) if name[-1] == "x" else (S, T)),
                        ready=h_ready(8) if name == "B.cq0.x" else None)
            for j in range(KD):
                project(f"B.g{j}.x", f"B.g{j}", HA, 0, S)
                if j == 1:
                    pe.wait_ge(sp_rope, 32)
                    rotate("B.kr.rot", "B.kr.x", QRAWB)
                    pe.wait_ge(lat_sq, 1)
                    out = acc_open("B.cq.stat")
                    for k in range(2):
                        mm = pe.matmul(out, ones, SQCQ[:, k, :], start=k == 0, stop=k == 1)
                    acc_close(mm, "B.cq.stat")
                    pe.wait_ge(lat_sq, 2)
                    acc_close(pe.matmul(acc_open("B.ckv.stat.x"), ones, SQCK[:, 0:S], start=True, stop=True), "B.ckv.stat.x")
                    acc_close(pe.matmul(acc_open("B.ckv.stat.c")[:, 0:C], ones, SQCK[:, S:T], start=True, stop=True),
                              "B.ckv.stat.c")
            pe.wait_ge(ckn_ready, 1)
            chunk_ready("B.uv")
            w = weight("B.uv")
            for t in range(T // P):
                for h in range(2):
                    mm = sum_of(acc_open(f"B.v.{t}.{h}"), three(
                        (CKN[:, 0, t * P:t * P + P], CKN[:, 1, t * P:t * P + P]),
                        (w[:, 0, 512 * h:512 * h + 512], w[:, 1, 512 * h:512 * h + 512])))
                    acc_close(mm, f"B.v.{t}.{h}")
            pe.wait_ge(cqn_ready, 1)
            for i in range(4):
                project(f"B.qr{i}.x", "B.uqr", (CQN[:, 0], CQN[:, 1]), 0, S, nk=2, at=256 * i)
                if i >= 1:
                    rotate(f"B.qr{i - 1}.rot", f"B.qr{i - 1}.x", QRAWB)
            rotate("B.qr3.rot", "B.qr3.x", QRAWB)
            for step in range(3):
                make(*fillers_b(0, step))

            def ready_b(p):
                pe.wait_ge(b_ready, p + 1)

            attend(A_END, B_END, ready_b,
                   lambda m: fillers_b((m - A_END) // 4 + 1, (m - A_END) % 4) if (m - A_END) // 4 + 1 < N_PAIR else [])
            for j in range(KD):
                ready = (lambda k: (pe.wait_ge(og_hi, 8 + k + 1), pe.wait_ge(og_lo, 8 + k + 1))) if j == 0 else None
                project(f"B.o{j}.x", f"B.o{j}", OB, 0, S, ready=ready)
                if j >= 1:
                    stats(j - 1, 16, [("C.stat.1", SQ2[:, (j - 1) % 2, 0, :]), ("C.stat.2", SQ2[:, (j - 1) % 2, 1, :])])
            stats(7, 16, [("C.stat.1", SQ2[:, 1, 0, :]), ("C.stat.2", SQ2[:, 1, 1, :])])

            def values_by_token(layer, ready=None):
                outs = [acc_open(f"{layer}.v.{t}") for t in range(QT)]
                for c in range(4):
                    chunk_ready(f"{layer}.v{c}")
                    w = weight(f"{layer}.v{c}")
                    for r in range(2):
                        k = 2 * c + r
                        if ready:
                            ready(k)
                        for t in range(QT):
                            for i, (a, b) in enumerate(three((HC[0][:, k, t * P:t * P + P], HC[1][:, k, t * P:t * P + P]),
                                                             (w[:, 0, r * 512:r * 512 + 512], w[:, 1, r * 512:r * 512 + 512]))):
                                mm = pe.matmul(outs[t], a, b, start=k == 0 and i == 0, stop=k == KD - 1 and i == 2)
                            if k == KD - 1:
                                acc_close(mm, f"{layer}.v.{t}")
                    if c < 3:
                        mm.then_inc(v_used, 1)

            values_by_token("C", h_ready(16))
            for name in ("C.q0.x", "C.k0.x", "C.z0.x"):
                make(name)

            def ready_c(p):
                pe.wait_ge(c_ready, p + 1)
                pe.wait_ge(bias_lo, p + 1)

            attend(B_END, C_END, ready_c,
                   lambda m: fillers_c((m - B_END) // 4 + 1, (m - B_END) % 4) if (m - B_END) // 4 + 1 < N_NA else [])
            project("D.gate.x", "D.gate", HC, 0, S)
            values_by_token("D")
            out = acc_open("D.gcol")
            pe.wait_ge(gates_max, 1)
            for way in range(2):
                for j in range(QT):
                    at = 4 * (QT * way + j)
                    mm = pe.transpose(out[:, at:at + 4], ROWS[0:4, 0, way, j * P:j * P + P], ident[0:4, 0:4])
            acc_close(mm, "D.gcol")
            project("D.q0.x", "D.q0", HC, 0, S)
            project("D.k0.x", "D.k0", HC, 0, S)
            for h in range(N_ML + 1):
                if h < N_ML:
                    project(f"D.o{h}.x", f"D.o{h}", HC, 0, S)
                    pe.wait_ge(qk_lo, 2 * h + 2)
                    for j in range(QT):
                        q, k = QM[:, h % 2], KM[:, h % 2, :, j * P:j * P + P]
                        acc_close(sum_of(acc_open(f"D.s{h}.{j}"), three((k[:, 0], k[:, 1]), (q[:, 0], q[:, 1]))), f"D.s{h}.{j}")
                if h >= 1:
                    out = acc_open(f"D.mu{h - 1}")
                    pe.wait_ge(hm_ready, h)
                    acc_close(pe.matmul(out, ones, HM, start=True, stop=True), f"D.mu{h - 1}")
                if h < N_ML:
                    project(f"D.z{h}.x", f"D.z{h}", HC, 0, S)
                if h >= 1:
                    out = acc_open(f"D.var{h - 1}")
                    pe.wait_ge(sqd_ready, h)
                    acc_close(pe.matmul(out, ones, SQD, start=True, stop=True), f"D.var{h - 1}")
                if h + 1 < N_ML:
                    project(f"D.q{h + 1}.x", f"D.q{h + 1}", HC, 0, S)
                if h < N_ML:
                    for way in range(2):
                        names = [f"D.{kind}{h}.{'fb'[way]}" for kind in ("num", "den")]
                        outs = [acc_open(name) for name in names]
                        for i, j in enumerate(key_tiles(way)):
                            pe.wait_ge(pm_ready, 8 * h + 4 * way + i + 1)
                            t0, t1 = reach(way, j)
                            for name, acc, stationary in zip(names, outs, (MV[:, j, h * P:h * P + P], ones)):
                                mm = pe.matmul(acc[:, t0:t1], stationary, PM[:, way, j, t0:t1], start=i == 0,
                                               stop=i == QT - 1, skip_group_check=True)
                                if i == QT - 1:
                                    acc_close(mm, name)
                if h + 1 < N_ML:
                    project(f"D.k{h + 1}.x", f"D.k{h + 1}", HC, 0, S)
            for j in range(KD):
                ready = (lambda k: (pe.wait_ge(og_hi, 16 + k + 1), pe.wait_ge(og_lo, 16 + k + 1))) if j == 0 else None
                project(f"C.o{j}.x", f"C.o{j}", OB, 0, S, ready=ready)
                if j >= 1:
                    stats(j - 1, 24, [("E.stat", SQ[:, (j - 1) % 2, 0:S])])
            stats(7, 24, [("E.stat", SQ[:, 1, 0:S])])

        @block.scalar
        def _(act):
            fed = [0]

            def feed(upto):
                while fed[0] < min(upto, len(splits)):
                    name = splits[fed[0]]
                    c = chunk_at[name]
                    act.wait_ge(raw_in[c % N_RAW], 16 * (c // N_RAW + 1))
                    if name in in_ring:
                        r = in_ring.index(name)
                        if r >= N_SPLIT:
                            old = in_ring[r - N_SPLIT]
                            if old in V_FREED:
                                act.wait_ge(v_used, V_FREED.index(old) + 1)
                            else:
                                b, i = tasks[last_use[old]]
                                act.wait_ge(acc_ready[b], i)
                    act.activation(weight(name)[:, 0, :], RAW[:, c % N_RAW, :], ACT.Copy).then_inc(hi_done, 1)
                    fed[0] += 1

            def need(name, ahead=N_SPLIT):
                feed(split_at[name] + ahead)

            def wait_acc(name):
                b, i = tasks[name]
                act.wait_ge(acc_ready[b], i)
                return bank[b]

            def read(ins, name):
                ins.then_inc(acc_read[tasks[name][0]], 1)

            chain = [0]

            def step(ins):
                chain[0] += 1
                ins.then_inc(act_step, 1)
                act.wait_ge(act_step, chain[0])

            def squares(j, base, reads, jobs):
                if j >= 2:
                    act.wait_ge(sq_read, reads + j - 1)
                for out, in_, scale in jobs:
                    ins = act.activation(out, in_, ACT.Square, scale=scale)
                ins.then_inc(sq_done, 1)

            def root(stats, dst):
                for name, n, out in stats:
                    act.activation(out, wait_acc(name)[:, 0:n], ACT.Sqrt, scale=1.0 / D, bias=EPS).then_inc(root_done, 1)

            def modulated(layer, parts, base):
                for k in range(KD):
                    act.wait_ge(xn_done, base + k + 1)
                    if k == 0:
                        act.wait_ge(mod_done, layer + 1)
                    if k >= 2:
                        act.wait_ge(hlo_done, base + k - 1)
                    for v, (src, dst) in enumerate(parts(k)):
                        ins = act.activation(dst, src, ACT.Identity, scale=GAIN[:, layer, k, v:v + 1],
                                             bias=MOD[:, layer, k, v:v + 1])
                    ins.then_inc(hf_done, 1)

            act.wait_ge(sp_x, 32)
            act.wait_ge(consts_ready, 1)
            act.activation(SILT, col("c", 0, 32), ACT.Tanh, scale=0.5).then_inc(silt_done, 1)
            for j in range(KD):
                squares(j, 0, 0, [(SQ[:, j % 2, 0:S], XL[:, j, :], 1.0), (SQ[:, j % 2, S:T], XC[:, j, :], 1.0)])
            root([("A.stat.x", S, RSTD[:, 0:S]), ("A.stat.c", C, RSTD[:, S:T])], None)
            feed(3)
            modulated(0, lambda k: [(XN[:, k % 2, 0:S], SQ[:, k % 2, 0:S]), (XN[:, k % 2, S:T], SQ[:, k % 2, S:T])], 0)

            ropes = [0]

            def rope_raw(name, dst, rows=P):
                r = ropes[0]
                ropes[0] += 1
                if r >= 1:
                    act.wait_ge(rope_sum, r)
                read(act.activation(dst, wait_acc(name), ACT.Copy), name)

            def chunk_of(name):
                return name[:-2].replace("qg", "g") if part_of(name) == "c" else name[:-2]

            def part_of(name):
                return name[-1]

            def evac_a(name):
                need(chunk_of(name), 1)
                what, part = name.split(".")[1], name.split(".")[2]
                if what[0] in "qk" and part == "x":
                    rope_raw(name, QRAW)
                elif what[0] == "k":
                    if what == "k1":
                        act.wait_ge(kz_done, 1)
                    read(act.activation(QP[:, S:T], wait_acc(name)[:, 0:C], ACT.Copy), name)
                elif what[0:2] == "qg":
                    p = int(what[2:])
                    if p >= 1:
                        act.wait_ge(q_lo, p)
                    else:
                        act.wait_ge(kz_done, 2)
                    act.activation(QP[:, S:T], wait_acc(name)[:, 0:C], ACT.Copy)
                    act.activation(OGC[:, p, :], wait_acc(name)[:, C:2 * C], ACT.Tanh, scale=0.5).then_inc(tanh_done, 1)
                else:
                    act.activation(OG[:, int(what[1:]), :], wait_acc(name), ACT.Tanh, scale=0.5).then_inc(tanh_done, 1)
                need(chunk_of(name), 2)

            for name in ("A.k0.x", "A.k0.c", "A.k1.x", "A.k1.c", "A.q0.x", "A.qg0.c", "A.g0.x"):
                evac_a(name)

            def attend(m0, m1, evacs):
                def exps(n):
                    u = units[n]
                    act.wait_ge(nm_ready, n + 1)
                    if n >= 2:
                        act.wait_ge(pt_ready, n - 1)
                    i = n % 4
                    if u["sink"] is not None:
                        act.activation(STAT[:, 3, i:i + 1], u["sink"], ACT.Exp, bias=STAT[:, 1, i:i + 1])
                    act.activation(PROB[:, n % 2, 0:u["c1"] - u["c0"]], SC[n % 2][:, u["c0"]:u["c1"]], ACT.Exp,
                                   bias=STAT[:, 1, i:i + 1], scale=u["scale"],
                                   accum_out=STAT[:, 2, i:i + 1]).then_inc(exp_done, 1)

                def turned(n):
                    m, w = n // 2, P * len(units[n]["values"])
                    act.wait_ge(pt_ready, n + 1)
                    if m >= 2:
                        act.wait_ge(pv_done, m - 1)
                    act.activation(PT[:, m % 2, n % 2, 0:w], PTP[:, 0:w], ACT.Copy).then_inc(pt_read, 1)

                for m in range(m0, m1 + 1):
                    if m > m0:
                        evacs(m - 1)
                    if m > m0:
                        turned(2 * m - 2)
                    if m < m1:
                        exps(2 * m)
                    if m > m0:
                        turned(2 * m - 1)
                    if m < m1:
                        exps(2 * m + 1)

            def out_high(layer, j, dst, parts):
                for i, (src, t0, t1) in enumerate(parts):
                    ins = act.activation(dst[0][:, j, t0:t1], src[:, j, :], ACT.Copy)
                ins.then_inc(og_hi, 1)

            A_PARTS = [(OG, 0, S), (OGC, S, T)]

            def out_high_a(j):
                act.wait_ge(o_read, 2 * j + 2)
                if j == 0:
                    b, i = tasks["A.g7.x"]
                    act.wait_ge(acc_ready[b], i)
                out_high("A", j, OA, A_PARTS)

            def evacs_a(m):
                p = m // 6 + 1
                if p == N_PAIR:
                    out_high_a(m % 6)
                if p < N_PAIR:
                    for name in fillers_a(p, m % 6):
                        if not name.startswith("ada") and not name.endswith("rot"):
                            evac_a(name)

            attend(0, A_END, evacs_a)
            for j in (6, 7):
                out_high_a(j)
            for j in range(KD):
                need(f"A.o{min(j + 2, KD - 1)}", 1)
                act.wait_ge(x_new, j + 1)
                squares(j, 8, 7, [(SQ[:, j % 2, 0:S], XL[:, j, :], 1.0), (SQ[:, j % 2, S:T], XC[:, j, :], 1.0)])
            root([("B.stat.x", S, RSTD[:, 0:S]), ("B.stat.c", C, RSTD[:, S:T])], None)
            modulated(1, lambda k: [(XN[:, k % 2, 0:S], SQ[:, k % 2, 0:S]), (XN[:, k % 2, S:T], SQ[:, k % 2, S:T])], 8)

            def copy_out(name, dst, n):
                need(name[:-2], 4)
                read(act.activation(dst, wait_acc(name)[:, 0:n], ACT.Copy), name)

            copy_out("B.cq0.x", CQR[:, 0, :], S)
            copy_out("B.cq1.x", CQR[:, 1, :], S)
            copy_out("B.ckv.x", CKR[:, 0:S], S)
            copy_out("B.ckv.c", CKR[:, S:T], C)
            b, i = tasks["B.ckv.c"]
            act.wait_ge(acc_read[b], i)
            act.activation(SQCQ, CQR, ACT.Square).then_inc(lat_sq, 1)
            act.activation(SQCK, CKR, ACT.Square).then_inc(lat_sq, 1)
            need("B.kr", 4)
            rope_raw("B.kr.x", QRAWB)
            read(act.activation(KRF[:, S:T], wait_acc("B.kr.c")[:, 0:C], ACT.Copy), "B.kr.c")

            def gate_b(j):
                need(f"B.g{j}", 4)
                act.activation(OG[:, j, :], wait_acc(f"B.g{j}.x"), ACT.Tanh, scale=0.5).then_inc(tanh_done, 1)

            gate_b(0)
            gate_b(1)
            for name, out, n, width in (("B.cq.stat", RSQ, S, 256), ("B.ckv.stat.x", RSK[:, 0:S], S, 128),
                                        ("B.ckv.stat.c", RSK[:, S:T], C, 128)):
                act.activation(out, wait_acc(name)[:, 0:n], ACT.Sqrt, scale=1.0 / width, bias=EPS).then_inc(root_done, 1)
            for j in range(2, KD):
                gate_b(j)
            for t in range(T // P):
                need("B.uv", 4)
                name = f"B.v.{t}.0"
                read(act.activation(VB[:, t, 0:512], wait_acc(name), ACT.Copy), name)
            for i in range(4):
                need("B.uqr", 4)
                rope_raw(f"B.qr{i}.x", QRAWB)

            def evac_b(name):
                p, part = int(name[4:-2]), name[-1]
                if p >= 2:
                    act.wait_ge(s_ready, pair_scored("B", p - 2))
                acc = wait_acc(name)
                t0, t1 = (0, S) if part == "x" else (S, T)
                for half in range(2):
                    dst = QB[0:64, 0, p % 2, half, :] if name[2] == "q" else KB[0:64, 0, p % 2, half, t0:t1]
                    ins = act.activation(dst, acc[64 * half:64 * half + 64, 0:t1 - t0], ACT.Copy)
                ins.then_inc(b_hi, 1)

            for part in range(3):
                evac_b(*fillers_b(0, part))

            def evacs_b(m):
                p, s = (m - A_END) // 4 + 1, (m - A_END) % 4
                if p < N_PAIR:
                    for name in fillers_b(p, s):
                        if not name.startswith("ada"):
                            evac_b(name)

            attend(A_END, B_END, evacs_b)
            need("B.o0", 2)
            for j in range(KD):
                act.wait_ge(o_read, 16 + 8)
                out_high("B", j, OB, [(OG, 0, S)])
            for j in range(KD):
                need(f"B.o{j}", 3)
                act.wait_ge(x_new, 8 + j + 1)
                squares(j, 16, 14, [(SQ2[:, j % 2, 0, :], XL[:, j, :], 1.0), (SQ2[:, j % 2, 1, :], XL[:, j, :], col("fg", j))])
            root([("C.stat.1", S, RSTD2[:, 0, :])], None)
            act.wait_ge(ms2_done, 1)
            act.activation(RSTD2[:, 1, :], XNC[:, 1, :], ACT.Sqrt, scale=1.0 / D, bias=EPS).then_inc(root2_done, 1)
            modulated(2, lambda k: [(XNC[:, k % 2, :], SQ2[:, k % 2, 0, :])], 16)

            def bias_high(p):
                act.wait_ge(bias_raw, p + 1)
                if p >= 2:
                    act.wait_ge(s_ready, pair_scored("C", p - 2))
                act.activation(BIAS[p % 2][0], BRAW2, ACT.Copy).then_inc(bias_hi, 1)

            def evac_c(name):
                what, p = name[2], int(name[3:-2])
                need(f"C.z{p}", 1)
                acc = wait_acc(name)
                if what in "qk" and p >= 2:
                    act.wait_ge(s_ready, pair_scored("C", p - 2))
                if what == "q":
                    act.activation(QC[:, 0, p % 2, :], acc, ACT.Identity, bias=col("bna", p)).then_inc(c_hi, 1)
                elif what == "k":
                    for half in range(2):
                        h = slice(64 * half, 64 * half + 64)
                        ins = act.activation(KC[h, 0, p % 2, half, :], acc[h, :], ACT.Identity, bias=col("bna", 4 + p)[h, :])
                    ins.then_inc(c_hi, 1)
                else:
                    if p >= 1:
                        act.wait_ge(zg_done, p)
                    read(act.activation(ZB, acc, ACT.Identity, bias=col("bna", 8 + p)), name)
                    b, i = tasks[name]
                    act.wait_ge(acc_read[b], i)
                    act.activation(ZT, ZB, ACT.Tanh, scale=0.5).then_inc(tanh_done, 1)

            bias_high(0)
            need("C.v0", 3)
            need("C.v3", 3)
            for name in ("C.q0.x", "C.k0.x", "C.z0.x"):
                evac_c(name)
            need("C.q1", 1)

            def evacs_c(m):
                p, s = (m - B_END) // 4 + 1, (m - B_END) % 4
                if p < N_NA:
                    for name in fillers_c(p, s):
                        evac_c(name)
                    if s == 2:
                        bias_high(p)
                    if s == 3:
                        need(f"C.z{p}", 2)

            attend(B_END, C_END, evacs_c)

            act.wait_ge(vm_ready, 1)
            need("D.v1", 1)
            read(act.activation(GALL, wait_acc("D.gate.x"), ACT.Identity, bias=col("bg")), "D.gate.x")
            need("D.v3", 1)
            act.wait_ge(gates_abs, 1)
            step(act.activation(GL[0:4], GX[0:4], ACT.Exp, scale=-1.0))
            act.activation(GL[0:4], GL[0:4], ACT.Ln, bias=1.0).then_inc(gates_log, 1)
            need("D.k0", 1)
            act.wait_ge(gates_max, 1)
            act.activation(ROWS[0:4, 2], GX[0:4], ACT.Exp, scale=-1.0).then_inc(rows_ready, 1)
            need("D.o0", 1)

            def conv_input(h, what):
                i = "qk".index(what)
                name = f"D.{what}{h}.x"
                if h >= 1:
                    act.wait_ge(conv_done, 2 * h + i - 1)
                read(act.activation(U[:, i, 2:2 + S], wait_acc(name), ACT.Identity, bias=col("bml", 4 * i + h)), name)

            def conv_tanh(h, what):
                i = "qk".index(what)
                act.wait_ge(conv_done, 2 * h + i + 1)
                if 2 * h + i >= 1:
                    act.wait_ge(tq_used, 2 * h + i)
                act.activation(TQ, CV[:, i], ACT.Tanh, scale=0.5).then_inc(tq_ready, 1)

            def decay(h, way):
                act.wait_ge(rows_in[h % 2], 16 * (h // 2 + 1))
                act.wait_ge(xd_ready, 2 * h + way + 1)
                for i, j in enumerate(key_tiles(way)):
                    n = 8 * h + 4 * way + i
                    if n >= 4:
                        act.wait_ge(pm_ready, n - 3)
                    t0, t1 = reach(way, j)
                    g = GCOL[:, way, j, h:h + 1]
                    w = W[:, n % 4]
                    ins = act.activation(w[:, j * P:j * P + P], XD[:, way, j], ACT.Exp, bias=g)
                    t0, t1 = ((j + 1) * P, S) if way == 0 else (0, j * P)
                    if t1 > t0:
                        ins = act.activation(w[:, t0:t1], RB[:, h % 2, 0, way, t0:t1], ACT.Exp, bias=g)
                    ins.then_inc(w_ready, 1)

            conv_input(0, "q")
            need("D.z0", 1)
            conv_tanh(0, "q")
            conv_input(0, "k")
            need("D.k0", 4)
            conv_tanh(0, "k")
            for h in range(N_ML + 1):
                if h < N_ML:
                    if h >= 1:
                        act.wait_ge(hm_ready, h)
                    name = f"D.o{h}.x"
                    read(act.activation(TO, wait_acc(name), ACT.Tanh, scale=0.5, bias=HALF_B[:, 8 + h:9 + h]), name)
                    need(f"D.o{h}", 4)
                    decay(h, 0)
                if h >= 1:
                    act.wait_ge(dv_ready, h)
                    act.activation(SQD, DV, ACT.Square).then_inc(sqd_ready, 1)
                if h < N_ML:
                    decay(h, 1)
                if h >= 1:
                    act.activation(RSM, wait_acc(f"D.var{h - 1}"), ACT.Sqrt, scale=1.0 / P, bias=4 * EPS).then_inc(root_done, 1)
                if h < N_ML:
                    if h >= 1:
                        act.wait_ge(ml_done, h)
                    name = f"D.z{h}.x"
                    acc = wait_acc(name)
                    act.activation(ZTM, acc, ACT.Tanh, scale=0.5, bias=HALF_B[:, 12 + h:13 + h])
                    read(act.activation(ZM, acc, ACT.Identity, scale=0.5, bias=HALF_B[:, 12 + h:13 + h]), name)
                    need(f"D.z{h}", 4)
                if h + 1 < N_ML:
                    conv_input(h + 1, "q")
                    need(f"D.q{h + 1}", 4)
                    conv_tanh(h + 1, "q")
                    conv_input(h + 1, "k")
                    need(f"D.k{h + 1}", 4)
                    conv_tanh(h + 1, "k")
                if h == N_ML - 1:
                    for j in range(4):
                        out_high("C", j, OB, [(OG, 0, S)])
            for j in range(4, KD):
                act.wait_ge(ml_done, j - 3)
                out_high("C", j, OB, [(OG, 0, S)])
            for j in range(KD):
                need(f"C.o{j}", 3)
                act.wait_ge(x_new, 16 + j + 1)
                squares(j, 24, 21, [(SQ[:, j % 2, 0:S], XL[:, j, :], 1.0)])
            root([("E.stat", S, RSTD[:, 0:S])], None)

        @block.vector
        def _(dve):
            chain = [0]

            def step(ins):
                chain[0] += 1
                ins.then_inc(dve_step, 1)
                dve.wait_ge(dve_step, chain[0])

            def wait_acc(name):
                b, i = tasks[name]
                dve.wait_ge(acc_ready[b], i)
                return bank[b]

            def read(ins, name):
                b, i = tasks[name]
                ins.then_inc(acc_read[b], 1)
                dve.wait_ge(acc_read[b], i)

            def signal(ins, s, value):
                ins.then_inc(s, 1)
                dve.wait_ge(s, value)

            def ada_row(layer, b):
                name = f"ada{layer}.{b}"
                acc = wait_acc(name)
                if b or layer:
                    last = f"ada{layer}.{b - 1}.t" if b else f"ada{layer - 1}.5.t"
                    dve.wait_ge(acc_ready[tasks[last][0]], tasks[last][1])
                read(dve.tensor_copy(AROW, acc), name)

            def ada_column(layer, b):
                name = f"ada{layer}.{b}.t"
                acc = wait_acc(name).rearrange("p (i g r) -> p i r g", i=4, g=4)[:, :, 0:2, :]
                read(dve.tensor_reduce(MOD[:, layer, 4 * b:4 * b + 4, :], acc, AX, ALU.add), name)
                if b == 5:
                    mod = MOD[:, layer].rearrange("p a v -> p (a v)")
                    step(dve.tensor_tensor(mod, mod, col(f"ab{layer}", 0, 48), ALU.add))
                    signal(dve.scalar_tensor_tensor(GAIN[:, layer].rearrange("p a v -> p (a v)"), mod[:, 16:32], 1.0,
                                                    col(f"ng{layer}", 0, 16), ALU.add, ALU.mult), mod_done, layer + 1)

            def modulate(layer, base, parts, h, between=None):
                def high(k):
                    dve.wait_ge(hf_done, base + k + 1)
                    src, dst = parts[1](k), h[0][:, k, :]
                    dve.tensor_copy(dst, src).then_inc(hhi_done, 1)
                for k in range(KD):
                    if k >= 2:
                        dve.wait_ge(hf_done, base + k - 1)
                    for out, in_, rstd in parts[0](k):
                        ins = dve.tensor_tensor(out, in_, rstd, ALU.mult)
                    ins.then_inc(xn_done, 1)
                    if between:
                        between(k)
                    if k >= 1:
                        high(k - 1)
                high(KD - 1)

            step(dve.memset(PS[:, :, :], 0.0))
            step(dve.memset(ones, 1.0))
            dve.wait_ge(sp_const, 16 * N_CONST)
            step(dve.tensor_copy(identR, ident))
            step(dve.tensor_copy(mask3R, PPT[:, 4 * T:4 * T + 384]))
            step(dve.tensor_scalar(NSINK, col("sink", 0, 16), -1.0, None, ALU.mult))
            dve.sem_inc(consts_ready, 1)
            dve.wait_ge(silt_done, 1)
            silc = SILC.rearrange("p l k v -> p (l k v)")
            step(dve.scalar_tensor_tensor(silc, SILT, 1.0, col("c", 0, 32), ALU.add, ALU.mult))
            signal(dve.tensor_scalar(silc, silc, 0.5, None, ALU.mult), silc_done, 1)
            def wait_read(name):
                b, i = tasks[name]
                dve.wait_ge(acc_read[b], i)

            roots = [0]

            def one_over_root(r, sums, t, width, eps=EPS):
                step(dve.reciprocal(r, r))
                step(dve.tensor_tensor(t, r, r, ALU.mult))
                at = 0
                for name, src, n in sums:
                    ins = dve.scalar_tensor_tensor(t[:, at:at + n], src[:, 0:n], width * eps, t[:, at:at + n], ALU.add, ALU.mult)
                    read(ins, name) if name else step(ins)
                    at += n
                step(dve.tensor_scalar(t, t, -0.5 / width, 1.5, ALU.mult, ALU.add))
                step(dve.tensor_tensor(r, r, t, ALU.mult))

            def rstd(names, r, t, width, eps=EPS):
                roots[0] += len(names)
                dve.wait_ge(root_done, roots[0])
                one_over_root(r, [(n, bank[tasks[n][0]], C if n.endswith("c") else S) for n in names], t, width, eps)

            dve.wait_ge(sp_x, 32)
            rstd(("A.stat.x", "A.stat.c"), RSTD, XN[:, 0, :], D)
            for b in range(6):
                ada_row(0, b)
                if b >= 1:
                    ada_column(0, b - 1)
            ada_column(0, 5)

            def normed(base_k):
                return lambda k: [(XN[:, k % 2, 0:S], XL[:, k, :], RSTD[:, 0:S]), (XN[:, k % 2, S:T], XC[:, k, :], RSTD[:, S:T])]

            modulate(0, 0, (normed(0), lambda k: SQ[:, k % 2, :]), HA)

            ropes = [0]

            def rope_turned(name, tmp, dst):
                r = ropes[0]
                ropes[0] += 1
                read(dve.tensor_tensor(tmp, wait_acc(name), ROPE[:, 1, :], ALU.mult), name)
                dve.wait_ge(cos_done, r + 1)
                signal(dve.tensor_tensor(dst, tmp, COSP if r < 10 else COSB, ALU.add), rope_sum, r + 1)

            def split_keys(j):
                wait_read(f"A.k{j}.c")
                dve.wait_ge(kz_zero, 1)
                for half in range(2):
                    h = slice(64 * half, 64 * half + 64)
                    step(dve.tensor_copy(KZ[h, 0, j, half, :], QP[h, :]))
                    low = dve.tensor_tensor(KZ[h, 1, j, half, :], QP[h, :], KZ[h, 0, j, half, :].bitcast(F32), ALU.subtract)
                    if half == 1:
                        signal(low, kz_done, j + 1)

            def rope_q(p):
                if p >= 1:
                    dve.wait_ge(q_lo, p)
                rope_turned(f"A.q{p}.rot", QP[:, 0:S], QP[:, 0:S])

            def high_q(p):
                dve.wait_ge(tanh_done, 2 * p + 1)
                if p >= 2:
                    dve.wait_ge(s_ready, pair_scored("A", p - 2))
                signal(dve.tensor_copy(QA[:, 0, p % 2, :], QP), q_hi, p + 1)

            def gate(name, dst, count, at=0):
                dve.wait_ge(tanh_done, count)
                n = dst.shape[-1]
                read(dve.scalar_tensor_tensor(dst, dst, 1.0, wait_acc(name)[:, at:at + n], ALU.add, ALU.mult), name)

            for j in range(2):
                rope_turned(f"A.k{j}.rot", QP[:, 0:S], QP[:, 0:S])
                split_keys(j)
            for t in range(T // P):
                read(dve.tensor_copy(VA[:, t, :], wait_acc(f"A.v.{t}")[:, 0:256]), f"A.v.{t}")
            rope_q(0)
            high_q(0)
            gate("A.qg0.c", OGC[:, 0, :], 1, C)
            gate("A.g0.x", OG[:, 0, :], 2)

            def attend(m0, m1, others):
                def negmax(n):
                    u, i = units[n], n % 4
                    dve.wait_ge(s_ready, n + 1)
                    step(dve.reduce_max(STAT[:, 0, i:i + 1], SC[n % 2][:, u["c0"]:u["c1"]], AX))
                    if u["sink"] is None:
                        ins = dve.tensor_scalar(STAT[:, 1, i:i + 1], STAT[:, 0, i:i + 1], -u["scale"], None, ALU.mult)
                    else:
                        h = 2 * u["pair"] + u["half"]
                        ins = dve.tensor_scalar(STAT[:, 1, i:i + 1], STAT[:, 0, i:i + 1], -u["scale"],
                                                NSINK[:, h:h + 1], ALU.mult, ALU.min)
                    ins.then_inc(nm_ready, 1)

                def normalise(n):
                    u, i = units[n], n % 4
                    w = u["c1"] - u["c0"]
                    dve.wait_ge(exp_done, n + 1)
                    total = STAT[:, 2, i:i + 1]
                    if u["sink"] is not None:
                        step(dve.tensor_tensor(total, total, STAT[:, 3, i:i + 1], ALU.add))
                    step(dve.reciprocal(STAT[:, 4, i:i + 1], total))
                    dve.tensor_scalar(PROB[:, n % 2, 0:w], PROB[:, n % 2, 0:w], STAT[:, 4, i:i + 1], None,
                                      ALU.mult).then_inc(p_ready, 1)

                def gate_output(m):
                    u = units[2 * m]
                    dve.wait_ge(pv_done, m + 1)
                    signal(dve.scalar_tensor_tensor(u["out"], bank[6][:, 0:u["width"]], 0.5, u["out"], ALU.mult, ALU.mult),
                           o_read, group_of[m] + 1)

                for m in range(m0, m1 + 2):
                    if m0 <= m - 3 and units[2 * (m - 3)]["out"] is not None:
                        gate_output(m - 3)
                    if m0 < m <= m1:
                        others(m - 1)
                    if m < m1:
                        negmax(2 * m)
                        negmax(2 * m + 1)
                    if m < m1:
                        normalise(2 * m)
                        normalise(2 * m + 1)
                gate_output(m1 - 1)

            def others_a(m):
                p = m // 6 + 1
                if p == N_PAIR:
                    return
                for name in fillers_a(p, m % 6):
                    if name.startswith("ada"):
                        layer, b = 1, int(name.split(".")[1])
                        ada_column(layer, b) if name.endswith("t") else ada_row(layer, b)
                    elif name == f"A.q{p}.rot":
                        rope_q(p)
                    elif name == f"A.qg{p}.c":
                        high_q(p)
                        gate(name, OGC[:, p, :], 2 * p + 1, C)
                    elif name == f"A.g{p}.x":
                        gate(name, OG[:, p, :], 2 * p + 2)

            attend(0, A_END, others_a)

            def residual(j, name, x, v, count):
                n = x.shape[-1]
                ins = dve.scalar_tensor_tensor(x[:, j, :], wait_acc(name)[:, 0:n], MOD[:, count, 16 + j, v:v + 1],
                                               x[:, j, :], ALU.mult, ALU.add)
                read(ins, name)

            for j in range(KD):
                residual(j, f"A.o{j}.x", XL, 0, 0)
                residual(j, f"A.o{j}.c", XC, 1, 0)
                dve.sem_inc(x_new, 1)
            rstd(("B.stat.x", "B.stat.c"), RSTD, XN[:, 0, :], D)

            def next_ada(k):
                if k < 6:
                    ada_row(2, k)
                if 1 <= k <= 6:
                    ada_column(2, k - 1)

            modulate(1, 8, (normed(0), lambda k: SQ[:, k % 2, :]), HA, next_ada)

            dve.wait_ge(sp_rope, 32)
            rope_turned("B.kr.rot", KRF[:, 0:S], KRF[:, 0:S])
            gate("B.g0.x", OG[:, 0, :], 17)
            gate("B.g1.x", OG[:, 1, :], 18)

            def split(high, low, src, done=None, value=None):
                step(dve.tensor_copy(high, src))
                ins = dve.tensor_tensor(low, src, high.bitcast(F32), ALU.subtract)
                step(ins) if done is None else signal(ins, done, value)

            rstd(("B.cq.stat",), RSQ, SQCQ[:, 0, :], 256)
            for k in range(2):
                step(dve.scalar_tensor_tensor(CQR[:, k, :], CQR[:, k, :], col("qg", k), RSQ, ALU.mult, ALU.mult))
                split(CQN[:, 0, k, :], CQN[:, 1, k, :], CQR[:, k, :])
            dve.sem_inc(cqn_ready, 1)
            rstd(("B.ckv.stat.x", "B.ckv.stat.c"), RSK[:, 0:T], SQCK, 128)
            step(dve.scalar_tensor_tensor(CKR, CKR, col("kg"), RSK, ALU.mult, ALU.mult))
            split(CKN[:, 0, :], CKN[:, 1, :], CKR, ckn_ready, 1)
            for j in range(2, KD):
                gate(f"B.g{j}.x", OG[:, j, :], 17 + j)
            wait_read("B.kr.c")
            for buf in range(2):
                for half in range(2):
                    split(KB[64:96, 0, buf, half, :], KB[64:96, 1, buf, half, :], KRF[64:96, :])
            for t in range(T // P):
                name = f"B.v.{t}.1"
                read(dve.tensor_copy(VB[:, t, 512:1024], wait_acc(name)), name)
            for i in range(4):
                rope_turned(f"B.qr{i}.rot", QR[:, i, :], QR[:, i, :])
                step(dve.tensor_copy(QRH[:, i, :], QR[:, i, :]))
                step(dve.tensor_tensor(QR[:, i, :], QR[:, i, :], QRH[:, i, :].bitcast(F32), ALU.subtract))

            lows = [0]

            def low_b(name):
                p, part = int(name[4:-2]), name[-1]
                lows[0] += 1
                dve.wait_ge(b_hi, lows[0])
                acc = wait_acc(name)
                t0, t1 = (0, S) if part == "x" else (S, T)
                for half in range(2):
                    buf = QB[0:64, :, p % 2, half, :] if name[2] == "q" else KB[0:64, :, p % 2, half, t0:t1]
                    ins = dve.tensor_tensor(buf[:, 1, :], acc[64 * half:64 * half + 64, 0:t1 - t0],
                                            buf[:, 0, :].bitcast(F32), ALU.subtract)
                read(ins, name)
                if name[2] == "q":
                    for half in range(2):
                        h = 2 * p + half
                        rows = slice(32 * (h % 4), 32 * (h % 4) + 32)
                        step(dve.tensor_copy(QB[64:96, 0, p % 2, half, :], QRH[rows, h // 4, :].bitcast(F32)))
                        step(dve.tensor_copy(QB[64:96, 1, p % 2, half, :], QR[rows, h // 4, :]))
                if name.endswith("c"):
                    dve.sem_inc(b_ready, 1)

            for part in range(3):
                low_b(*fillers_b(0, part))

            def others_b(m):
                p, s = (m - A_END) // 4 + 1, (m - A_END) % 4
                if p < N_PAIR:
                    for name in fillers_b(p, s):
                        low_b(name)

            attend(A_END, B_END, others_b)

            def out_low(layer, j, dst, src):
                dve.wait_ge(og_hi, 8 * layer + j + 1)
                dve.tensor_tensor(dst[1][:, j, :], src, dst[0][:, j, :].bitcast(F32), ALU.subtract).then_inc(og_lo, 1)

            for j in range(KD):
                out_low(1, j, OB, OG[:, j, :])
            for j in range(KD):
                residual(j, f"B.o{j}.x", XL, 0, 1)
                dve.sem_inc(x_new, 1)
            rstd(("C.stat.1",), RSTD2[:, 0, :], XNC[:, 0, :], D)
            ms2 = XNC[:, 1, :]
            read(dve.tensor_tensor(ms2, wait_acc("C.stat.2"), RSTD2[:, 0, :], ALU.mult), "C.stat.2")
            signal(dve.tensor_tensor(ms2, ms2, RSTD2[:, 0, :], ALU.mult), ms2_done, 1)
            for k in range(KD):
                step(dve.scalar_tensor_tensor(XL[:, k, :], XL[:, k, :], col("fg", k), RSTD2[:, 0, :], ALU.mult, ALU.mult))
            dve.wait_ge(root2_done, 1)
            one_over_root(RSTD2[:, 1, :], [(None, ms2, S)], XNC[:, 0, :], D)
            modulate(2, 16, (lambda k: [(XNC[:, k % 2, :], XL[:, k, :], RSTD2[:, 1, :])], lambda k: SQ2[:, k % 2, 0, :]), HC)

            def mask_bias(p):
                dve.wait_ge(bias_in, 64 * (p + 1))
                for half in range(2):
                    mask = CMASK.unsqueeze(1).to_broadcast([P, 14, GRID])
                    ins = dve.scalar_tensor_tensor(BRAW[:, half], BRAW[:, half], 1 / SCALE_A, mask, ALU.mult, ALU.add)
                signal(ins, bias_raw, p + 1)

            lows_c = [0]

            def low_c(name):
                what, p = name[2], int(name[3:-2])
                if what == "z":
                    dve.wait_ge(tanh_done, 24 + p + 1)
                    wait_read(name)
                    signal(dve.scalar_tensor_tensor(OG[:, p, :], ZT, 1.0, ZB, ALU.add, ALU.mult), zg_done, p + 1)
                    return
                lows_c[0] += 1
                dve.wait_ge(c_hi, lows_c[0])
                acc = wait_acc(name)
                if what == "q":
                    ins = dve.scalar_tensor_tensor(QC[:, 1, p % 2, :], acc, col("bna", p),
                                                   QC[:, 0, p % 2, :].bitcast(F32), ALU.add, ALU.subtract)
                else:
                    for half in range(2):
                        h = slice(64 * half, 64 * half + 64)
                        ins = dve.scalar_tensor_tensor(KC[h, 1, p % 2, half, :], acc[h, :], col("bna", 4 + p)[h, :],
                                                       KC[h, 0, p % 2, half, :].bitcast(F32), ALU.add, ALU.subtract)
                read(ins, name)
                if what == "k":
                    dve.sem_inc(c_ready, 1)

            mask_bias(0)
            dve.wait_ge(sp_vb, 32)
            for t in range(QT):
                read(dve.tensor_tensor(VC[:, t, :], wait_acc(f"C.v.{t}"), VBC[:, 0, :], ALU.add), f"C.v.{t}")
            dve.wait_ge(kc_zero, 1)
            for name in ("C.q0.x", "C.k0.x", "C.z0.x"):
                low_c(name)

            def others_c(m):
                p, s = (m - B_END) // 4 + 1, (m - B_END) % 4
                if p < N_NA:
                    for name in fillers_c(p, s):
                        low_c(name)
                    if s == 1:
                        mask_bias(p)

            attend(B_END, C_END, others_c)

            step(dve.memset(U[:, :, :], 0.0))
            step(dve.tensor_scalar(HALF_B, col("bml", 0, 16), 0.5, None, ALU.mult))
            dve.sem_inc(vm_ready, 1)
            wait_read("D.gate.x")
            for dst, at in ((GI[0:4, 0], 0), (GI[0:4, 1], 32), (GF[0:4, 0], 64), (GF[0:4, 1], 96)):
                step(dve.tensor_copy(dst, GALL[at:at + 4]))
            signal(dve.scalar_tensor_tensor(GX[0:4], GF[0:4], -1.0, GF[0:4], ALU.mult, ALU.max), gates_abs, 1)
            dve.wait_ge(gates_log, 1)
            step(dve.scalar_tensor_tensor(GL[0:4], GF[0:4], 0.0, GL[0:4], ALU.min, ALU.subtract))
            one = ones[0:4, 0:1].to_broadcast([4, S])

            def along(ap, way):
                return ap[0:4, way, :] if way == 0 else ap[0:4, way, ::-1]

            for way in range(2):
                step(dve.tensor_tensor_scan(along(GX, way), one, along(GL, way), 0.0, ALU.mult, ALU.add))
            step(dve.tensor_tensor(ROWS[0:4, 0], GI[0:4], GX[0:4], ALU.subtract))
            for way in range(2):
                g = along(ROWS[:, 0], way)
                step(dve.tensor_tensor_scan(along(GF, way), g, g, 0.0, ALU.max, ALU.max))
            step(dve.tensor_scalar(ROWS[0:4, 1], GF[0:4], -1.0, None, ALU.mult))
            signal(dve.tensor_tensor(GX[0:4], GX[0:4], GF[0:4], ALU.add), gates_max, 1)
            for t in range(QT):
                name = f"D.v.{t}"
                read(dve.tensor_tensor(MV[:, t, :], wait_acc(name), VBC[:, 1, :], ALU.add), name)
            read(dve.tensor_copy(GCOL.rearrange("p a j h -> p (a j h)"), wait_acc("D.gcol")[:, 0:32]), "D.gcol")

            def convolve(h, what):
                i = "qk".index(what)
                wait_read(f"D.{what}{h}.x")
                if h >= 1:
                    dve.wait_ge(qk_lo, 2 * h + i - 1)
                tile = 4 * i + h
                step(dve.tensor_scalar(CV[:, i], U[:, i, 0:S], col("cw", 5 * tile), col("cb", tile), ALU.mult, ALU.add))
                for tap in range(1, 5):
                    ins = dve.scalar_tensor_tensor(CV[:, i], U[:, i, tap:tap + S], col("cw", 5 * tile + tap), CV[:, i],
                                                   ALU.mult, ALU.add)
                    step(ins) if tap < 4 else signal(ins, conv_done, 2 * h + i + 1)

            def doubled_silu(h, what):
                i = "qk".index(what)
                dve.wait_ge(tq_ready, 2 * h + i + 1)
                signal(dve.scalar_tensor_tensor(CV[:, i], TQ, 1.0, CV[:, i], ALU.add, ALU.mult), tq_used, 2 * h + i + 1)
                dst = (QM, KM)[i][:, h % 2, 0]
                dve.tensor_copy(dst, CV[:, i]).then_inc(qk_hi, 1)

            def diagonals(h):
                dve.wait_ge(rows_in[h % 2], 16 * (h // 2 + 1))
                if h >= 1:
                    dve.wait_ge(w_ready, 8 * h)
                for way in range(2):
                    dve.tensor_tensor(XD[:, way], RB[:, h % 2, 0, way].rearrange("p (j n) -> p j n", j=QT),
                                      DIAG[:, way].unsqueeze(1).to_broadcast([P, QT, P]), ALU.add).then_inc(xd_ready, 1)

            def weigh(h, way):
                if h >= 1:
                    b, i = tasks[f"D.den{h - 1}.{'fb'[way]}"]
                    dve.wait_ge(acc_ready[b], i)
                for i, j in enumerate(key_tiles(way)):
                    acc = wait_acc(f"D.s{h}.{j}")
                    n = 8 * h + 4 * way + i
                    dve.wait_ge(w_ready, n + 1)
                    t0, t1 = reach(way, j)
                    signal(dve.scalar_tensor_tensor(PM[:, way, j, t0:t1], acc[:, t0:t1], 0.25 * P ** -0.5,
                                                    W[:, n % 4, t0:t1], ALU.mult, ALU.mult), pm_ready, n + 1)
                    if way == 1:
                        dve.sem_inc(acc_read[j], 1)

            def divide(h, way):
                den, num = f"D.den{h}.{'fb'[way]}", f"D.num{h}.{'fb'[way]}"
                acc = wait_acc(den)
                step(dve.tensor_copy(T1, acc))
                read(dve.scalar_tensor_tensor(T1, acc, -1.0, T1, ALU.mult, ALU.max), den)
                step(dve.tensor_tensor(T1, T1, RB[:, h % 2, 1, way], ALU.max))
                step(dve.reciprocal(T1, T1))
                read(dve.tensor_tensor(T2 if way else HM, wait_acc(num), T1, ALU.mult), num)
                if way:
                    step(dve.tensor_tensor(HM, HM, T2, ALU.add))
                    signal(dve.scalar_tensor_tensor(HM, TO, 1.0, HM, ALU.add, ALU.mult), hm_ready, h + 1)

            def centre(h):
                name = f"D.mu{h}"
                read(dve.scalar_tensor_tensor(DV, wait_acc(name), -1.0 / P, HM, ALU.mult, ALU.add), name)
                dve.sem_inc(dv_ready, 1)

            def finish(h):
                rstd((f"D.var{h}",), RSM, T1, P, 4 * EPS)
                step(dve.tensor_tensor(DV, DV, RSM, ALU.mult))
                signal(dve.scalar_tensor_tensor(OG[:, 4 + h, :], DV, col("mw", h), ZM, ALU.mult, ALU.mult), ml_done, h + 1)

            convolve(0, "q")
            doubled_silu(0, "q")
            convolve(0, "k")
            doubled_silu(0, "k")
            for h in range(N_ML + 1):
                if h < N_ML:
                    diagonals(h)
                    weigh(h, 0)
                if h >= 1:
                    centre(h - 1)
                if h < N_ML:
                    weigh(h, 1)
                if h >= 1:
                    finish(h - 1)
                if h < N_ML:
                    wait_read(f"D.z{h}.x")
                    step(dve.scalar_tensor_tensor(ZM, ZTM, 1.0, ZM, ALU.add, ALU.mult))
                if h + 1 < N_ML:
                    convolve(h + 1, "q")
                if h < N_ML:
                    divide(h, 0)
                if h + 1 < N_ML:
                    doubled_silu(h + 1, "q")
                if h < N_ML:
                    wait_read(f"D.o{h}.x")
                    divide(h, 1)
                if h + 1 < N_ML:
                    convolve(h + 1, "k")
                    doubled_silu(h + 1, "k")
                if h == N_ML - 1:
                    for j in range(4):
                        out_low(2, j, OB, OG[:, j, :])
            for j in range(4, KD):
                out_low(2, j, OB, OG[:, j, :])
            for j in range(KD):
                residual(j, f"C.o{j}.x", XL, 0, 2)
                dve.sem_inc(x_new, 1)
            rstd(("E.stat",), RSTD[:, 0:S], XN[:, 0, 0:S], D)
            for j in range(KD):
                if j == 0:
                    dve.wait_ge(og_hi, 24)
                dve.scalar_tensor_tensor(OG[:, j, :], XL[:, j, :], col("fw", j), RSTD[:, 0:S], ALU.mult, ALU.mult).then_inc(y_ready, 1)

        @block.gpsimd
        def _(pool):
            fed = [0]

            def feed(upto):
                while fed[0] < min(upto, len(splits)):
                    name = splits[fed[0]]
                    c = chunk_at[name]
                    pool.wait_ge(hi_done, fed[0] + 1)
                    w = weight(name)
                    pool.tensor_tensor(w[:, 1, :], RAW[:, c % N_RAW, :], w[:, 0, :].bitcast(F32),
                                       ALU.subtract).then_inc(lo_done, 1)
                    fed[0] += 1

            def need(name, ahead=1):
                feed(split_at[name] + ahead)

            def wait_read(name):
                b, i = tasks[name]
                pool.wait_ge(acc_read[b], i)

            def h_low(base, src, h):
                for k in range(KD):
                    pool.wait_ge(hhi_done, base + k + 1)
                    pool.tensor_tensor(h[1][:, k, :], src(k), h[0][:, k, :].bitcast(F32), ALU.subtract).then_inc(hlo_done, 1)

            ropes = [0]

            def cosine(name, raw, dst):
                r = ropes[0]
                ropes[0] += 1
                wait_read(name)
                if r >= 1:
                    pool.wait_ge(rope_sum, r)
                pool.tensor_tensor(dst, raw, ROPE[:, 0, :], ALU.mult).then_inc(cos_done, 1)

            def low_q(p):
                if p >= 2:
                    pool.wait_ge(s_ready, pair_scored("A", p - 2))
                pool.wait_ge(q_hi, p + 1)
                pool.tensor_tensor(QA[:, 1, p % 2, :], QP, QA[:, 0, p % 2, :].bitcast(F32), ALU.subtract).then_inc(q_lo, 1)

            pool.memset(R2.bitcast(F32), 0.0).then_inc(kz_zero, 1)
            pool.wait_ge(sp_const, 16 * N_CONST)
            feed(1)
            h_low(0, lambda k: SQ[:, k % 2, :], HA)
            feed(2)
            cosine("A.k0.x", QRAW, COSP)
            feed(4)
            cosine("A.k1.x", QRAW, COSP)
            feed(5)
            cosine("A.q0.x", QRAW, COSP)
            feed(6)
            low_q(0)
            for p in range(1, N_PAIR):
                need(f"A.q{p}", 1)
                cosine(f"A.q{p}.x", QRAW, COSP)
                need(f"A.g{p}", 1)
                low_q(p)
            for j in range(KD):
                pool.wait_ge(og_hi, j + 1)
                pool.tensor_tensor(OA[1][:, j, 0:S], OG[:, j, :], OA[0][:, j, 0:S].bitcast(F32), ALU.subtract)
                pool.tensor_tensor(OA[1][:, j, S:T], OGC[:, j, :], OA[0][:, j, S:T].bitcast(F32),
                                   ALU.subtract).then_inc(og_lo, 1)
                if j == 2:
                    need("A.o0", 2)
            need("A.o7", 1)
            h_low(8, lambda k: SQ[:, k % 2, :], HA)
            need("B.g0", 1)
            pool.wait_ge(sp_rope, 32)
            cosine("B.kr.x", QRAWB, COSB)
            need("B.uqr", 1)
            for i in range(4):
                cosine(f"B.qr{i}.x", QRAWB, COSB)
                if i == 3:
                    need("B.uk", 1)
            need("B.o7", 1)
            pool.wait_ge(o_read, group_of[B_END - 1] + 1)
            pool.memset(R2[:, 2048:].bitcast(F32), 0.0).then_inc(kc_zero, 1)
            need("C.v0", 1)
            h_low(16, lambda k: SQ2[:, k % 2, 0, :], HC)

            def bias_low(p):
                pool.wait_ge(bias_hi, p + 1)
                pool.tensor_tensor(BIAS[p % 2][1], BRAW2, BIAS[p % 2][0].bitcast(F32), ALU.subtract).then_inc(bias_lo, 1)

            for p in range(N_NA):
                if p == 0:
                    bias_low(0)
                need(f"C.z{p}", 1)
                if p:
                    bias_low(p)

            def low_m(h, what):
                i = "qk".index(what)
                pool.wait_ge(qk_hi, 2 * h + i + 1)
                dst = (QM, KM)[i][:, h % 2]
                pool.tensor_tensor(dst[:, 1], CV[:, i], dst[:, 0].bitcast(F32), ALU.subtract).then_inc(qk_lo, 1)

            need("D.z0", 1)
            low_m(0, "q")
            need("D.q1", 1)
            low_m(0, "k")
            for h in range(N_ML):
                need(f"D.o{h}", 4)
                need(f"D.z{h}", 4)
                if h + 1 < N_ML:
                    need(f"D.q{h + 1}", 4)
                    low_m(h + 1, "q")
                    need(f"D.k{h + 1}", 4)
                    low_m(h + 1, "k")
            need("C.o7", 1)

        @block.sync
        def _(sp):
            sp.dma_start(CST[:, 0:256], cst[:, 0:256]).then_inc(sp_const, 16)
            sp.dma_start(PPT[:, 4 * T:4 * T + 384], cst[:, 256:640]).then_inc(sp_const, 16)
            sp.dma_start(ROPE, rope[0]).then_inc(sp_const, 16)
            sp.dma_start(COLS, cols).then_inc(sp_const, 16)
            sp.dma_start(XL, x_in).then_inc(sp_x, 16)
            sp.dma_start(XC, ctx_in).then_inc(sp_x, 16)

            def freed(c):
                name, split = chunks[c]
                if split:
                    sp.wait_ge(lo_done, split_at[name] + 1)
                else:
                    b, i = tasks[name[:name.rindex(".")]]
                    sp.wait_ge(acc_ready[b], i)

            def others(c):
                name = chunks[c][0]
                if name == "B.cq0":
                    sp.wait_ge(rope_sum, 10)
                    sp.dma_start(CST[:, 128:256], cst[:, 640:768]).then_inc(sp_rope, 16)
                    sp.dma_start(ROPE, rope[1]).then_inc(sp_rope, 16)

                if name == "B.o5":
                    sp.wait_ge(o_read, group_of[B_END - 1] + 1)
                    sp.dma_start(OGC_[:, 0:320], cst[:, 768:1088]).then_inc(sp_vb, 16)
                    sp.dma_start(VBC, vbias.to_broadcast([P, 2 * S]).rearrange("p (a n) -> p a n", a=2)).then_inc(sp_vb, 16)
                    load_bias(0)
                if name in ("C.k1", "C.k2", "C.k3"):
                    p = int(name[3:])
                    sp.wait_ge(bias_lo, p)
                    load_bias(p)

                if name == "D.o0":
                    sp.wait_ge(rows_ready, 1)
                    sp.dma_start(rows_dram.rearrange("a d h t -> h a d t"), ROWS[0:4]).then_inc(rows_stored, 16)
                    sp.wait_ge(rows_stored, 16)
                    load_rows(0)
                    load_rows(1)
                if name in ("D.k2", "D.k3"):
                    h = int(name[3:])
                    sp.wait_ge(hm_ready, h - 1)
                    load_rows(h)

            def load_rows(h):
                src = bass.AP(tensor=rows_dram.tensor, offset=8 * S + h * S, ap=[[0, P], [8 * S, 2], [4 * S, 2], [1, S]])
                sp.dma_start(RB[:, h % 2], src).then_inc(rows_in[h % 2], 16)

            def load_bias(p):
                for half in range(2):
                    for r in range(2):
                        src = rpb_band[2 * p + half, :, 1 - r:15 - r, :]
                        sp.dma_start(BRAW[64 * r:64 * r + 64, half], src).then_inc(bias_in, 16)

            for c, (name, _) in enumerate(chunks):
                others(c)
                if c >= N_RAW:
                    freed(c - N_RAW)
                sp.dma_start(RAW[:, c % N_RAW, :], wstream[c]).then_inc(raw_in[c % N_RAW], 16)
            for j in range(KD):
                sp.wait_ge(y_ready, j + 1)
                sp.dma_start(out[:, j, :], OG[:, j, :]).then_inc(s_out, 16)
            sp.wait_ge(s_out, 16 * KD)


def quarter_turn(head, quarter):
    m = np.zeros((P, P), np.float32)
    for i in range(P):
        part = (i % head) // quarter
        if part % 2 == 0:
            m[i + quarter, i] = -1.0
        else:
            m[i - quarter, i] = 1.0
    return m


def rope_table(head):
    n = np.arange(S)
    nf = head // 4
    inv = (np.float32(10000.0) ** (-np.arange(nf, dtype=np.float32) / np.float32(nf))).astype(np.float32)
    ar = (n // GRID).astype(np.float32)[:, None] * inv
    ac = (n % GRID).astype(np.float32)[:, None] * inv
    ang = np.concatenate([ar, ar, ac, ac], axis=-1).astype(np.float32)
    both = np.stack([np.cos(ang), np.sin(ang)]).astype(np.float32)
    return np.ascontiguousarray(np.tile(both.transpose(2, 0, 1), (P // head, 1, 1)))


def constants():
    i, j = np.arange(P)[:, None], np.arange(P)[None, :]
    off = np.float32(MASKED)
    left = np.where(j >= i, 0, off)
    right = np.where(j <= i, 0, off)
    col = np.arange(P)[:, None] % GRID
    start = np.clip(col - 8, 0, GRID - 16)
    k = np.arange(GRID)[None, :]
    window = np.where((k >= start) & (k < start + 16), 0, off)
    return np.concatenate([np.eye(P), quarter_turn(64, 16), left, np.zeros((P, P)), right, quarter_turn(32, 8),
                           left, right, window], axis=1).astype(np.float32)


def channel_columns(v, n):
    return np.reshape(v, (n, P)).T


def twice(v):
    return np.repeat(v, 2, axis=1)


PAIR_HEADS = [(8 * (p // 4) + p % 4, 8 * (p // 4) + 4 + p % 4) for p in range(N_PAIR)]


def by_pair(w):
    heads = [h for pair in PAIR_HEADS for h in pair]
    return np.reshape(np.reshape(w, (w.shape[0], 16, 64))[:, heads, :], (w.shape[0], 1024))


def stationary(w):
    return w.reshape(KD, P, P).transpose(1, 0, 2).reshape(P, CHUNK)


def weight_stream(i):
    a_in, b_in_w, c_in = i["a_w_in_0"], i["b_w_in_1"], np.reshape(i["w_in_2"], (D, -1))
    aq, ak, av, ag = by_pair(a_in[:, 0:1024]), a_in[:, 1024:1280], a_in[:, 1280:1536], by_pair(a_in[:, 1536:2560])
    a_o = by_pair(np.ascontiguousarray(i["a_w_o_0"].T)).T
    kr = np.tile(b_in_w[:, 384:416], (1, 4))
    uq = i["b_w_uq_1"].reshape(256, 16, 96)
    ukv = i["b_w_ukv_1"].reshape(128, 16, 128)
    qn = np.ascontiguousarray(uq[:, :, 0:64]).reshape(2, P, 8, P)
    qr = np.ascontiguousarray(uq[:, :, 64:96]).reshape(2, P, 4, P)
    gate = np.zeros((D, P), np.float32)
    for at, src in ((0, 4608), (32, 4616), (64, 4612), (96, 4620)):
        gate[:, at:at + 4] = c_in[:, src:src + 4]
    ada = {0: i["ada_w_0"], 1: i["ada_w_1"], 2: np.reshape(i["w_ada_2"], (D, 3 * D))}
    main = {"A.q": aq, "A.g": ag, "A.k": ak, "A.o": a_o, "B.g": b_in_w[:, 416:], "B.cq": b_in_w[:, 0:256],
            "B.o": i["b_w_o_1"], "C.q": c_in[:, 0:512], "C.k": c_in[:, 512:1024], "C.z": c_in[:, 1536:2048],
            "D.q": c_in[:, 2048:2560], "D.k": c_in[:, 2560:3072], "D.o": c_in[:, 3584:4096],
            "D.z": c_in[:, 4096:4608], "C.o": np.reshape(i["w_out_2"], (D, D))}
    out = []
    for name, _ in chunk_plan():
        if name.startswith("ada"):
            layer, b, q = name[3:].split(".")
            w = ada[int(layer)].reshape(4, 2, P, 6, 512)[int(q), :, :, int(b), :]
            out.append(w.transpose(1, 0, 2).reshape(P, CHUNK))
        elif name.startswith("A.v"):
            h = int(name[3:])
            out.append(av.reshape(2, 4, P, 256)[h].transpose(1, 0, 2).reshape(P, CHUNK))
        elif name.startswith(("C.v", "D.v")):
            v = c_in[:, 1024:1536] if name[0] == "C" else c_in[:, 3072:3584]
            out.append(v.reshape(4, 2, P, 512)[int(name[3:])].transpose(1, 0, 2).reshape(P, CHUNK))
        elif name == "B.ckv":
            out.append(stationary(b_in_w[:, 256:384]))
        elif name == "B.kr":
            out.append(stationary(kr))
        elif name == "B.uv":
            out.append(np.ascontiguousarray(ukv[:, :, 64:128]).reshape(P, CHUNK))
        elif name == "B.uk":
            out.append(np.ascontiguousarray(ukv[:, :, 0:64]).reshape(P, CHUNK))
        elif name == "B.uqr":
            out.append(qr.transpose(1, 2, 0, 3).reshape(P, CHUNK))
        elif name.startswith("B.uq"):
            p = 4 * int(name[4:])
            out.append(qn[:, :, p:p + 4, :].transpose(1, 2, 0, 3).reshape(P, CHUNK))
        elif name == "D.gate":
            out.append(stationary(gate))
        else:
            key = name.rstrip("0123456789")
            j = int(name[len(key):])
            out.append(stationary(main[key][:, j * P:j * P + P]))
    return np.stack(out)


def column_vectors(i):
    b_in = np.reshape(i["b_in_2"], (-1,))
    gate = np.zeros((P, 1), np.float32)
    for at, src in ((0, 4608), (32, 4616), (64, 4612), (96, 4620)):
        gate[at:at + 4, 0] = b_in[src:src + 4]
    c = np.stack([channel_columns(i["c"], 8), channel_columns(i["c_ctx"], 8)], axis=2).reshape(P, 16)
    sinks = np.reshape(i["a_sinks_0"], (16,))[[h for pair in PAIR_HEADS for h in pair]]
    cw = np.reshape(i["conv_w_2"], (5, 8, P)).transpose(2, 1, 0).reshape(P, 40)
    parts = {
        "c": c, "c2": twice(channel_columns(i["c_2"], 8)),
        "ab0": twice(channel_columns(i["ada_b_0"], 24)), "ab1": twice(channel_columns(i["ada_b_1"], 24)),
        "ab2": twice(channel_columns(i["b_ada_2"], 24)), "ng0": twice(channel_columns(i["norm_g_0"], 8)),
        "ng1": twice(channel_columns(i["norm_g_1"], 8)), "ng2": twice(channel_columns(i["norm_w_2"], 8)),
        "fg": channel_columns(i["final_g"], 8), "fw": channel_columns(i["final_norm_w_2"], 8),
        "qg": channel_columns(i["b_q_norm_1"], 2), "kg": channel_columns(i["b_kv_norm_1"], 1),
        "bna": np.concatenate([channel_columns(b_in[0:1024], 8), channel_columns(b_in[1536:2048], 4)], axis=1),
        "bml": np.concatenate([channel_columns(b_in[2048:3072], 8), channel_columns(b_in[3584:4608], 8)], axis=1),
        "cw": cw, "cb": channel_columns(i["conv_b_2"], 8), "mw": channel_columns(i["ml_norm_w_2"], 4), "bg": gate,
        "sink": np.broadcast_to(sinks, (P, 16)),
    }
    at, n = column_layout()
    return np.ascontiguousarray(np.concatenate([parts[name] for name in at], axis=1))


def host_arrays(i):
    b_in = np.reshape(i["b_in_2"], (-1,))
    column = np.arange(GRID)
    dx = np.clip(column[None, :] - column[:, None], -15, 15) + 15
    rpb_band = np.ascontiguousarray(np.reshape(i["rpb_2"], (8, 15, 31))[:, :, dx].transpose(0, 2, 1, 3))
    return {
        "wstream": weight_stream(i), "cst": constants(), "rope": np.stack([rope_table(64), rope_table(32)]),
        "cols": column_vectors(i),
        "x_in": np.ascontiguousarray(np.reshape(i["x"], (S, KD, P)).transpose(2, 1, 0)),
        "ctx_in": np.ascontiguousarray(np.reshape(i["ctx"], (C, KD, P)).transpose(2, 1, 0)),
        "vbias": np.concatenate([b_in[1024:1536], b_in[3072:3584]]).reshape(1, 1024), "rpb_band": rpb_band,
    }


def kernel(**inputs):
    import concourse.bacc as bacc
    from concourse.bass_utils import run_bass_kernel_spmd

    arrays = host_arrays({k: np.asarray(v) for k, v in inputs.items()})
    nc = bacc.Bacc("TRN2", target_bir_lowering=False, num_devices=1, dynamic_dma_scratch_size=1024)
    args = {n: nc.dram_tensor(n, a.shape, F32, kind="ExternalInput").ap() for n, a in arrays.items()}
    rows_dram = nc.dram_tensor("rows", (3, 2, 4, S), F32, kind="Internal").ap()
    out = nc.dram_tensor("out", (P, KD, S), F32, kind="ExternalOutput").ap()
    build(nc, rows_dram=rows_dram, out=out, **args)
    result = run_bass_kernel_spmd(nc, [arrays], core_ids=[0]).results[0]["out"]
    return np.ascontiguousarray(np.reshape(result, (P, KD, S)).transpose(2, 1, 0)).reshape(1, S, D)
```

```python
from contextlib import ExitStack

import numpy as np
import concourse.bass as bass
from concourse import mybir

P = 128
D = 1024
KD = D // P
S = 512
C = 256
T = S + C
QT = S // P
GRID = 64
EPS = 1e-6
MASKED = -1e30
N_PAIR = 8
N_NA = 4
N_ML = 4
N_RAW = 5
N_CONST = 4
N_SPLIT = 3
CHUNK = 1024
SCALE_A = 64 ** -0.5
SCALE_B = 96 ** -0.5

F32 = mybir.dt.float32
F32R = mybir.dt.float32r
ALU = mybir.AluOpType
ACT = mybir.ActivationFunctionType
AX = mybir.AxisListType.X


def column_layout():
    at, n = {}, 0
    for name, width in (("c", 16), ("c2", 16), ("ab0", 48), ("ab1", 48), ("ab2", 48), ("ng0", 16), ("ng1", 16),
                        ("ng2", 16), ("fg", 8), ("fw", 8), ("qg", 2), ("kg", 1), ("bna", 12), ("bml", 16),
                        ("cw", 40), ("cb", 8), ("mw", 4), ("bg", 1), ("sink", 16)):
        at[name] = n
        n += width
    return at, n


def chunk_plan():
    plan = []

    def ada(layer, b):
        plan.extend((f"ada{layer}.{b}.{q}", False) for q in range(4))

    def split(*names):
        plan.extend((n, True) for n in names)

    for b in range(6):
        ada(0, b)
    split("A.k0", "A.k1", "A.v0", "A.v1", "A.q0", "A.g0")
    for p in range(1, N_PAIR):
        split(f"A.q{p}", f"A.g{p}")
        if p <= 6:
            ada(1, p - 1)
    for b in range(3):
        ada(2, b)
    split(*[f"A.o{j}" for j in range(KD)])
    split("B.cq0", "B.cq1", "B.ckv", "B.kr", *[f"B.g{j}" for j in range(KD)])
    split("B.uv", "B.uqr", "B.uq0", "B.uq1", "B.uk")
    for b in range(3, 6):
        ada(2, b)
    split(*[f"B.o{j}" for j in range(KD)])
    split("C.v0", "C.v1", "C.v2", "C.v3")
    for p in range(N_NA):
        split(f"C.q{p}", f"C.k{p}", f"C.z{p}")
    split("D.gate", "D.v0", "D.v1", "D.v2", "D.v3")
    for h in range(N_ML):
        split(f"D.q{h}", f"D.k{h}", f"D.o{h}", f"D.z{h}")
    split(*[f"C.o{j}" for j in range(KD)])
    return plan


def task_plan():
    count, tasks, last_use, ring = {}, {}, {}, [0]

    def task(name, bank, *chunks):
        count[bank] = count.get(bank, 0) + 1
        tasks[name] = (bank, count[bank])
        for c in chunks:
            last_use[c] = name

    def spread(name, *chunks, banks=(0, 1, 2, 3, 7)):
        task(name, banks[ring[0] % len(banks)], *chunks)
        ring[0] += 1

    def ada(layer, b, put):
        put(f"ada{layer}.{b}", *[f"ada{layer}.{b}.{q}" for q in range(4)])

    alone = lambda name, *chunks: task(name, 7, *chunks)
    for part in ("x", "c"):
        task(f"A.stat.{part}", {"x": 4, "c": 5}[part])
    for b in range(6):
        ada(0, b, spread)
        if b >= 1:
            spread(f"ada0.{b - 1}.t")
    spread("ada0.5.t")
    for j in range(2):
        spread(f"A.k{j}.x", f"A.k{j}")
        spread(f"A.k{j}.c", f"A.k{j}")
    for j in range(2):
        spread(f"A.k{j}.rot")
    for t in range(T // P):
        spread(f"A.v.{t}", "A.v0", "A.v1")
    spread("A.q0.x", "A.q0")
    spread("A.q0.rot")
    spread("A.qg0.c", "A.q0", "A.g0")
    spread("A.g0.x", "A.g0")
    for p in range(1, N_PAIR + 1):
        for step in range(6):
            for name in fillers_a(p, step):
                alone(name, *filler_chunks(name))
    for j in range(KD):
        spread(f"A.o{j}.x", f"A.o{j}")
        spread(f"A.o{j}.c", f"A.o{j}")
        if j == 0:
            task("B.stat.x", 4)
            task("B.stat.c", 5)
    for name in ("B.cq0.x", "B.cq1.x", "B.ckv.x", "B.ckv.c", "B.kr.x", "B.kr.c"):
        spread(name, name[:-2])
    for j in range(KD):
        spread(f"B.g{j}.x", f"B.g{j}")
        if j == 1:
            spread("B.kr.rot")
            task("B.cq.stat", 4)
            task("B.ckv.stat.x", 5)
            task("B.ckv.stat.c", 4)
    for i in range(4):
        spread(f"B.qr{i}.x", "B.uqr")
        for t, h in value_parts(i):
            spread(f"B.v.{t}.{h}", "B.uv")
        spread(f"B.qr{i}.rot")
    for step in range(3):
        spread(*fillers_b(0, step))
    for p in range(1, N_PAIR):
        for step in range(4):
            for name in fillers_b(p, step):
                alone(name, *filler_chunks(name))
    for j in range(KD):
        spread(f"B.o{j}.x", f"B.o{j}")
        if j == 0:
            task("C.stat.1", 4)
            task("C.stat.2", 5)
    for t in range(QT):
        spread(f"C.v.{t}", "C.v0", "C.v1", "C.v2", "C.v3")
    for name in ("C.q0.x", "C.k0.x", "C.z0.x"):
        spread(name, name[:-2])
    for p in range(1, N_NA):
        for step in range(4):
            for name in fillers_c(p, step):
                alone(name, *filler_chunks(name))
    spread("D.gate.x", "D.gate")
    for t in range(QT):
        spread(f"D.v.{t}", "D.v0", "D.v1", "D.v2", "D.v3")
    order_d(lambda name, bank, *chunks: task(name, bank, *chunks))
    for j in range(KD):
        task(f"C.o{j}.x", (0, 1, 2, 3)[j % 4], f"C.o{j}")
    task("E.stat", 4)
    return tasks, last_use


def fillers_a(p, step):
    if p == N_PAIR:
        return [f"ada2.{step // 2}" + ".t" * (step % 2)]
    out = [f"A.q{p}.x", f"A.q{p}.rot", f"A.qg{p}.c", f"A.g{p}.x"] + [f"ada1.{p - 1}", f"ada1.{p - 1}.t"] * (p <= 6)
    return out[step:step + 1]


def value_parts(i):
    return [(t, h) for t in range(T // P) for h in range(2)][3 * i:3 * i + 3]


def fillers_b(p, step):
    if step == 3 and 1 <= p <= 6:
        return [f"ada2.{3 + (p - 1) // 2}" + ".t" * ((p - 1) % 2)]
    return [f"B.qn{p}.x", f"B.kn{p}.x", f"B.kn{p}.c"][step:step + 1]


def fillers_c(p, step):
    return [f"C.q{p}.x", f"C.k{p}.x", f"C.z{p}.x"][step:step + 1]


def filler_chunks(name):
    if name.startswith("ada"):
        return [f"{name}.{q}" for q in range(4)] if name.count(".") == 1 else []
    if name.endswith(".rot") or name.startswith(("B.qn", "B.kn")):
        return []
    if name.startswith("A.qg"):
        return [f"A.q{name[4:-2]}", f"A.g{name[4:-2]}"]
    return [name[:-2]]


def order_d(task):
    def project(h, what, bank):
        task(f"D.{what}{h}.x", bank, f"D.{what}{h}")

    task("D.gcol", 6)
    project(0, "q", 5)
    project(0, "k", 5)
    for h in range(N_ML + 1):
        if h < N_ML:
            project(h, "o", 4)
            project(h, "z", 5)
            for j in range(QT):
                task(f"D.s{h}.{j}", j)
        if h >= 1:
            task(f"D.mu{h - 1}", 4)
        if h + 1 < N_ML:
            project(h + 1, "q", 5)
        if h >= 1:
            task(f"D.var{h - 1}", 4)
        if h < N_ML:
            for way, num, den in (("f", 6, 7), ("b", 3, 2)):
                task(f"D.num{h}.{way}", num)
                task(f"D.den{h}.{way}", den)
                if way == "f" and h + 1 < N_ML:
                    project(h + 1, "k", 5)


def build(nc, wstream, cst, rope, cols, x_in, ctx_in, vbias, rpb_band, rows_dram, out):
    AT, _ = column_layout()
    chunks = chunk_plan()
    chunk_at = {name: c for c, (name, _) in enumerate(chunks)}
    splits = [name for name, split in chunks if split]
    split_at = {name: g for g, name in enumerate(splits)}
    RESIDENT = ["B.uq0", "B.uq1", "B.uk"]
    in_ring = [name for name in splits if name not in RESIDENT]
    tasks, last_use = task_plan()

    es = ExitStack()
    with es:
        def sb(name, shape, dt):
            return es.enter_context(nc.sbuf_tensor(name, shape, dt))

        def sem(name):
            return es.enter_context(nc.semaphore(name))

        NR = 12288 + 6144 + 3840 + 512 + N_SPLIT * 2048
        AR_BASE = -(-nc.sbuf_base // 32) * 32
        AR = sb("AR", [P, NR], F32R)
        NF = 28120
        AF = sb("AF", [P, NF], F32)
        place = {"F": 0, "R": 0}

        def region(kind, n):
            at = place[kind]
            place[kind] += n
            assert place[kind] <= (NF if kind == "F" else NR), (kind, place)
            return (AF if kind == "F" else AR)[:, at:at + n]

        def tiles(ap, *dims):
            n = int(np.prod(dims))
            ap = ap[:, 0:n]
            if len(dims) == 1:
                return ap
            names = "abcd"[:len(dims)]
            return ap.rearrange(f"p ({' '.join(names)}) -> p {' '.join(names)}",
                                **{k: d for k, d in zip(names, dims)})

        R1, R3, R2 = region("R", 12288), region("R", 3840), region("R", 6144)
        RC, RW = region("R", 512), region("R", N_SPLIT * 2048)
        identR, mask3R = RC[:, 0:128], RC[:, 128:512]
        WS = tiles(RW, N_SPLIT, 2, CHUNK)

        XL = tiles(region("F", KD * S), KD, S)
        OG = tiles(region("F", KD * S), KD, S)
        OGC_ = region("F", KD * C)
        LOC_ = region("F", KD * C + 4096)
        XC = tiles(LOC_, KD, C)
        RAW = tiles(region("F", N_RAW * CHUNK), N_RAW, CHUNK)
        PPT = region("F", 6 * T)
        PROB = tiles(PPT, 2, T)
        PT = tiles(PPT[:, 2 * T:], 2, 2, T)
        CST = region("F", 384)
        ident, perm, ones = CST[:, 0:128], CST[:, 128:256], CST[:, 256:384]
        ROPE = tiles(region("F", 2 * S), 2, S)
        COLS = region("F", column_layout()[1])
        MOD = tiles(region("F", 3 * 48), 3, 24, 2)
        GAIN = tiles(region("F", 3 * 16), 3, KD, 2)
        SILC = tiles(region("F", 32), 2, KD, 2)
        NSINK = region("F", 16)
        SILT = LOC_[:, 5888:5920]
        STAT = tiles(region("F", 20), 5, 4)

        PS = es.enter_context(nc.psum_tensor("PS", [P, 8, 512], F32))
        bank = [PS[:, b, :] for b in range(8)]
        SC = [PS[:, 0:2, :].rearrange("p b n -> p (b n)"), PS[:, 2:4, :].rearrange("p b n -> p (b n)")]
        PTP = PS[:, 4:6, :].rearrange("p b n -> p (b n)")

        def col(name, i=0, n=1):
            return COLS[:, AT[name] + i:AT[name] + i + n]

        HA = [tiles(R1, KD, T), tiles(R1[:, KD * T:], KD, T)]
        KZ = tiles(R2, 2, 2, 2, T)
        QA = tiles(R3, 2, 2, T)
        VA = tiles(LOC_[:, 2048:], T // P, 256)
        QRAW, COSP, QP = LOC_[:, 3584:4096], LOC_[:, 4096:4608], LOC_[:, 4608:5376]
        SQ = tiles(PPT, 2, T)
        RSTD = PPT[:, 2 * T:3 * T]
        XN = tiles(PPT[:, 3 * T:], 2, T)
        OGC = tiles(OGC_, KD, C)
        OA = HA
        KB = tiles(R1, 2, 2, 2, T)
        QB = tiles(R1[:, 6144:], 2, 2, 2, S)
        UB = tiles(R2, 3, 2, CHUNK)
        CQN = tiles(R3, 2, 2, S)
        CKN = tiles(R3[:, 2048:], 2, T)
        VB = tiles(LOC_, T // P, D)
        QR = tiles(OGC_, 4, S)
        QRH = tiles(R1[:, 10240:], 4, S)
        CQR, SQCQ, RSQ = tiles(PPT, 2, S), tiles(PPT[:, 1024:], 2, S), PPT[:, 2048:2560]
        QRAWB, COSB, KRF = PPT[:, 2560:3072], PPT[:, 3072:3584], PPT[:, 3584:4352]
        CKR, SQCK, RSK = LOC_[:, 0:768], LOC_[:, 768:1536], LOC_[:, 1536:2304]
        OB = [tiles(R1, KD, S), tiles(R1[:, KD * S:], KD, S)]
        def ada_buffer(layer, b):
            return ROPE[:, 0, :] if layer == 2 and b >= 3 else LOC_[:, 5376:5888]

        SQ2 = tiles(PPT, 2, 2, S)
        SQSUM = PPT[:, 3072:4096]
        RSTD2 = tiles(PPT[:, 2048:], 2, S)
        XNC = tiles(PPT[:, 3072:], 2, S)
        HC = OB
        KC = tiles(R2[:, 2048:], 2, 2, 2, S)
        QC = tiles(R3, 2, 2, S)
        BIAS = [[tiles(R1[:, 8192:], 2, 896), tiles(R1[:, 9984:], 2, 896)],
                [tiles(R2, 2, 896), tiles(R3[:, 2048:], 2, 896)]]
        VC = tiles(LOC_, QT, S)
        BRAW = tiles(LOC_[:, 2048:], 2, 14, GRID)
        ZB, ZT = LOC_[:, 3840:4352], LOC_[:, 4352:4864]
        DIAG = tiles(OGC_, 2, P)
        CMASK = OGC_[:, 256:320]
        BRAW2 = tiles(LOC_[:, 2048:], 2, 896)
        VBC = tiles(OGC_[:, 320:], 2, S)
        QM, KM = tiles(R2[:, 2048:], 2, 2, S), tiles(R2[:, 4096:], 2, 2, S)
        AD = nc.alloc_sbuf_tensor_at("AD", [P, 4096 + 3840 + 2048], F32, offset=AR_BASE + 4 * 8192)
        RB = tiles(AD[:, 0:4096], 2, 2, 2, S)
        R3F = AD[:, 4096:7936]
        U, CV = tiles(R3F, 2, S + 4), tiles(R3F[:, 1032:], 2, S)
        TQ, XD = R3F[:, 2056:2568], tiles(R3F[:, 2568:], 2, QT, P)
        W = tiles(AD[:, 7936:], 4, S)
        PM = tiles(LOC_[:, 2048:], 2, QT, S)
        ROWS = tiles(LOC_[:, 2048:], 3, 2, S)
        MV = tiles(LOC_, QT, S)
        PPW = tiles(PPT, 9, S)
        GALL, GI, GF = PPW[:, 0], PPW[:, 1:3], PPW[:, 3:5]
        GX, GL = PPW[:, 5:7], PPW[:, 7:9]
        TO, ZTM, TO2, T1, T2, HM, DV, SQD, RSM = (PPW[:, i] for i in range(9))
        HALF_B = OGC_[:, 1344:1360]
        GCOL = tiles(OGC_[:, 1360:], 2, QT, N_ML)

        sp_x2, ada_used = sem("x_in2"), sem("modulation_chunk_used")
        sp_const, sp_x, sp_rope, sp_vb = (sem(n) for n in ("const_in", "x_in", "rope_in", "vbias_in"))
        raw_in = [sem(f"raw_in{i}") for i in range(N_RAW)]
        hi_done, lo_done, v_used = sem("weights_high"), sem("weights_low"), sem("v_chunk_used")
        acc_ready = [sem(f"acc_ready{b}") for b in range(8)]
        acc_read = [sem(f"acc_read{b}") for b in range(8)]
        dve_step, act_step = sem("dve_step"), sem("act_step")
        s_ready, nm_ready, exp_done, p_ready = (sem(n) for n in ("scores_ready", "negmax_ready", "exp_done", "probs_ready"))
        pt_ready, pt_read, pv_done, o_read = (sem(n) for n in ("probs_turned", "turned_read", "pv_done", "o_read"))
        cos_done, rope_sum = sem("cos_done"), sem("rope_sum")
        kz_done, q_hi, q_lo = sem("keys_split", ), sem("q_high"), sem("q_low")
        sq_done, sq_read = sem("squares_done"), sem("squares_read")
        sq_added = sem("squares_added")
        root_done = sem("root_done")
        xn_done, hf_done, hhi_done, hlo_done = (sem(n) for n in ("normed", "modulated", "h_high", "h_low"))
        og_hi, og_lo = sem("out_high"), sem("out_low")
        x_new = sem("x_new")
        s_out = sem("out_stored")
        kz_zero, kc_zero = sem("keys_zeroed_a"), sem("keys_zeroed_c")
        tanh_done, b_hi = sem("tanh_done"), sem("pair_high_b")
        mod_done, silt_done, silc_done = sem("modulation_done"), sem("tanh_c"), sem("silu_c")
        consts_ready = sem("consts_ready")
        lat_sq, cqn_ready, ckn_ready, b_ready, c_ready = (sem(n) for n in (
            "latent_squares", "cq_normed", "ckv_normed", "pair_ready_b", "pair_ready_c"))
        bias_raw, bias_hi, bias_lo, bias_in = (sem(n) for n in ("bias_masked", "bias_high", "bias_low", "bias_in"))
        c_hi, zg_done, ms2_done = (sem(n) for n in ("pair_high_c", "gate_c", "mean_square2"))

        vm_ready, gates_abs, gates_log, gates_max, rows_ready = (sem(n) for n in (
            "mlstm_begin", "gates_abs", "gates_log", "gates_max", "rows_ready"))
        rows_stored, rows_in = sem("rows_stored"), [sem("rows_in0"), sem("rows_in1")]
        conv_done, tq_ready, tq_used, qk_hi, qk_lo = (sem(n) for n in (
            "conv_done", "tanh_conv", "tanh_conv_used", "qk_high", "qk_low"))
        xd_ready, w_ready, pm_ready = sem("diagonals"), sem("decay_weights"), sem("weighted_scores")
        o_gate, z_gate, hm_ready, dv_ready, sqd_ready, root_m, ml_done = (sem(n) for n in (
            "o_gate", "z_gate", "hm_ready", "centred", "centred_squares", "root_m", "head_done"))
        rs_ready, y_ready, y_ready2, tap_done, xw_done = (sem(n) for n in ("rstd_ready", "y_ready", "y_ready2", "first_tap", "weighted_x"))

        block = es.enter_context(nc.Block())

        units, groups = [], []

        def unit(**u):
            u["n"] = len(units)
            units.append(u)

        for p in range(N_PAIR):
            tile = p // 4
            for part, n_q in (("x", QT), ("c", C // P)):
                for t in range(n_q):
                    q0 = t * P if part == "x" else S + t * P
                    for half in range(2):
                        near = [b for b in (t - 1, t, t + 1) if 0 <= b < QT] if part == "x" else []
                        segments = []
                        if near:
                            c0 = 512 - P * len(near)
                            m0 = 0 if t > 0 else P
                            k0 = near[0] * P
                            segments.append((c0, P * len(near), [(identR, mask3R[:, m0:m0 + P * len(near)])] + [
                                (QA[:, a, p % 2, q0:q0 + P], KZ[:, b, tile, half, k0:k0 + P * len(near)])
                                for a, b in ((0, 0), (0, 1), (1, 0))]))
                        segments.append((512, C, [
                            (QA[:, a, p % 2, q0:q0 + P], KZ[:, b, tile, half, S:T])
                            for a, b in ((0, 0), (0, 1), (1, 0))]))
                        g0 = 64 * (2 * tile + half)
                        unit(c0=segments[0][0], c1=512 + C, segments=segments, scale=SCALE_A,
                             sink=col("sink", 2 * p + half), half=half,
                             values=[VA[:, b, g0:g0 + 64] for b in near + [4, 5]],
                             o0=t * P, first=t == 0, layer="A", pair=p, pair_first=part == "x" and t == 0,
                             out=(OG if part == "x" else OGC)[:, p, :] if t == n_q - 1 else None, width=P * n_q)
        A_END = len(units) // 2
        for p in range(N_PAIR):
            for t in range(QT):
                for half in range(2):
                    pairs = ((0, 0), (0, 1), (1, 0))
                    q = [QB[0:96, a, p % 2, half, t * P:t * P + P] for a in range(2)]
                    k = [KB[0:96, b, p % 2, half, :] for b in range(2)]
                    unit(c0=256, c1=1024, segments=[
                        (256, C, [(q[a], k[b][:, S:T]) for a, b in pairs]),
                        (512, S, [(q[a], k[b][:, 0:S]) for a, b in pairs])],
                         scale=SCALE_B, sink=None, half=half,
                         values=[VB[:, b, 64 * (2 * p + half):64 * (2 * p + half) + 64] for b in (4, 5, 0, 1, 2, 3)],
                         o0=t * P, first=t == 0, layer="B", pair=p, pair_first=t == 0,
                         out=OG[:, p, :] if t == QT - 1 else None, width=S)
        B_END = len(units) // 2
        for p in range(N_NA):
            for t in range(QT):
                for half in range(2):
                    q = [QC[:, a, p % 2, t * P:t * P + P] for a in range(2)]
                    d0 = (6 - 2 * t) * GRID
                    unit(c0=0, c1=S, segments=[
                        (0, S, [(identR, BIAS[p % 2][a][:, half, d0:d0 + S]) for a in range(2)]
                         + [(q[a], KC[:, b, p % 2, half, :]) for a, b in ((0, 0), (0, 1), (1, 0))])],
                         scale=SCALE_A, sink=None, half=half,
                         values=[VC[:, b, 64 * (2 * p + half):64 * (2 * p + half) + 64] for b in range(QT)],
                         o0=t * P, first=t == 0, layer="C", pair=p, pair_first=t == 0,
                         out=OG[:, p, :] if t == QT - 1 else None, width=S)
        C_END = len(units) // 2
        group_of, g = {}, 0
        for m in range(C_END):
            group_of[m] = g
            g += units[2 * m]["out"] is not None
        per_pair = {"A": 6, "B": 4, "C": 4}
        start_of = {"A": 0, "B": A_END, "C": B_END}

        def pair_scored(layer, p):
            return 2 * (start_of[layer] + per_pair[layer] * (p + 1))

        def weight(name):
            return UB[:, RESIDENT.index(name)] if name in RESIDENT else WS[:, in_ring.index(name) % N_SPLIT]

        def reach(way, j):
            return (j * P, S) if way == 0 else (0, (j + 1) * P)

        def key_tiles(way):
            return range(QT) if way == 0 else range(QT - 1, -1, -1)

        ada_order = [name[:-2] for name, _ in chunks if name.startswith("ada") and name.endswith(".0") and name.count(".") == 2]
        V_FREED = ["C.v0", "C.v1", "C.v2", "D.v0", "D.v1", "D.v2"]

        @block.tensor
        def _(pe):
            opened = []

            def acc_open(name):
                b, i = tasks[name]
                opened.append(name)
                if i > 1:
                    pe.wait_ge(acc_read[b], i - 1)
                return bank[b]

            def acc_close(mm, name):
                mm.then_inc(acc_ready[tasks[name][0]], 1)

            def chunk_ready(name):
                pe.wait_ge(lo_done, split_at[name] + 1)

            def sum_of(out, products):
                for i, (stationary, moving) in enumerate(products):
                    mm = pe.matmul(out, stationary, moving, start=i == 0, stop=i == len(products) - 1)
                return mm

            def three(w, x):
                return [(w[0], x[0]), (w[0], x[1]), (w[1], x[0])]

            def project(name, chunk, src, t0, t1, nk=KD, at=0, ready=None):
                out = acc_open(name)
                chunk_ready(chunk)
                w = weight(chunk)
                for k in range(nk):
                    if ready:
                        ready(k)
                    for i, (a, b) in enumerate(three((w[:, 0, at + k * P:at + k * P + P], w[:, 1, at + k * P:at + k * P + P]),
                                                     (src[0][:, k, t0:t1], src[1][:, k, t0:t1]))):
                        mm = pe.matmul(out[:, 0:t1 - t0], a, b, start=k == 0 and i == 0, stop=k == nk - 1 and i == 2)
                acc_close(mm, name)

            def project_together(jobs, ready, k0=0, k1=KD):
                outs = [acc_open(name) if k0 == 0 else bank[tasks[name][0]] for name, *_ in jobs]
                for k in range(k0, k1):
                    ready(k)
                    for out, (name, chunk, src, t0, t1) in zip(outs, jobs):
                        if k == 0:
                            chunk_ready(chunk)
                        w = weight(chunk)
                        mm = None
                        for i, (a, b) in enumerate(three((w[:, 0, k * P:k * P + P], w[:, 1, k * P:k * P + P]),
                                                         (src[0][:, k, t0:t1], src[1][:, k, t0:t1]))):
                            mm = pe.matmul(out[:, 0:t1 - t0], a, b, start=k == 0 and i == 0, stop=k == KD - 1 and i == 2)
                        if k == KD - 1:
                            acc_close(mm, name)

            def rotate(name, raw_name, raw):
                out = acc_open(name)
                b, i = tasks[raw_name]
                pe.wait_ge(acc_read[b], i)
                acc_close(pe.matmul(out, perm, raw, start=True, stop=True), name)

            def ada_rows(layer, b):
                name = f"ada{layer}.{b}"
                out = acc_open(name)
                pe.wait_ge(silc_done, 1)
                for k in range(KD):
                    c = chunk_at[f"{name}.{k // 2}"]
                    if k % 2 == 0:
                        pe.wait_ge(raw_in[c % N_RAW], 16 * (c // N_RAW + 1))
                    g = k % 4
                    mm = pe.matmul(out[32 * g:32 * g + 2, :], SILC[:, layer // 2, k, :],
                                   RAW[:, c % N_RAW, (k % 2) * 512:(k % 2) * 512 + 512], start=k < 4, stop=k >= 4)
                    if k % 2 and k < KD - 1:
                        mm.then_inc(ada_used, 1)
                acc_close(mm, name)

            def ada_columns(layer, b):
                name = f"ada{layer}.{b}.t"
                out = acc_open(name)
                rows, i = tasks[f"ada{layer}.{b}"]
                pe.wait_ge(acc_read[rows], i)
                for i in range(4):
                    mm = pe.transpose(out[:, i * P:i * P + P], ada_buffer(layer, b)[:, i * P:i * P + P], ident)
                acc_close(mm, name)

            def make(name):
                what, part = name.split(".")[1], name.split(".")[-1]
                if name.startswith("ada"):
                    layer, b = int(name[3]), int(what)
                    ada_columns(layer, b) if part == "t" else ada_rows(layer, b)
                elif name.startswith("A."):
                    if what[0:2] == "qg":
                        out = acc_open(name)
                        for at, chunk in ((0, f"A.q{what[2:]}"), (C, f"A.g{what[2:]}")):
                            chunk_ready(chunk)
                            w = weight(chunk)
                            mm = sum_of(out[:, at:at + C], [
                                ab for k in range(KD) for ab in three((w[:, 0, k * P:k * P + P], w[:, 1, k * P:k * P + P]),
                                                                      (HA[0][:, k, S:T], HA[1][:, k, S:T]))])
                        acc_close(mm, name)
                    elif part == "rot":
                        rotate(name, name[:-3] + "x", QRAW)
                    else:
                        project(name, name[:-2], HA, *((0, S) if part == "x" else (S, T)))
                elif name.startswith("B.qn"):
                    p = int(what[2:])
                    project(name, f"B.uq{p // 4}", (CQN[:, 0], CQN[:, 1]), 0, S, nk=2, at=256 * (p % 4))
                elif name.startswith("B.kn"):
                    p = int(what[2:])
                    project(name, "B.uk", (CKN[:, 0:1], CKN[:, 1:2]), *((0, S) if part == "x" else (S, T)), nk=1, at=P * p)
                elif name.startswith("C."):
                    project(name, name[:-2], HC, 0, S)
                else:
                    raise ValueError(name)

            def scores(n):
                u = units[n]
                if n >= 2:
                    pe.wait_ge(exp_done, n - 1)
                for c0, width, products in u["segments"]:
                    mm = sum_of(SC[n % 2][:, c0:c0 + width], products)
                mm.then_inc(s_ready, 1)

            def turn(n):
                u = units[n]
                pe.wait_ge(p_ready, n + 1)
                if n >= 1:
                    pe.wait_ge(pt_read, n)
                for i in range(len(u["values"])):
                    mm = pe.transpose(PTP[:, i * P:i * P + P], PROB[:, n % 2, i * P:i * P + P], ident)
                mm.then_inc(pt_ready, 1)

            def weigh_values(m):
                a, b = units[2 * m], units[2 * m + 1]
                pe.wait_ge(pt_read, 2 * m + 2)
                if a["first"] and group_of[m] >= 1:
                    pe.wait_ge(o_read, group_of[m])
                nk = len(a["values"])
                for i in range(nk):
                    for u in (a, b):
                        h = u["half"]
                        mm = pe.matmul(bank[6][64 * h:64 * h + 64, u["o0"]:u["o0"] + P], u["values"][i],
                                       PT[:, m % 2, h, i * P:i * P + P], start=i == 0, stop=i == nk - 1,
                                       skip_group_check=True)
                mm.then_inc(pv_done, 1)

            def attend(m0, m1, pair_ready, fillers):
                for b in (0, 1, 2, 3, 4, 5, 6, 7):
                    last = max((tasks[n][1] for n in opened if tasks[n][0] == b), default=0)
                    if last:
                        pe.wait_ge(acc_read[b], last)
                for m in range(m0, m1 + 2):
                    if m < m1:
                        if units[2 * m]["pair_first"]:
                            pair_ready(units[2 * m]["pair"])
                        scores(2 * m)
                    if m0 <= m - 1 < m1:
                        turn(2 * (m - 1))
                    if m < m1:
                        scores(2 * m + 1)
                    if m0 <= m - 2 < m1:
                        weigh_values(m - 2)
                    if m0 <= m - 1 < m1:
                        turn(2 * (m - 1) + 1)
                    if m < m1:
                        for name in fillers(m):
                            make(name)
                pe.wait_ge(exp_done, 2 * m1)
                pe.wait_ge(pt_read, 2 * m1)
                pe.wait_ge(o_read, group_of[m1 - 1] + 1)

            def stats(j, base, jobs):
                pe.wait_ge(sq_done, base + j + 1)
                for name, moving in jobs:
                    out = acc_open(name) if j == 0 else bank[tasks[name][0]]
                    mm = pe.matmul(out[:, 0:moving.shape[-1]], ones, moving, start=j == 0, stop=j == KD - 1)
                    if j == KD - 1:
                        acc_close(mm, name)
                if j < KD - 1:
                    mm.then_inc(sq_read, 1)

            def total(n, jobs):
                pe.wait_ge(sq_added, (KD - 1) * n)
                for name, moving in jobs:
                    acc_close(pe.matmul(acc_open(name)[:, 0:moving.shape[-1]], ones, moving, start=True, stop=True), name)

            pe.wait_ge(consts_ready, 1)
            for j in range(KD):
                stats(j, 0, [("A.stat.x", SQ[:, j % 2, 0:S]), ("A.stat.c", SQ[:, j % 2, S:T])])
                if j == 2:
                    ada_rows(0, 0)
                if j == 5:
                    ada_rows(0, 1)
                    ada_columns(0, 0)
            for b in range(2, 6):
                ada_rows(0, b)
                ada_columns(0, b - 1)
            ada_columns(0, 5)
            h_ready = lambda base: (lambda k: pe.wait_ge(hlo_done, base + k + 1))
            project_together([(f"A.k{j}.{part}", f"A.k{j}", HA, t0, t1) for j in range(2)
                              for part, t0, t1 in (("x", 0, S), ("c", S, T))], h_ready(0))
            for j in range(2):
                rotate(f"A.k{j}.rot", f"A.k{j}.x", QRAW)
            for t in range(T // P):
                out = acc_open(f"A.v.{t}")
                for k in range(KD):
                    chunk = f"A.v{k // 4}"
                    chunk_ready(chunk)
                    w = weight(chunk)
                    for i, (a, b) in enumerate(three((HA[0][:, k, t * P:t * P + P], HA[1][:, k, t * P:t * P + P]),
                                                     (w[:, 0, (k % 4) * 256:(k % 4) * 256 + 256],
                                                      w[:, 1, (k % 4) * 256:(k % 4) * 256 + 256]))):
                        mm = pe.matmul(out[:, 0:256], a, b, start=k == 0 and i == 0, stop=k == KD - 1 and i == 2)
                acc_close(mm, f"A.v.{t}")
            for name in ("A.q0.x", "A.q0.rot", "A.qg0.c", "A.g0.x"):
                make(name)

            def ready_a(p):
                pe.wait_ge(q_lo, p + 1)
                if p == 0:
                    pe.wait_ge(kz_done, 2)

            attend(0, A_END, ready_a, lambda m: fillers_a(m // 6 + 1, m % 6))
            for j in range(KD):
                ready = (lambda k: (pe.wait_ge(og_hi, k + 1), pe.wait_ge(og_lo, k + 1))) if j == 0 else None
                project(f"A.o{j}.x", f"A.o{j}", OA, 0, S, ready=ready)
                project(f"A.o{j}.c", f"A.o{j}", OA, S, T)
            total(1, [("B.stat.x", SQSUM[:, 0:S]), ("B.stat.c", SQSUM[:, S:T])])
            parts = {"x": (0, S), "c": (S, T)}
            project_together([(name, name[:-2], HA, *parts[name[-1]])
                              for name in ("B.cq0.x", "B.cq1.x", "B.ckv.x", "B.ckv.c")], h_ready(8))
            for name in ("B.kr.x", "B.kr.c"):
                project(name, name[:-2], HA, *parts[name[-1]])
            for j in range(KD):
                project(f"B.g{j}.x", f"B.g{j}", HA, 0, S)
                if j == 1:
                    pe.wait_ge(sp_rope, 32)
                    rotate("B.kr.rot", "B.kr.x", QRAWB)
                    pe.wait_ge(lat_sq, 1)
                    out = acc_open("B.cq.stat")
                    for k in range(2):
                        mm = pe.matmul(out, ones, SQCQ[:, k, :], start=k == 0, stop=k == 1)
                    acc_close(mm, "B.cq.stat")
                    pe.wait_ge(lat_sq, 2)
                    acc_close(pe.matmul(acc_open("B.ckv.stat.x"), ones, SQCK[:, 0:S], start=True, stop=True), "B.ckv.stat.x")
                    acc_close(pe.matmul(acc_open("B.ckv.stat.c")[:, 0:C], ones, SQCK[:, S:T], start=True, stop=True),
                              "B.ckv.stat.c")
            pe.wait_ge(ckn_ready, 1)
            chunk_ready("B.uv")
            w = weight("B.uv")
            pe.wait_ge(cqn_ready, 1)
            for i in range(4):
                project(f"B.qr{i}.x", "B.uqr", (CQN[:, 0], CQN[:, 1]), 0, S, nk=2, at=256 * i)
                for t, h in value_parts(i):
                    mm = sum_of(acc_open(f"B.v.{t}.{h}"), three(
                        (CKN[:, 0, t * P:t * P + P], CKN[:, 1, t * P:t * P + P]),
                        (w[:, 0, 512 * h:512 * h + 512], w[:, 1, 512 * h:512 * h + 512])))
                    acc_close(mm, f"B.v.{t}.{h}")
                rotate(f"B.qr{i}.rot", f"B.qr{i}.x", QRAWB)
            for step in range(3):
                make(*fillers_b(0, step))

            def ready_b(p):
                pe.wait_ge(b_ready, p + 1)

            attend(A_END, B_END, ready_b,
                   lambda m: fillers_b((m - A_END) // 4 + 1, (m - A_END) % 4) if (m - A_END) // 4 + 1 < N_PAIR else [])
            for j in range(KD):
                ready = (lambda k: (pe.wait_ge(og_hi, 8 + k + 1), pe.wait_ge(og_lo, 8 + k + 1))) if j == 0 else None
                project(f"B.o{j}.x", f"B.o{j}", OB, 0, S, ready=ready)
            total(2, [("C.stat.2", SQSUM[:, S:2 * S]), ("C.stat.1", SQSUM[:, 0:S])])

            def values_by_token(layer, ready=None):
                outs = [acc_open(f"{layer}.v.{t}") for t in range(QT)]
                for c in range(4):
                    chunk_ready(f"{layer}.v{c}")
                    w = weight(f"{layer}.v{c}")
                    for r in range(2):
                        k = 2 * c + r
                        if ready:
                            ready(k)
                        for t in range(QT):
                            for i, (a, b) in enumerate(three((HC[0][:, k, t * P:t * P + P], HC[1][:, k, t * P:t * P + P]),
                                                             (w[:, 0, r * 512:r * 512 + 512], w[:, 1, r * 512:r * 512 + 512]))):
                                mm = pe.matmul(outs[t], a, b, start=k == 0 and i == 0, stop=k == KD - 1 and i == 2)
                            if k == KD - 1:
                                acc_close(mm, f"{layer}.v.{t}")
                    if c < 3:
                        mm.then_inc(v_used, 1)

            values_by_token("C", h_ready(16))
            for name in ("C.q0.x", "C.k0.x", "C.z0.x"):
                make(name)

            def ready_c(p):
                pe.wait_ge(c_ready, p + 1)
                pe.wait_ge(bias_lo, p + 1)

            attend(B_END, C_END, ready_c,
                   lambda m: fillers_c((m - B_END) // 4 + 1, (m - B_END) % 4) if (m - B_END) // 4 + 1 < N_NA else [])
            project("D.gate.x", "D.gate", HC, 0, S)
            values_by_token("D")
            out = acc_open("D.gcol")
            pe.wait_ge(gates_max, 1)
            for way in range(2):
                for j in range(QT):
                    at = 4 * (QT * way + j)
                    mm = pe.transpose(out[:, at:at + 4], ROWS[0:4, 0, way, j * P:j * P + P], ident[0:4, 0:4])
            acc_close(mm, "D.gcol")
            project("D.q0.x", "D.q0", HC, 0, S)
            project("D.k0.x", "D.k0", HC, 0, S)
            for h in range(N_ML + 1):
                if h < N_ML:
                    project(f"D.o{h}.x", f"D.o{h}", HC, 0, S)
                    project(f"D.z{h}.x", f"D.z{h}", HC, 0, S)
                    pe.wait_ge(qk_lo, 2 * h + 2)
                    for j in range(QT):
                        q, k = QM[:, h % 2], KM[:, h % 2, :, j * P:j * P + P]
                        acc_close(sum_of(acc_open(f"D.s{h}.{j}"), three((k[:, 0], k[:, 1]), (q[:, 0], q[:, 1]))), f"D.s{h}.{j}")
                if h == N_ML:
                    begun = [(f"C.o{j}.x", f"C.o{j}", OB, 0, S) for j in range(3)]
                    out_ready = lambda k: (pe.wait_ge(og_hi, 16 + k + 1), pe.wait_ge(og_lo, 16 + k + 1))
                    project_together(begun[0:2], out_ready, 0, KD - 1)
                if h >= 1:
                    out = acc_open(f"D.mu{h - 1}")
                    pe.wait_ge(hm_ready, h)
                    acc_close(pe.matmul(out, ones, HM, start=True, stop=True), f"D.mu{h - 1}")
                if h + 1 < N_ML:
                    project(f"D.q{h + 1}.x", f"D.q{h + 1}", HC, 0, S)
                if h >= 1:
                    out = acc_open(f"D.var{h - 1}")
                    pe.wait_ge(sqd_ready, h)
                    acc_close(pe.matmul(out, ones, SQD, start=True, stop=True), f"D.var{h - 1}")
                if h == N_ML:
                    project_together(begun[2:3], out_ready, 0, KD - 1)
                if h < N_ML:
                    for way in range(2):
                        names = [f"D.{kind}{h}.{'fb'[way]}" for kind in ("num", "den")]
                        outs = [acc_open(name) for name in names]
                        for i, j in enumerate(key_tiles(way)):
                            pe.wait_ge(pm_ready, 8 * h + 4 * way + i + 1)
                            t0, t1 = reach(way, j)
                            for name, acc, stationary in zip(names, outs, (MV[:, j, h * P:h * P + P], ones)):
                                mm = pe.matmul(acc[:, t0:t1], stationary, PM[:, way, j, t0:t1], start=i == 0,
                                               stop=i == QT - 1, skip_group_check=True)
                                if i == QT - 1:
                                    acc_close(mm, name)
                        if way == 0 and h + 1 < N_ML:
                            project(f"D.k{h + 1}.x", f"D.k{h + 1}", HC, 0, S)
            for job in begun:
                project_together([job], out_ready, KD - 1, KD)
            for j in range(3, KD):
                project(f"C.o{j}.x", f"C.o{j}", OB, 0, S)
            total(3, [("E.stat", SQSUM[:, 0:S])])

        @block.scalar
        def _(act):
            fed = [0]

            def feed(upto):
                while fed[0] < min(upto, len(splits)):
                    name = splits[fed[0]]
                    c = chunk_at[name]
                    act.wait_ge(raw_in[c % N_RAW], 16 * (c // N_RAW + 1))
                    if name in in_ring:
                        r = in_ring.index(name)
                        if r >= N_SPLIT:
                            old = in_ring[r - N_SPLIT]
                            if old in V_FREED:
                                act.wait_ge(v_used, V_FREED.index(old) + 1)
                            else:
                                b, i = tasks[last_use[old]]
                                act.wait_ge(acc_ready[b], i)
                    act.activation(weight(name)[:, 0, :], RAW[:, c % N_RAW, :], ACT.Copy).then_inc(hi_done, 1)
                    fed[0] += 1

            def need(name, ahead=N_SPLIT):
                feed(split_at[name] + ahead)

            def wait_acc(name):
                b, i = tasks[name]
                act.wait_ge(acc_ready[b], i)
                return bank[b]

            def read(ins, name):
                ins.then_inc(acc_read[tasks[name][0]], 1)

            chain = [0]

            def step(ins):
                chain[0] += 1
                ins.then_inc(act_step, 1)
                act.wait_ge(act_step, chain[0])

            def squares(j, base, added, jobs):
                if j >= 2 and added == 0:
                    act.wait_ge(sq_read, j - 1)
                elif j >= 2:
                    act.wait_ge(sq_added, added - (KD - 1) + max(1, j - 2))
                for out, in_, scale in jobs:
                    ins = act.activation(out, in_, ACT.Square, scale=scale)
                ins.then_inc(sq_done, 1)

            def one_over_root(out, sums, width, eps=EPS):
                step(act.activation(out, sums, ACT.Ln, scale=1.0 / width, bias=eps))
                act.activation(out, out, ACT.Exp, scale=-0.5).then_inc(root_done, 1)

            def root(stats, width=D):
                for name, n, out in stats:
                    step(act.activation(out, wait_acc(name)[:, 0:n], ACT.Ln, scale=1.0 / width, bias=EPS))
                for name, n, out in stats:
                    act.activation(out, out, ACT.Exp, scale=-0.5).then_inc(root_done, 1)

            def modulated(layer, parts, base, between=None):
                for k in range(KD):
                    act.wait_ge(xn_done, base + k + 1)
                    if k == 0:
                        act.wait_ge(mod_done, layer + 1)
                    if k >= 2:
                        act.wait_ge(hlo_done, base + k - 1)
                    for v, (src, dst) in enumerate(parts(k)):
                        ins = act.activation(dst, src, ACT.Identity, scale=GAIN[:, layer, k, v:v + 1],
                                             bias=MOD[:, layer, k, v:v + 1])
                    ins.then_inc(hf_done, 1)
                    if between:
                        between(k)

            act.wait_ge(consts_ready, 1)
            act.activation(SILT, col("c", 0, 32), ACT.Tanh, scale=0.5).then_inc(silt_done, 1)
            act.wait_ge(sp_x, 32)
            for j in range(KD):
                if j == KD // 2:
                    act.wait_ge(sp_x2, 16)
                squares(j, 0, 0, [(SQ[:, j % 2, 0:S], XL[:, j, :], 1.0), (SQ[:, j % 2, S:T], XC[:, j, :], 1.0)])
            root([("A.stat.x", S, RSTD[:, 0:S]), ("A.stat.c", C, RSTD[:, S:T])])
            feed(3)
            modulated(0, lambda k: [(XN[:, k % 2, 0:S], SQ[:, k % 2, 0:S]), (XN[:, k % 2, S:T], SQ[:, k % 2, S:T])], 0)

            ropes = [0]

            def rope_raw(name, dst, rows=P):
                r = ropes[0]
                ropes[0] += 1
                if r >= 1:
                    act.wait_ge(rope_sum, r)
                read(act.activation(dst, wait_acc(name), ACT.Copy), name)

            def chunk_of(name):
                return name[:-2].replace("qg", "g") if part_of(name) == "c" else name[:-2]

            def part_of(name):
                return name[-1]

            def evac_a(name):
                need(chunk_of(name), 1)
                what, part = name.split(".")[1], name.split(".")[2]
                if what[0] in "qk" and part == "x":
                    rope_raw(name, QRAW)
                elif what[0] == "k":
                    if what == "k1":
                        act.wait_ge(kz_done, 1)
                    read(act.activation(QP[:, S:T], wait_acc(name)[:, 0:C], ACT.Copy), name)
                elif what[0:2] == "qg":
                    p = int(what[2:])
                    if p >= 1:
                        act.wait_ge(q_lo, p)
                    else:
                        act.wait_ge(kz_done, 2)
                    act.activation(QP[:, S:T], wait_acc(name)[:, 0:C], ACT.Copy)
                    act.activation(OGC[:, p, :], wait_acc(name)[:, C:2 * C], ACT.Tanh, scale=0.5).then_inc(tanh_done, 1)
                else:
                    act.activation(OG[:, int(what[1:]), :], wait_acc(name), ACT.Tanh, scale=0.5).then_inc(tanh_done, 1)
                if chunk_of(name) != "A.g7":
                    need(chunk_of(name), 2)

            for name in ("A.k0.x", "A.k0.c", "A.k1.x", "A.k1.c", "A.q0.x", "A.qg0.c", "A.g0.x"):
                evac_a(name)

            def attend(m0, m1, evacs):
                def exps(n):
                    u = units[n]
                    act.wait_ge(nm_ready, n + 1)
                    if n >= 2:
                        act.wait_ge(pt_ready, n - 1)
                    i = n % 4
                    if u["sink"] is not None:
                        act.activation(STAT[:, 3, i:i + 1], u["sink"], ACT.Exp, bias=STAT[:, 1, i:i + 1])
                    act.activation(PROB[:, n % 2, 0:u["c1"] - u["c0"]], SC[n % 2][:, u["c0"]:u["c1"]], ACT.Exp,
                                   bias=STAT[:, 1, i:i + 1], scale=u["scale"],
                                   accum_out=STAT[:, 2, i:i + 1]).then_inc(exp_done, 1)

                def turned(n):
                    m, w = n // 2, P * len(units[n]["values"])
                    act.wait_ge(pt_ready, n + 1)
                    if m >= 2:
                        act.wait_ge(pv_done, m - 1)
                    act.activation(PT[:, m % 2, n % 2, 0:w], PTP[:, 0:w], ACT.Copy).then_inc(pt_read, 1)

                for m in range(m0, m1 + 1):
                    if m > m0:
                        evacs(m - 1)
                    if m > m0:
                        turned(2 * m - 2)
                    if m < m1:
                        exps(2 * m)
                    if m > m0:
                        turned(2 * m - 1)
                    if m < m1:
                        exps(2 * m + 1)

            def out_high(layer, j, dst, parts):
                for i, (src, t0, t1) in enumerate(parts):
                    ins = act.activation(dst[0][:, j, t0:t1], src[:, j, :], ACT.Copy)
                ins.then_inc(og_hi, 1)

            A_PARTS = [(OG, 0, S), (OGC, S, T)]

            def out_high_a(j):
                act.wait_ge(o_read, 2 * j + 2)
                if j == 0:
                    b, i = tasks["A.g7.x"]
                    act.wait_ge(acc_ready[b], i)
                out_high("A", j, OA, A_PARTS)

            def evacs_a(m):
                p = m // 6 + 1
                if p == N_PAIR:
                    out_high_a(m % 6)
                if p < N_PAIR:
                    for name in fillers_a(p, m % 6):
                        if not name.startswith("ada") and not name.endswith("rot"):
                            evac_a(name)

            attend(0, A_END, evacs_a)
            need("A.o0", 3)
            for j in (6, 7):
                out_high_a(j)
            for j in range(KD):
                need(f"A.o{min(j + 2, KD - 1)}", 1)
                act.wait_ge(x_new, j + 1)
                squares(j, 8, 7, [(SQ[:, j % 2, 0:S], XL[:, j, :], 1.0), (SQ[:, j % 2, S:T], XC[:, j, :], 1.0)])
            root([("B.stat.x", S, RSTD[:, 0:S]), ("B.stat.c", C, RSTD[:, S:T])])
            need("B.cq0", 3)
            modulated(1, lambda k: [(XN[:, k % 2, 0:S], SQ[:, k % 2, 0:S]), (XN[:, k % 2, S:T], SQ[:, k % 2, S:T])], 8)

            def copy_out(name, dst, n):
                need(name[:-2], 4)
                read(act.activation(dst, wait_acc(name)[:, 0:n], ACT.Copy), name)

            copy_out("B.cq0.x", CQR[:, 0, :], S)
            copy_out("B.cq1.x", CQR[:, 1, :], S)
            copy_out("B.ckv.x", CKR[:, 0:S], S)
            copy_out("B.ckv.c", CKR[:, S:T], C)
            b, i = tasks["B.ckv.c"]
            act.wait_ge(acc_read[b], i)
            act.activation(SQCQ, CQR, ACT.Square).then_inc(lat_sq, 1)
            act.activation(SQCK, CKR, ACT.Square).then_inc(lat_sq, 1)
            need("B.kr", 4)
            rope_raw("B.kr.x", QRAWB)
            read(act.activation(KRF[:, S:T], wait_acc("B.kr.c")[:, 0:C], ACT.Copy), "B.kr.c")

            def gate_b(j):
                need(f"B.g{j}", 4)
                act.activation(OG[:, j, :], wait_acc(f"B.g{j}.x"), ACT.Tanh, scale=0.5).then_inc(tanh_done, 1)

            gate_b(0)
            gate_b(1)
            for name, out, n, width in (("B.cq.stat", RSQ, S, 256), ("B.ckv.stat.x", RSK[:, 0:S], S, 128),
                                        ("B.ckv.stat.c", RSK[:, S:T], C, 128)):
                one_over_root(out, wait_acc(name)[:, 0:n], width)
            for j in range(2, KD):
                gate_b(j)
            need("B.uv", 4)
            for i in range(4):
                rope_raw(f"B.qr{i}.x", QRAWB)
                for t, h in value_parts(i):
                    if h == 0:
                        name = f"B.v.{t}.0"
                        read(act.activation(VB[:, t, 0:512], wait_acc(name), ACT.Copy), name)
            need("B.uqr", 4)

            def evac_b(name):
                p, part = int(name[4:-2]), name[-1]
                if p >= 2:
                    act.wait_ge(s_ready, pair_scored("B", p - 2))
                acc = wait_acc(name)
                t0, t1 = (0, S) if part == "x" else (S, T)
                for half in range(2):
                    dst = QB[0:64, 0, p % 2, half, :] if name[2] == "q" else KB[0:64, 0, p % 2, half, t0:t1]
                    ins = act.activation(dst, acc[64 * half:64 * half + 64, 0:t1 - t0], ACT.Copy)
                ins.then_inc(b_hi, 1)

            for part in range(3):
                evac_b(*fillers_b(0, part))

            def evacs_b(m):
                p, s = (m - A_END) // 4 + 1, (m - A_END) % 4
                if p < N_PAIR:
                    for name in fillers_b(p, s):
                        if not name.startswith("ada"):
                            evac_b(name)

            attend(A_END, B_END, evacs_b)
            need("B.o0", 2)
            for j in range(KD):
                act.wait_ge(o_read, 16 + 8)
                out_high("B", j, OB, [(OG, 0, S)])
            for j in range(KD):
                need(f"B.o{j}", 3)
                act.wait_ge(x_new, 8 + j + 1)
                squares(j, 16, 14, [(SQ2[:, j % 2, 0, :], XL[:, j, :], 1.0), (SQ2[:, j % 2, 1, :], XL[:, j, :], col("fg", j))])
            act.wait_ge(ms2_done, 1)
            one_over_root(RSTD2[:, 1, :], XNC[:, 1, :], D, 0.0)
            one_over_root(RSTD2[:, 0, :], wait_acc("C.stat.1"), D)
            need("C.v0", 3)
            modulated(2, lambda k: [(XNC[:, k % 2, :], SQ2[:, k % 2, 0, :])], 16,
                      lambda k: need("C.v0", {4: 4, 6: 5}.get(k, 3)))

            def bias_high(p):
                act.wait_ge(bias_raw, p + 1)
                if p >= 2:
                    act.wait_ge(s_ready, pair_scored("C", p - 2))
                act.activation(BIAS[p % 2][0], BRAW2, ACT.Copy).then_inc(bias_hi, 1)

            def evac_c(name):
                what, p = name[2], int(name[3:-2])
                need(f"C.z{p}", 1)
                acc = wait_acc(name)
                if what in "qk" and p >= 2:
                    act.wait_ge(s_ready, pair_scored("C", p - 2))
                if what == "q":
                    act.activation(QC[:, 0, p % 2, :], acc, ACT.Identity, bias=col("bna", p)).then_inc(c_hi, 1)
                elif what == "k":
                    for half in range(2):
                        h = slice(64 * half, 64 * half + 64)
                        ins = act.activation(KC[h, 0, p % 2, half, :], acc[h, :], ACT.Identity, bias=col("bna", 4 + p)[h, :])
                    ins.then_inc(c_hi, 1)
                else:
                    if p >= 1:
                        act.wait_ge(zg_done, p)
                    read(act.activation(ZB, acc, ACT.Identity, bias=col("bna", 8 + p)), name)
                    b, i = tasks[name]
                    act.wait_ge(acc_read[b], i)
                    act.activation(ZT, ZB, ACT.Tanh, scale=0.5).then_inc(tanh_done, 1)

            need("C.v3", 3)
            bias_high(0)
            for name in ("C.q0.x", "C.k0.x", "C.z0.x"):
                evac_c(name)
            need("C.q1", 1)

            def evacs_c(m):
                p, s = (m - B_END) // 4 + 1, (m - B_END) % 4
                if p < N_NA:
                    for name in fillers_c(p, s):
                        evac_c(name)
                    if s == 2:
                        bias_high(p)
                    if s == 3:
                        need(f"C.z{p}", 2)

            attend(B_END, C_END, evacs_c)

            act.wait_ge(vm_ready, 1)
            need("D.v1", 1)
            read(act.activation(GALL, wait_acc("D.gate.x"), ACT.Identity, bias=col("bg")), "D.gate.x")
            need("D.v3", 1)
            act.wait_ge(gates_abs, 1)
            step(act.activation(GL[0:4], GX[0:4], ACT.Exp, scale=-1.0))
            act.activation(GL[0:4], GL[0:4], ACT.Ln, bias=1.0).then_inc(gates_log, 1)
            need("D.k0", 1)
            act.wait_ge(gates_max, 1)
            act.activation(ROWS[0:4, 2], GX[0:4], ACT.Exp, scale=-1.0).then_inc(rows_ready, 1)
            need("D.o0", 1)

            def conv_input(h, what):
                i = "qk".index(what)
                name = f"D.{what}{h}.x"
                if h >= 1:
                    act.wait_ge(conv_done, 2 * h + i - 1)
                read(act.activation(U[:, i, 2:2 + S], wait_acc(name), ACT.Identity, bias=col("bml", 4 * i + h)), name)
                b, n = tasks[name]
                act.wait_ge(acc_read[b], n)
                if h >= 1:
                    act.wait_ge(qk_lo, 2 * h + i - 1)
                tile = 4 * i + h
                act.activation(CV[:, i], U[:, i, 0:S], ACT.Identity, scale=col("cw", 5 * tile),
                               bias=col("cb", tile)).then_inc(tap_done, 1)

            def conv_tanh(h, what):
                i = "qk".index(what)
                act.wait_ge(conv_done, 2 * h + i + 1)
                if 2 * h + i >= 1:
                    act.wait_ge(tq_used, 2 * h + i)
                act.activation(TQ, CV[:, i], ACT.Tanh, scale=0.5).then_inc(tq_ready, 1)

            def decay(h, way):
                act.wait_ge(rows_in[h % 2], 16 * (h // 2 + 1))
                act.wait_ge(xd_ready, 2 * h + way + 1)
                for i, j in enumerate(key_tiles(way)):
                    n = 8 * h + 4 * way + i
                    if n >= 4:
                        act.wait_ge(pm_ready, n - 3)
                    g = GCOL[:, way, j, h:h + 1]
                    w = W[:, n % 4]
                    ins = act.activation(w[:, j * P:j * P + P], XD[:, way, j], ACT.Exp, bias=g)
                    t0, t1 = ((j + 1) * P, S) if way == 0 else (0, j * P)
                    if t1 > t0:
                        ins = act.activation(w[:, t0:t1], RB[:, h % 2, 0, way, t0:t1], ACT.Exp, bias=g)
                    ins.then_inc(w_ready, 1)

            conv_input(0, "q")
            need("D.z0", 1)
            conv_tanh(0, "q")
            conv_input(0, "k")
            need("D.k0", 4)
            conv_tanh(0, "k")
            decay(0, 0)
            for h in range(N_ML + 1):
                if h < N_ML:
                    if h >= 2:
                        act.wait_ge(hm_ready, h - 1)
                    name = f"D.o{h}.x"
                    read(act.activation((TO, TO2)[h % 2], wait_acc(name), ACT.Tanh, scale=0.5,
                                        bias=HALF_B[:, 8 + h:9 + h]), name)
                    need(f"D.o{h}", 4)
                    if h >= 1:
                        act.wait_ge(z_gate, h)
                    name = f"D.z{h}.x"
                    acc = wait_acc(name)
                    act.activation(ZTM, acc, ACT.Tanh, scale=0.5, bias=HALF_B[:, 12 + h:13 + h])
                    read(act.activation(OG[:, 4 + h, :], acc, ACT.Identity, scale=0.5, bias=HALF_B[:, 12 + h:13 + h]), name)
                    need(f"D.z{h}", 4)
                    decay(h, 1)
                if h >= 1:
                    act.wait_ge(dv_ready, h)
                    act.activation(SQD, DV, ACT.Square).then_inc(sqd_ready, 1)
                if h + 1 < N_ML:
                    conv_input(h + 1, "q")
                    need(f"D.q{h + 1}", 4)
                if h >= 1:
                    one_over_root(RSM, wait_acc(f"D.var{h - 1}"), P, 4 * EPS)
                if h + 1 < N_ML:
                    conv_tanh(h + 1, "q")
                    conv_input(h + 1, "k")
                    need(f"D.k{h + 1}", 4)
                    conv_tanh(h + 1, "k")
                    decay(h + 1, 0)
                if h == N_ML - 1:
                    for j in range(KD - 1):
                        if j >= 4:
                            act.wait_ge(ml_done, j - 3)
                        out_high("C", j, OB, [(OG, 0, S)])
            act.wait_ge(ml_done, N_ML)
            out_high("C", KD - 1, OB, [(OG, 0, S)])
            need("C.o3", 1)

            def weighted(j):
                act.activation(OG[:, j, :], XL[:, j, :], ACT.Copy, scale=col("fw", j)).then_inc(xw_done, 1)

            for j in range(KD):
                need(f"C.o{j}", 3)
                act.wait_ge(x_new, 16 + j + 1)
                squares(j, 24, 21, [(SQ[:, j % 2, 0:S], XL[:, j, :], 1.0)])
                if j == 0:
                    act.wait_ge(og_lo, 24)
                if j >= 1:
                    weighted(j - 1)
            root([("E.stat", S, RSTD[:, 0:S])])
            weighted(KD - 1)

        @block.vector
        def _(dve):
            chain = [0]

            def step(ins):
                chain[0] += 1
                ins.then_inc(dve_step, 1)
                dve.wait_ge(dve_step, chain[0])

            def wait_acc(name):
                b, i = tasks[name]
                dve.wait_ge(acc_ready[b], i)
                return bank[b]

            def read(ins, name):
                b, i = tasks[name]
                ins.then_inc(acc_read[b], 1)
                dve.wait_ge(acc_read[b], i)

            def signal(ins, s, value):
                ins.then_inc(s, 1)
                dve.wait_ge(s, value)

            def ada_row(layer, b):
                name = f"ada{layer}.{b}"
                acc = wait_acc(name)
                if b or layer:
                    last = f"ada{layer}.{b - 1}.t" if b else f"ada{layer - 1}.5.t"
                    dve.wait_ge(acc_ready[tasks[last][0]], tasks[last][1])
                read(dve.tensor_copy(ada_buffer(layer, b), acc), name)

            def ada_column(layer, b):
                name = f"ada{layer}.{b}.t"
                acc = wait_acc(name).rearrange("p (i g r) -> p i r g", i=4, g=4)[:, :, 0:2, :]
                read(dve.tensor_reduce(MOD[:, layer, 4 * b:4 * b + 4, :], acc, AX, ALU.add), name)
                if b == 5:
                    mod = MOD[:, layer].rearrange("p a v -> p (a v)")
                    step(dve.tensor_tensor(mod, mod, col(f"ab{layer}", 0, 48), ALU.add))
                    signal(dve.scalar_tensor_tensor(GAIN[:, layer].rearrange("p a v -> p (a v)"), mod[:, 16:32], 1.0,
                                                    col(f"ng{layer}", 0, 16), ALU.add, ALU.mult), mod_done, layer + 1)

            def ada_part(name):
                layer, b = int(name[3]), int(name.split(".")[1])
                ada_column(layer, b) if name.endswith("t") else ada_row(layer, b)

            def modulate(layer, base, parts, h):
                def high(k):
                    dve.wait_ge(hf_done, base + k + 1)
                    src, dst = parts[1](k), h[0][:, k, :]
                    dve.tensor_copy(dst, src).then_inc(hhi_done, 1)
                for k in range(KD):
                    if k >= 2:
                        dve.wait_ge(hf_done, base + k - 1)
                    for out, in_, *factors in parts[0](k):
                        if len(factors) == 1:
                            ins = dve.tensor_tensor(out, in_, factors[0], ALU.mult)
                        else:
                            ins = dve.scalar_tensor_tensor(out, in_, factors[0], factors[1], ALU.mult, ALU.mult)
                    ins.then_inc(xn_done, 1)
                    if k >= 1:
                        high(k - 1)
                high(KD - 1)

            step(dve.memset(PS[:, :, :], 0.0))
            step(dve.memset(ones, 1.0))
            dve.wait_ge(sp_const, 16 * N_CONST)
            step(dve.tensor_copy(identR, ident))
            step(dve.tensor_copy(mask3R, PPT[:, 4 * T:4 * T + 384]))
            step(dve.tensor_scalar(NSINK, col("sink", 0, 16), -1.0, None, ALU.mult))
            dve.sem_inc(consts_ready, 1)
            dve.wait_ge(silt_done, 1)
            silc = SILC.rearrange("p l k v -> p (l k v)")
            step(dve.scalar_tensor_tensor(silc, SILT, 1.0, col("c", 0, 32), ALU.add, ALU.mult))
            signal(dve.tensor_scalar(silc, silc, 0.5, None, ALU.mult), silc_done, 1)
            def wait_read(name):
                b, i = tasks[name]
                dve.wait_ge(acc_read[b], i)

            roots = [0]

            def sharpen(r, sums, t, width, eps=EPS):
                step(dve.tensor_tensor(t, r, r, ALU.mult))
                at = 0
                for name, src, n in sums:
                    ins = dve.scalar_tensor_tensor(t[:, at:at + n], src[:, 0:n], width * eps, t[:, at:at + n], ALU.add, ALU.mult)
                    read(ins, name) if name else step(ins)
                    at += n
                step(dve.tensor_scalar(t, t, -0.5 / width, 1.5, ALU.mult, ALU.add))
                step(dve.tensor_tensor(r, r, t, ALU.mult))

            def rstd(names, r, t, width, eps=EPS):
                roots[0] += len(names)
                dve.wait_ge(root_done, roots[0])
                sharpen(r, [(n, bank[tasks[n][0]], C if n.endswith("c") else S) for n in names], t, width, eps)

            ada_row(0, 0)
            ada_row(0, 1)
            ada_column(0, 0)
            dve.wait_ge(sp_x, 32)
            dve.wait_ge(sp_x2, 16)
            rstd(("A.stat.x", "A.stat.c"), RSTD, XN[:, 0, :], D)
            for b in range(2, 6):
                ada_row(0, b)
                if b >= 1:
                    ada_column(0, b - 1)
            ada_column(0, 5)

            def normed(base_k):
                return lambda k: [(XN[:, k % 2, 0:S], XL[:, k, :], RSTD[:, 0:S]), (XN[:, k % 2, S:T], XC[:, k, :], RSTD[:, S:T])]

            modulate(0, 0, (normed(0), lambda k: SQ[:, k % 2, :]), HA)

            ropes = [0]

            def rope_turned(name, tmp, dst):
                r = ropes[0]
                ropes[0] += 1
                read(dve.tensor_tensor(tmp, wait_acc(name), ROPE[:, 1, :], ALU.mult), name)
                dve.wait_ge(cos_done, r + 1)
                signal(dve.tensor_tensor(dst, tmp, COSP if r < 10 else COSB, ALU.add), rope_sum, r + 1)

            def split_keys(j):
                wait_read(f"A.k{j}.c")
                dve.wait_ge(kz_zero, 1)
                for half in range(2):
                    h = slice(64 * half, 64 * half + 64)
                    step(dve.tensor_copy(KZ[h, 0, j, half, :], QP[h, :]))
                    low = dve.tensor_tensor(KZ[h, 1, j, half, :], QP[h, :], KZ[h, 0, j, half, :].bitcast(F32), ALU.subtract)
                    if half == 1:
                        signal(low, kz_done, j + 1)

            def rope_q(p):
                if p >= 1:
                    dve.wait_ge(q_lo, p)
                rope_turned(f"A.q{p}.rot", QP[:, 0:S], QP[:, 0:S])

            def high_q(p):
                dve.wait_ge(tanh_done, 2 * p + 1)
                if p >= 2:
                    dve.wait_ge(s_ready, pair_scored("A", p - 2))
                signal(dve.tensor_copy(QA[:, 0, p % 2, :], QP), q_hi, p + 1)

            def gate(name, dst, count, at=0):
                dve.wait_ge(tanh_done, count)
                n = dst.shape[-1]
                read(dve.scalar_tensor_tensor(dst, dst, 1.0, wait_acc(name)[:, at:at + n], ALU.add, ALU.mult), name)

            for j in range(2):
                rope_turned(f"A.k{j}.rot", QP[:, 0:S], QP[:, 0:S])
                split_keys(j)
            for t in range(T // P):
                read(dve.tensor_copy(VA[:, t, :], wait_acc(f"A.v.{t}")[:, 0:256]), f"A.v.{t}")
            rope_q(0)
            high_q(0)
            gate("A.qg0.c", OGC[:, 0, :], 1, C)
            gate("A.g0.x", OG[:, 0, :], 2)

            def attend(m0, m1, others, later=None):
                def negmax(n):
                    u, i = units[n], n % 4
                    dve.wait_ge(s_ready, n + 1)
                    step(dve.reduce_max(STAT[:, 0, i:i + 1], SC[n % 2][:, u["c0"]:u["c1"]], AX))
                    if u["sink"] is None:
                        ins = dve.tensor_scalar(STAT[:, 1, i:i + 1], STAT[:, 0, i:i + 1], -u["scale"], None, ALU.mult)
                    else:
                        h = 2 * u["pair"] + u["half"]
                        ins = dve.tensor_scalar(STAT[:, 1, i:i + 1], STAT[:, 0, i:i + 1], -u["scale"],
                                                NSINK[:, h:h + 1], ALU.mult, ALU.min)
                    ins.then_inc(nm_ready, 1)

                def normalise(n):
                    u, i = units[n], n % 4
                    w = u["c1"] - u["c0"]
                    dve.wait_ge(exp_done, n + 1)
                    total = STAT[:, 2, i:i + 1]
                    if u["sink"] is not None:
                        step(dve.tensor_tensor(total, total, STAT[:, 3, i:i + 1], ALU.add))
                    step(dve.reciprocal(STAT[:, 4, i:i + 1], total))
                    dve.tensor_scalar(PROB[:, n % 2, 0:w], PROB[:, n % 2, 0:w], STAT[:, 4, i:i + 1], None,
                                      ALU.mult).then_inc(p_ready, 1)

                def gate_output(m):
                    u = units[2 * m]
                    dve.wait_ge(pv_done, m + 1)
                    signal(dve.scalar_tensor_tensor(u["out"], bank[6][:, 0:u["width"]], 0.5, u["out"], ALU.mult, ALU.mult),
                           o_read, group_of[m] + 1)

                for m in range(m0, m1 + 2):
                    if m0 <= m - 3 and units[2 * (m - 3)]["out"] is not None:
                        gate_output(m - 3)
                    if m0 < m <= m1:
                        others(m - 1)
                    if m < m1:
                        negmax(2 * m)
                        negmax(2 * m + 1)
                    if m < m1:
                        normalise(2 * m)
                        normalise(2 * m + 1)
                    if later and m0 < m <= m1:
                        later(m - 1)
                gate_output(m1 - 1)

            def others_a(m):
                p = m // 6 + 1
                for name in fillers_a(p, m % 6):
                    if name.startswith("ada"):
                        ada_part(name)
                    elif name == f"A.q{p}.rot":
                        rope_q(p)
                    elif name == f"A.qg{p}.c":
                        high_q(p)
                        gate(name, OGC[:, p, :], 2 * p + 1, C)
                    elif name == f"A.g{p}.x":
                        gate(name, OG[:, p, :], 2 * p + 2)

            attend(0, A_END, others_a)

            def residual(j, name, x, v, count):
                n = x.shape[-1]
                ins = dve.scalar_tensor_tensor(x[:, j, :], wait_acc(name)[:, 0:n], MOD[:, count, 16 + j, v:v + 1],
                                               x[:, j, :], ALU.mult, ALU.add)
                read(ins, name)

            def add_squares(n, j, parts, width):
                dve.wait_ge(sq_done, 8 * n + j + 1)
                dst = SQSUM[:, 0:width]
                signal(dve.tensor_tensor(dst, parts(0) if j == 1 else dst, parts(j % 2), ALU.add), sq_added, 7 * (n - 1) + j)

            def residuals(n, update, parts, width):
                for j in range(KD):
                    update(j)
                    dve.sem_inc(x_new, 1)
                    if j >= 2:
                        add_squares(n, j - 1, parts, width)
                add_squares(n, KD - 1, parts, width)

            def update_a(j):
                residual(j, f"A.o{j}.x", XL, 0, 0)
                residual(j, f"A.o{j}.c", XC, 1, 0)

            residuals(1, update_a, lambda i: SQ[:, i, :], T)
            rstd(("B.stat.x", "B.stat.c"), RSTD, XN[:, 0, :], D)

            modulate(1, 8, (normed(0), lambda k: SQ[:, k % 2, :]), HA)

            dve.wait_ge(sp_rope, 32)
            rope_turned("B.kr.rot", KRF[:, 0:S], KRF[:, 0:S])
            gate("B.g0.x", OG[:, 0, :], 17)
            gate("B.g1.x", OG[:, 1, :], 18)

            def split(high, low, src, done=None, value=None):
                step(dve.tensor_copy(high, src))
                ins = dve.tensor_tensor(low, src, high.bitcast(F32), ALU.subtract)
                step(ins) if done is None else signal(ins, done, value)

            rstd(("B.cq.stat",), RSQ, SQCQ[:, 0, :], 256)
            for k in range(2):
                step(dve.scalar_tensor_tensor(CQR[:, k, :], CQR[:, k, :], col("qg", k), RSQ, ALU.mult, ALU.mult))
                split(CQN[:, 0, k, :], CQN[:, 1, k, :], CQR[:, k, :])
            dve.sem_inc(cqn_ready, 1)
            rstd(("B.ckv.stat.x", "B.ckv.stat.c"), RSK[:, 0:T], SQCK, 128)
            step(dve.scalar_tensor_tensor(CKR, CKR, col("kg"), RSK, ALU.mult, ALU.mult))
            split(CKN[:, 0, :], CKN[:, 1, :], CKR, ckn_ready, 1)
            for j in range(2, KD):
                gate(f"B.g{j}.x", OG[:, j, :], 17 + j)
            for i in range(4):
                for t, h in value_parts(i):
                    if h == 1:
                        name = f"B.v.{t}.1"
                        read(dve.tensor_copy(VB[:, t, 512:1024], wait_acc(name)), name)
                rope_turned(f"B.qr{i}.rot", QR[:, i, :], QR[:, i, :])
                step(dve.tensor_copy(QRH[:, i, :], QR[:, i, :]))
                step(dve.tensor_tensor(QR[:, i, :], QR[:, i, :], QRH[:, i, :].bitcast(F32), ALU.subtract))
                if i == 0:
                    wait_read("B.kr.c")
                buf, half = i // 2, i % 2
                split(KB[64:96, 0, buf, half, :], KB[64:96, 1, buf, half, :], KRF[64:96, :])

            lows = [0]

            def low_b(name):
                p, part = int(name[4:-2]), name[-1]
                lows[0] += 1
                dve.wait_ge(b_hi, lows[0])
                acc = wait_acc(name)
                t0, t1 = (0, S) if part == "x" else (S, T)
                for half in range(2):
                    buf = QB[0:64, :, p % 2, half, :] if name[2] == "q" else KB[0:64, :, p % 2, half, t0:t1]
                    ins = dve.tensor_tensor(buf[:, 1, :], acc[64 * half:64 * half + 64, 0:t1 - t0],
                                            buf[:, 0, :].bitcast(F32), ALU.subtract)
                read(ins, name)
                if name.endswith("c"):
                    dve.sem_inc(b_ready, 1)

            def roped_queries(p):
                for half in range(2):
                    h = 2 * p + half
                    rows = slice(32 * (h % 4), 32 * (h % 4) + 32)
                    step(dve.tensor_copy(QB[64:96, 0, p % 2, half, :], QRH[rows, h // 4, :].bitcast(F32)))
                    step(dve.tensor_copy(QB[64:96, 1, p % 2, half, :], QR[rows, h // 4, :]))

            for part in range(3):
                low_b(*fillers_b(0, part))
                if part == 0:
                    roped_queries(0)

            def others_b(m):
                p, s = (m - A_END) // 4 + 1, (m - A_END) % 4
                if p < N_PAIR:
                    for name in fillers_b(p, s):
                        ada_part(name) if name.startswith("ada") else low_b(name)

            def later_b(m):
                p, s = (m - A_END) // 4 + 1, (m - A_END) % 4
                if p < N_PAIR and s == 1:
                    roped_queries(p)

            attend(A_END, B_END, others_b, later_b)

            def out_low(layer, j, dst, src):
                dve.wait_ge(og_hi, 8 * layer + j + 1)
                dve.tensor_tensor(dst[1][:, j, :], src, dst[0][:, j, :].bitcast(F32), ALU.subtract).then_inc(og_lo, 1)

            for j in range(KD):
                out_low(1, j, OB, OG[:, j, :])
            residuals(2, lambda j: residual(j, f"B.o{j}.x", XL, 0, 1), lambda i: SQ2[:, i].rearrange("p a n -> p (a n)"), 2 * S)
            v = XNC[:, 1, :]
            step(dve.tensor_scalar(v, wait_acc("C.stat.1"), EPS, D * EPS * EPS, ALU.mult, ALU.add))
            read(dve.tensor_tensor(v, wait_acc("C.stat.2"), v, ALU.add), "C.stat.2")
            dve.sem_inc(ms2_done, 1)
            roots[0] += 1
            dve.wait_ge(root_done, roots[0])
            sharpen(RSTD2[:, 1, :], [(None, v, S)], XNC[:, 0, :], D, 0.0)
            modulate(2, 16, (lambda k: [(XNC[:, k % 2, :], XL[:, k, :], col("fg", k), RSTD2[:, 1, :])],
                             lambda k: SQ2[:, k % 2, 0, :]), HC)

            def mask_bias(p):
                dve.wait_ge(bias_in, 64 * (p + 1))
                for half in range(2):
                    mask = CMASK.unsqueeze(1).to_broadcast([P, 14, GRID])
                    ins = dve.scalar_tensor_tensor(BRAW[:, half], BRAW[:, half], 1 / SCALE_A, mask, ALU.mult, ALU.add)
                signal(ins, bias_raw, p + 1)

            lows_c = [0]

            def low_c(name):
                what, p = name[2], int(name[3:-2])
                if what == "z":
                    dve.wait_ge(tanh_done, 24 + p + 1)
                    wait_read(name)
                    signal(dve.scalar_tensor_tensor(OG[:, p, :], ZT, 1.0, ZB, ALU.add, ALU.mult), zg_done, p + 1)
                    return
                lows_c[0] += 1
                dve.wait_ge(c_hi, lows_c[0])
                acc = wait_acc(name)
                if what == "q":
                    ins = dve.scalar_tensor_tensor(QC[:, 1, p % 2, :], acc, col("bna", p),
                                                   QC[:, 0, p % 2, :].bitcast(F32), ALU.add, ALU.subtract)
                else:
                    for half in range(2):
                        h = slice(64 * half, 64 * half + 64)
                        ins = dve.scalar_tensor_tensor(KC[h, 1, p % 2, half, :], acc[h, :], col("bna", 4 + p)[h, :],
                                                       KC[h, 0, p % 2, half, :].bitcast(F32), ALU.add, ALU.subtract)
                read(ins, name)
                if what == "k":
                    dve.sem_inc(c_ready, 1)

            mask_bias(0)
            dve.wait_ge(sp_vb, 32)
            for t in range(QT):
                read(dve.tensor_tensor(VC[:, t, :], wait_acc(f"C.v.{t}"), VBC[:, 0, :], ALU.add), f"C.v.{t}")
            dve.wait_ge(kc_zero, 1)
            for name in ("C.q0.x", "C.k0.x", "C.z0.x"):
                low_c(name)
                if name == "C.q0.x":
                    rstd(("C.stat.1",), RSTD2[:, 0, :], XNC[:, 0, :], D)
                    for k in range(KD):
                        step(dve.scalar_tensor_tensor(XL[:, k, :], XL[:, k, :], col("fg", k), RSTD2[:, 0, :],
                                                      ALU.mult, ALU.mult))

            def others_c(m):
                p, s = (m - B_END) // 4 + 1, (m - B_END) % 4
                if p < N_NA:
                    for name in fillers_c(p, s):
                        low_c(name)
                    if s == 1:
                        mask_bias(p)

            attend(B_END, C_END, others_c)

            step(dve.memset(U[:, :, :], 0.0))
            step(dve.tensor_scalar(HALF_B, col("bml", 0, 16), 0.5, None, ALU.mult))
            dve.sem_inc(vm_ready, 1)
            wait_read("D.gate.x")
            for dst, at in ((GI[0:4, 0], 0), (GI[0:4, 1], 32), (GF[0:4, 0], 64), (GF[0:4, 1], 96)):
                step(dve.tensor_copy(dst, GALL[at:at + 4]))
            signal(dve.scalar_tensor_tensor(GX[0:4], GF[0:4], -1.0, GF[0:4], ALU.mult, ALU.max), gates_abs, 1)
            dve.wait_ge(gates_log, 1)
            step(dve.scalar_tensor_tensor(GL[0:4], GF[0:4], 0.0, GL[0:4], ALU.min, ALU.subtract))
            one = ones[0:4, 0:1].to_broadcast([4, S])

            def along(ap, way):
                return ap[0:4, way, :] if way == 0 else ap[0:4, way, ::-1]

            for way in range(2):
                step(dve.tensor_tensor_scan(along(GX, way), one, along(GL, way), 0.0, ALU.mult, ALU.add))
            step(dve.tensor_tensor(ROWS[0:4, 0], GI[0:4], GX[0:4], ALU.subtract))
            for way in range(2):
                g = along(ROWS[:, 0], way)
                step(dve.tensor_tensor_scan(along(GF, way), g, g, 0.0, ALU.max, ALU.max))
            step(dve.tensor_scalar(ROWS[0:4, 1], GF[0:4], -1.0, None, ALU.mult))
            signal(dve.tensor_tensor(GX[0:4], GX[0:4], GF[0:4], ALU.add), gates_max, 1)
            for t in range(QT):
                name = f"D.v.{t}"
                read(dve.tensor_tensor(MV[:, t, :], wait_acc(name), VBC[:, 1, :], ALU.add), name)
            read(dve.tensor_copy(GCOL.rearrange("p a j h -> p (a j h)"), wait_acc("D.gcol")[:, 0:32]), "D.gcol")

            def convolve(h, what):
                i = "qk".index(what)
                dve.wait_ge(tap_done, 2 * h + i + 1)
                tile = 4 * i + h
                for tap in range(1, 5):
                    ins = dve.scalar_tensor_tensor(CV[:, i], U[:, i, tap:tap + S], col("cw", 5 * tile + tap), CV[:, i],
                                                   ALU.mult, ALU.add)
                    step(ins) if tap < 4 else signal(ins, conv_done, 2 * h + i + 1)

            def doubled_silu(h, what):
                i = "qk".index(what)
                dve.wait_ge(tq_ready, 2 * h + i + 1)
                signal(dve.scalar_tensor_tensor(CV[:, i], TQ, 1.0, CV[:, i], ALU.add, ALU.mult), tq_used, 2 * h + i + 1)
                dst = (QM, KM)[i][:, h % 2, 0]
                dve.tensor_copy(dst, CV[:, i]).then_inc(qk_hi, 1)

            def weigh(h, way):
                if h >= 1:
                    b, i = tasks[f"D.den{h - 1}.{'fb'[way]}"]
                    dve.wait_ge(acc_ready[b], i)
                for i, j in enumerate(key_tiles(way)):
                    acc = wait_acc(f"D.s{h}.{j}")
                    n = 8 * h + 4 * way + i
                    dve.wait_ge(w_ready, n + 1)
                    t0, t1 = reach(way, j)
                    signal(dve.scalar_tensor_tensor(PM[:, way, j, t0:t1], acc[:, t0:t1], 0.25 * P ** -0.5,
                                                    W[:, n % 4, t0:t1], ALU.mult, ALU.mult), pm_ready, n + 1)
                    if way == 1:
                        dve.sem_inc(acc_read[j], 1)

            def divide(h, way):
                den, num = f"D.den{h}.{'fb'[way]}", f"D.num{h}.{'fb'[way]}"
                acc = wait_acc(den)
                step(dve.scalar_tensor_tensor(T1, acc, -1.0, RB[:, h % 2, 1, way], ALU.mult, ALU.max))
                read(dve.tensor_tensor(T1, acc, T1, ALU.max), den)
                step(dve.reciprocal(T1, T1))
                read(dve.tensor_tensor(T2 if way else HM, wait_acc(num), T1, ALU.mult), num)
                if way:
                    step(dve.tensor_tensor(HM, HM, T2, ALU.add))
                    signal(dve.scalar_tensor_tensor(HM, (TO, TO2)[h % 2], 1.0, HM, ALU.add, ALU.mult), hm_ready, h + 1)

            def centre(h):
                name = f"D.mu{h}"
                read(dve.scalar_tensor_tensor(DV, wait_acc(name), -1.0 / P, HM, ALU.mult, ALU.add), name)
                dve.sem_inc(dv_ready, 1)

            def finish(h):
                rstd((f"D.var{h}",), RSM, T1, P, 4 * EPS)
                step(dve.tensor_tensor(DV, DV, RSM, ALU.mult))
                signal(dve.scalar_tensor_tensor(OG[:, 4 + h, :], DV, col("mw", h), OG[:, 4 + h, :], ALU.mult, ALU.mult),
                       ml_done, h + 1)

            convolve(0, "q")
            doubled_silu(0, "q")
            convolve(0, "k")
            doubled_silu(0, "k")
            for h in range(N_ML + 1):
                if h < N_ML:
                    weigh(h, 0)
                    weigh(h, 1)
                    wait_read(f"D.z{h}.x")
                    signal(dve.scalar_tensor_tensor(OG[:, 4 + h, :], ZTM, 1.0, OG[:, 4 + h, :], ALU.add, ALU.mult),
                           z_gate, h + 1)
                if h >= 1:
                    centre(h - 1)
                if h + 1 < N_ML:
                    convolve(h + 1, "q")
                if h >= 1:
                    finish(h - 1)
                if h + 1 < N_ML:
                    doubled_silu(h + 1, "q")
                if h < N_ML:
                    divide(h, 0)
                if h + 1 < N_ML:
                    convolve(h + 1, "k")
                    doubled_silu(h + 1, "k")
                if h < N_ML:
                    wait_read(f"D.o{h}.x")
                    divide(h, 1)
            residuals(3, lambda j: residual(j, f"C.o{j}.x", XL, 0, 2), lambda i: SQ[:, i, 0:S], S)
            rstd(("E.stat",), RSTD[:, 0:S], XN[:, 0, 0:S], D)
            dve.sem_inc(rs_ready, 1)
            for j in (0, 1, 3, 4, 6):
                dve.wait_ge(xw_done, j + 1)
                dve.tensor_tensor(OG[:, j, :], OG[:, j, :], RSTD[:, 0:S], ALU.mult).then_inc(y_ready, 1)

        @block.gpsimd
        def _(pool):
            fed = [0]

            def feed(upto):
                while fed[0] < min(upto, len(splits)):
                    name = splits[fed[0]]
                    c = chunk_at[name]
                    pool.wait_ge(hi_done, fed[0] + 1)
                    w = weight(name)
                    pool.tensor_tensor(w[:, 1, :], RAW[:, c % N_RAW, :], w[:, 0, :].bitcast(F32),
                                       ALU.subtract).then_inc(lo_done, 1)
                    fed[0] += 1

            def need(name, ahead=1):
                feed(split_at[name] + ahead)

            def wait_read(name):
                b, i = tasks[name]
                pool.wait_ge(acc_read[b], i)

            def h_low(base, src, h, between=None):
                for k in range(KD):
                    pool.wait_ge(hhi_done, base + k + 1)
                    pool.tensor_tensor(h[1][:, k, :], src(k), h[0][:, k, :].bitcast(F32), ALU.subtract).then_inc(hlo_done, 1)
                    if between:
                        between(k)

            ropes = [0]

            def cosine(name, raw, dst):
                r = ropes[0]
                ropes[0] += 1
                wait_read(name)
                if r >= 1:
                    pool.wait_ge(rope_sum, r)
                pool.tensor_tensor(dst, raw, ROPE[:, 0, :], ALU.mult).then_inc(cos_done, 1)

            def low_q(p):
                if p >= 2:
                    pool.wait_ge(s_ready, pair_scored("A", p - 2))
                pool.wait_ge(q_hi, p + 1)
                pool.tensor_tensor(QA[:, 1, p % 2, :], QP, QA[:, 0, p % 2, :].bitcast(F32), ALU.subtract).then_inc(q_lo, 1)

            pool.memset(R2.bitcast(F32), 0.0).then_inc(kz_zero, 1)
            pool.wait_ge(sp_const, 16 * N_CONST)
            feed(2)
            h_low(0, lambda k: SQ[:, k % 2, :], HA)
            feed(3)
            cosine("A.k0.x", QRAW, COSP)
            feed(4)
            cosine("A.k1.x", QRAW, COSP)
            feed(5)
            cosine("A.q0.x", QRAW, COSP)
            feed(6)
            low_q(0)
            for p in range(1, N_PAIR):
                need(f"A.q{p}", 1)
                cosine(f"A.q{p}.x", QRAW, COSP)
                need(f"A.g{p}", 1)
                low_q(p)
            for j in range(KD):
                pool.wait_ge(og_hi, j + 1)
                pool.tensor_tensor(OA[1][:, j, 0:S], OG[:, j, :], OA[0][:, j, 0:S].bitcast(F32), ALU.subtract)
                pool.tensor_tensor(OA[1][:, j, S:T], OGC[:, j, :], OA[0][:, j, S:T].bitcast(F32),
                                   ALU.subtract).then_inc(og_lo, 1)
                if j == 2:
                    need("A.o0", 2)
            need("A.o7", 1)
            need("B.cq0", 3)
            h_low(8, lambda k: SQ[:, k % 2, :], HA)
            need("B.g0", 1)
            pool.wait_ge(sp_rope, 32)
            cosine("B.kr.x", QRAWB, COSB)
            need("B.uqr", 1)
            for i in range(4):
                cosine(f"B.qr{i}.x", QRAWB, COSB)
                if i == 3:
                    need("B.uk", 1)
            need("B.o7", 1)
            pool.wait_ge(o_read, group_of[B_END - 1] + 1)
            pool.memset(R2[:, 2048:].bitcast(F32), 0.0).then_inc(kc_zero, 1)
            need("C.v0", 1)
            h_low(16, lambda k: SQ2[:, k % 2, 0, :], HC, lambda k: need("C.v0", {4: 4, 6: 5}.get(k, 3)))

            def bias_low(p):
                pool.wait_ge(bias_hi, p + 1)
                pool.tensor_tensor(BIAS[p % 2][1], BRAW2, BIAS[p % 2][0].bitcast(F32), ALU.subtract).then_inc(bias_lo, 1)

            for p in range(N_NA):
                if p == 0:
                    bias_low(0)
                need(f"C.z{p}", 1)
                if p:
                    bias_low(p)

            def low_m(h, what):
                i = "qk".index(what)
                pool.wait_ge(qk_hi, 2 * h + i + 1)
                dst = (QM, KM)[i][:, h % 2]
                pool.tensor_tensor(dst[:, 1], CV[:, i], dst[:, 0].bitcast(F32), ALU.subtract).then_inc(qk_lo, 1)

            def diagonals(h):
                pool.wait_ge(rows_in[h % 2], 16 * (h // 2 + 1))
                if h >= 1:
                    pool.wait_ge(w_ready, 8 * h)
                for way in range(2):
                    pool.tensor_tensor(XD[:, way], RB[:, h % 2, 0, way].rearrange("p (j n) -> p j n", j=QT),
                                      DIAG[:, way].unsqueeze(1).to_broadcast([P, QT, P]), ALU.add).then_inc(xd_ready, 1)

            need("D.z0", 1)
            low_m(0, "q")
            diagonals(0)
            need("D.q1", 1)
            low_m(0, "k")
            for h in range(N_ML):
                need(f"D.o{h}", 4)
                need(f"D.z{h}", 4)
                if h + 1 < N_ML:
                    need(f"D.q{h + 1}", 4)
                    low_m(h + 1, "q")
                    diagonals(h + 1)
                    need(f"D.k{h + 1}", 4)
                    low_m(h + 1, "k")
            for j in range(KD):
                pool.wait_ge(og_hi, 16 + j + 1)
                pool.tensor_tensor(OB[1][:, j, :], OG[:, j, :], OB[0][:, j, :].bitcast(F32), ALU.subtract).then_inc(og_lo, 1)
            need("C.o7", 1)
            pool.wait_ge(rs_ready, 1)
            for j in (2, 5, 7):
                pool.wait_ge(xw_done, j + 1)
                pool.tensor_tensor(OG[:, j, :], OG[:, j, :], RSTD[:, 0:S], ALU.mult).then_inc(y_ready2, 1)

        @block.sync
        def _(sp):
            sp.dma_start(CST[:, 0:256], cst[:, 0:256]).then_inc(sp_const, 16)
            sp.dma_start(PPT[:, 4 * T:4 * T + 384], cst[:, 256:640]).then_inc(sp_const, 16)
            sp.dma_start(ROPE, rope[0]).then_inc(sp_const, 16)
            sp.dma_start(COLS, cols).then_inc(sp_const, 16)
            sp.dma_start(XC, ctx_in).then_inc(sp_x, 16)
            sp.dma_start(XL[:, 0:KD // 2, :], x_in[:, 0:KD // 2, :]).then_inc(sp_x, 16)
            sp.dma_start(XL[:, KD // 2:, :], x_in[:, KD // 2:, :]).then_inc(sp_x2, 16)

            def freed(c):
                name, split = chunks[c]
                if split:
                    sp.wait_ge(lo_done, split_at[name] + 1)
                else:
                    rows, q = name[:name.rindex(".")], int(name[-1])
                    if q < 3:
                        sp.wait_ge(ada_used, 3 * ada_order.index(rows) + q + 1)
                    else:
                        b, i = tasks[rows]
                        sp.wait_ge(acc_ready[b], i)

            def others(c):
                name = chunks[c][0]
                if name == "B.cq0":
                    sp.wait_ge(rope_sum, 10)
                    sp.dma_start(CST[:, 128:256], cst[:, 640:768]).then_inc(sp_rope, 16)
                    sp.dma_start(ROPE, rope[1]).then_inc(sp_rope, 16)

                if name == "B.o5":
                    sp.wait_ge(o_read, group_of[B_END - 1] + 1)
                    sp.dma_start(OGC_[:, 0:320], cst[:, 768:1088]).then_inc(sp_vb, 16)
                    sp.dma_start(VBC, vbias.to_broadcast([P, 2 * S]).rearrange("p (a n) -> p a n", a=2)).then_inc(sp_vb, 16)
                    load_bias(0)
                if name in ("C.k1", "C.k2", "C.k3"):
                    p = int(name[3:])
                    sp.wait_ge(bias_lo, p)
                    load_bias(p)

                if name == "D.q1":
                    sp.wait_ge(rows_ready, 1)
                    sp.dma_start(rows_dram.rearrange("a d h t -> h a d t"), ROWS[0:4]).then_inc(rows_stored, 16)
                    sp.wait_ge(rows_stored, 16)
                    load_rows(0)
                    load_rows(1)
                if name in ("D.z2", "D.z3"):
                    h = int(name[3:])
                    sp.wait_ge(hm_ready, h - 1)
                    load_rows(h)

            def load_rows(h):
                src = bass.AP(tensor=rows_dram.tensor, offset=8 * S + h * S, ap=[[0, P], [8 * S, 2], [4 * S, 2], [1, S]])
                sp.dma_start(RB[:, h % 2], src).then_inc(rows_in[h % 2], 16)

            def load_bias(p):
                for half in range(2):
                    for r in range(2):
                        src = rpb_band[2 * p + half, :, 1 - r:15 - r, :]
                        sp.dma_start(BRAW[64 * r:64 * r + 64, half], src).then_inc(bias_in, 16)

            for c, (name, _) in enumerate(chunks):
                others(c)
                if c >= N_RAW:
                    freed(c - N_RAW)
                sp.dma_start(RAW[:, c % N_RAW, :], wstream[c]).then_inc(raw_in[c % N_RAW], 16)
            for j, done, count in ((0, y_ready, 1), (2, y_ready2, 1), (1, y_ready, 2), (3, y_ready, 3), (5, y_ready2, 2),
                                   (4, y_ready, 4), (6, y_ready, 5), (7, y_ready2, 3)):
                sp.wait_ge(done, count)
                sp.dma_start(out[:, j, :], OG[:, j, :]).then_inc(s_out, 16)
            sp.wait_ge(s_out, 16 * KD)


def quarter_turn(head, quarter):
    m = np.zeros((P, P), np.float32)
    for i in range(P):
        part = (i % head) // quarter
        if part % 2 == 0:
            m[i + quarter, i] = -1.0
        else:
            m[i - quarter, i] = 1.0
    return m


def rope_table(head):
    n = np.arange(S)
    nf = head // 4
    inv = (np.float32(10000.0) ** (-np.arange(nf, dtype=np.float32) / np.float32(nf))).astype(np.float32)
    ar = (n // GRID).astype(np.float32)[:, None] * inv
    ac = (n % GRID).astype(np.float32)[:, None] * inv
    ang = np.concatenate([ar, ar, ac, ac], axis=-1).astype(np.float32)
    both = np.stack([np.cos(ang), np.sin(ang)]).astype(np.float32)
    return np.ascontiguousarray(np.tile(both.transpose(2, 0, 1), (P // head, 1, 1)))


def constants():
    i, j = np.arange(P)[:, None], np.arange(P)[None, :]
    off = np.float32(MASKED)
    left = np.where(j >= i, 0, off)
    right = np.where(j <= i, 0, off)
    col = np.arange(P)[:, None] % GRID
    start = np.clip(col - 8, 0, GRID - 16)
    k = np.arange(GRID)[None, :]
    window = np.where((k >= start) & (k < start + 16), 0, off)
    return np.concatenate([np.eye(P), quarter_turn(64, 16), left, np.zeros((P, P)), right, quarter_turn(32, 8),
                           left, right, window], axis=1).astype(np.float32)


def channel_columns(v, n):
    return np.reshape(v, (n, P)).T


def twice(v):
    return np.repeat(v, 2, axis=1)


PAIR_HEADS = [(8 * (p // 4) + p % 4, 8 * (p // 4) + 4 + p % 4) for p in range(N_PAIR)]


def by_pair(w):
    heads = [h for pair in PAIR_HEADS for h in pair]
    return np.reshape(np.reshape(w, (w.shape[0], 16, 64))[:, heads, :], (w.shape[0], 1024))


def stationary(w):
    return w.reshape(KD, P, P).transpose(1, 0, 2).reshape(P, CHUNK)


def weight_stream(i):
    a_in, b_in_w, c_in = i["a_w_in_0"], i["b_w_in_1"], np.reshape(i["w_in_2"], (D, -1))
    aq, ak, av, ag = by_pair(a_in[:, 0:1024]), a_in[:, 1024:1280], a_in[:, 1280:1536], by_pair(a_in[:, 1536:2560])
    a_o = by_pair(np.ascontiguousarray(i["a_w_o_0"].T)).T
    kr = np.tile(b_in_w[:, 384:416], (1, 4))
    uq = i["b_w_uq_1"].reshape(256, 16, 96)
    ukv = i["b_w_ukv_1"].reshape(128, 16, 128)
    qn = np.ascontiguousarray(uq[:, :, 0:64]).reshape(2, P, 8, P)
    qr = np.ascontiguousarray(uq[:, :, 64:96]).reshape(2, P, 4, P)
    gate = np.zeros((D, P), np.float32)
    for at, src in ((0, 4608), (32, 4616), (64, 4612), (96, 4620)):
        gate[:, at:at + 4] = c_in[:, src:src + 4]
    ada = {0: i["ada_w_0"], 1: i["ada_w_1"], 2: np.reshape(i["w_ada_2"], (D, 3 * D))}
    main = {"A.q": aq, "A.g": ag, "A.k": ak, "A.o": a_o, "B.g": b_in_w[:, 416:], "B.cq": b_in_w[:, 0:256],
            "B.o": i["b_w_o_1"], "C.q": c_in[:, 0:512], "C.k": c_in[:, 512:1024], "C.z": c_in[:, 1536:2048],
            "D.q": c_in[:, 2048:2560], "D.k": c_in[:, 2560:3072], "D.o": c_in[:, 3584:4096],
            "D.z": c_in[:, 4096:4608], "C.o": np.reshape(i["w_out_2"], (D, D))}
    out = []
    for name, _ in chunk_plan():
        if name.startswith("ada"):
            layer, b, q = name[3:].split(".")
            w = ada[int(layer)].reshape(4, 2, P, 6, 512)[int(q), :, :, int(b), :]
            out.append(w.transpose(1, 0, 2).reshape(P, CHUNK))
        elif name.startswith("A.v"):
            h = int(name[3:])
            out.append(av.reshape(2, 4, P, 256)[h].transpose(1, 0, 2).reshape(P, CHUNK))
        elif name.startswith(("C.v", "D.v")):
            v = c_in[:, 1024:1536] if name[0] == "C" else c_in[:, 3072:3584]
            out.append(v.reshape(4, 2, P, 512)[int(name[3:])].transpose(1, 0, 2).reshape(P, CHUNK))
        elif name == "B.ckv":
            out.append(stationary(b_in_w[:, 256:384]))
        elif name == "B.kr":
            out.append(stationary(kr))
        elif name == "B.uv":
            out.append(np.ascontiguousarray(ukv[:, :, 64:128]).reshape(P, CHUNK))
        elif name == "B.uk":
            out.append(np.ascontiguousarray(ukv[:, :, 0:64]).reshape(P, CHUNK))
        elif name == "B.uqr":
            out.append(qr.transpose(1, 2, 0, 3).reshape(P, CHUNK))
        elif name.startswith("B.uq"):
            p = 4 * int(name[4:])
            out.append(qn[:, :, p:p + 4, :].transpose(1, 2, 0, 3).reshape(P, CHUNK))
        elif name == "D.gate":
            out.append(stationary(gate))
        else:
            key = name.rstrip("0123456789")
            j = int(name[len(key):])
            out.append(stationary(main[key][:, j * P:j * P + P]))
    return np.stack(out)


def column_vectors(i):
    b_in = np.reshape(i["b_in_2"], (-1,))
    gate = np.zeros((P, 1), np.float32)
    for at, src in ((0, 4608), (32, 4616), (64, 4612), (96, 4620)):
        gate[at:at + 4, 0] = b_in[src:src + 4]
    c = np.stack([channel_columns(i["c"], 8), channel_columns(i["c_ctx"], 8)], axis=2).reshape(P, 16)
    sinks = np.reshape(i["a_sinks_0"], (16,))[[h for pair in PAIR_HEADS for h in pair]]
    cw = np.reshape(i["conv_w_2"], (5, 8, P)).transpose(2, 1, 0).reshape(P, 40)
    parts = {
        "c": c, "c2": twice(channel_columns(i["c_2"], 8)),
        "ab0": twice(channel_columns(i["ada_b_0"], 24)), "ab1": twice(channel_columns(i["ada_b_1"], 24)),
        "ab2": twice(channel_columns(i["b_ada_2"], 24)), "ng0": twice(channel_columns(i["norm_g_0"], 8)),
        "ng1": twice(channel_columns(i["norm_g_1"], 8)), "ng2": twice(channel_columns(i["norm_w_2"], 8)),
        "fg": channel_columns(i["final_g"], 8), "fw": channel_columns(i["final_norm_w_2"], 8),
        "qg": channel_columns(i["b_q_norm_1"], 2), "kg": channel_columns(i["b_kv_norm_1"], 1),
        "bna": np.concatenate([channel_columns(b_in[0:1024], 8), channel_columns(b_in[1536:2048], 4)], axis=1),
        "bml": np.concatenate([channel_columns(b_in[2048:3072], 8), channel_columns(b_in[3584:4608], 8)], axis=1),
        "cw": cw, "cb": channel_columns(i["conv_b_2"], 8), "mw": channel_columns(i["ml_norm_w_2"], 4), "bg": gate,
        "sink": np.broadcast_to(sinks, (P, 16)),
    }
    at, n = column_layout()
    return np.ascontiguousarray(np.concatenate([parts[name] for name in at], axis=1))


def host_arrays(i):
    b_in = np.reshape(i["b_in_2"], (-1,))
    column = np.arange(GRID)
    dx = np.clip(column[None, :] - column[:, None], -15, 15) + 15
    rpb_band = np.ascontiguousarray(np.reshape(i["rpb_2"], (8, 15, 31))[:, :, dx].transpose(0, 2, 1, 3))
    return {
        "wstream": weight_stream(i), "cst": constants(), "rope": np.stack([rope_table(64), rope_table(32)]),
        "cols": column_vectors(i),
        "x_in": np.ascontiguousarray(np.reshape(i["x"], (S, KD, P)).transpose(2, 1, 0)),
        "ctx_in": np.ascontiguousarray(np.reshape(i["ctx"], (C, KD, P)).transpose(2, 1, 0)),
        "vbias": np.concatenate([b_in[1024:1536], b_in[3072:3584]]).reshape(1, 1024), "rpb_band": rpb_band,
    }


def kernel(**inputs):
    import concourse.bacc as bacc
    from concourse.bass_utils import run_bass_kernel_spmd

    arrays = host_arrays({k: np.asarray(v) for k, v in inputs.items()})
    nc = bacc.Bacc("TRN2", target_bir_lowering=False, num_devices=1, dynamic_dma_scratch_size=1024)
    args = {n: nc.dram_tensor(n, a.shape, F32, kind="ExternalInput").ap() for n, a in arrays.items()}
    rows_dram = nc.dram_tensor("rows", (3, 2, 4, S), F32, kind="Internal").ap()
    out = nc.dram_tensor("out", (P, KD, S), F32, kind="ExternalOutput").ap()
    build(nc, rows_dram=rows_dram, out=out, **args)
    result = run_bass_kernel_spmd(nc, [arrays], core_ids=[0]).results[0]["out"]
    return np.ascontiguousarray(np.reshape(result, (P, KD, S)).transpose(2, 1, 0)).reshape(1, S, D)
```
